# Optimizing a Trainium2 kernel written in Bass

```python
import math
import jax, jax.numpy as jnp
from jax import lax
import numpy as np

D_MODEL = 1024
BATCH = 1
SEQ = 256
DEPTH = 1

GLA_HEADS = 4
GLA_DK = D_MODEL // 16
GLA_DV = D_MODEL // 8
GLA_LOWRANK = 16
GLA_TAU = 16.0
GLA_CHUNK = 64
MOBA_HEADS = 4
MOBA_DH = 128
MOBA_BLOCK = 256
MOBA_TOPK = 3
MOBA_QCHUNK = 32
NUM_BUCKETS = 32
MAX_DISTANCE = 128
MAX_EXACT = NUM_BUCKETS // 2
D_FF = 2816
FFN_RES = 0.5
EPS = 1e-6
N_MOD = 9
GLA_QK_W = GLA_HEADS * GLA_DK
GLA_V_W = GLA_HEADS * GLA_DV
MOBA_W = MOBA_HEADS * MOBA_DH
IN_SIZES = (GLA_QK_W, GLA_QK_W, GLA_V_W, GLA_LOWRANK, GLA_V_W, MOBA_W, MOBA_W, MOBA_W, D_MODEL, D_MODEL)
IN_WIDTH = sum(IN_SIZES)


def rmsnorm(x, g):
    xf = x.astype(jnp.float32)
    y = xf * lax.rsqrt(jnp.mean(xf * xf, axis=-1, keepdims=True) + EPS) * g.astype(jnp.float32)
    return y.astype(x.dtype)

def modulate(x, shift, scale):
    return x * (1.0 + scale[:, None, :]) + shift[:, None, :]

def swiglu(x, w_gate, w_up, w_down):
    return (jax.nn.silu(x @ w_gate) * (x @ w_up)) @ w_down

def rel_bucket(dist):
    n = jnp.maximum(dist, 0)
    nf = jnp.maximum(n, 1).astype(jnp.float32)
    large = MAX_EXACT + (jnp.log(nf / MAX_EXACT) / math.log(MAX_DISTANCE / MAX_EXACT)
                         * (NUM_BUCKETS - MAX_EXACT)).astype(jnp.int32)
    large = jnp.minimum(large, NUM_BUCKETS - 1)
    return jnp.where(n < MAX_EXACT, n, large)

def gla_chunked(q, k, v, log_a):
    B, H, S, dk = q.shape
    dv = v.shape[-1]
    nc = S // GLA_CHUNK

    def to_chunks(t):
        return jnp.moveaxis(t.astype(jnp.float32).reshape(B, H, nc, GLA_CHUNK, t.shape[-1]), 2, 0)

    causal = jnp.tril(jnp.ones((GLA_CHUNK, GLA_CHUNK), dtype=bool))

    def step(state, inp):
        qc, kc, vc, gc = inp
        b = jnp.cumsum(gc, axis=2)
        o_inter = jnp.einsum('bhcd,bhde->bhce', qc * jnp.exp(b), state)
        diff = b[:, :, :, None, :] - b[:, :, None, :, :]
        decay = jnp.exp(jnp.where(causal[:, :, None], diff, -jnp.inf))
        attn = jnp.einsum('bhid,bhijd,bhjd->bhij', qc, decay, kc)
        o = o_inter + jnp.einsum('bhij,bhje->bhie', attn, vc)
        b_last = b[:, :, -1:, :]
        state = (jnp.exp(b_last[:, :, 0, :])[..., None] * state
                 + jnp.einsum('bhcd,bhce->bhde', kc * jnp.exp(b_last - b), vc))
        return state, o

    state0 = jnp.zeros((B, H, dk, dv), jnp.float32)
    _, o = lax.scan(step, state0, (to_chunks(q), to_chunks(k), to_chunks(v), to_chunks(log_a)))
    return jnp.moveaxis(o, 0, 2).reshape(B, H, S, dv)

def moba_attention(q, k, v, rel_bias):
    B, H, S, dh = q.shape
    nb = -(-S // MOBA_BLOCK)
    s_pad = nb * MOBA_BLOCK
    pad = ((0, 0), (0, 0), (0, s_pad - S), (0, 0))
    q = q.astype(jnp.float32)
    k = jnp.pad(k.astype(jnp.float32), pad)
    v = jnp.pad(v.astype(jnp.float32), pad)
    k_blocks = k.reshape(B, H, nb, MOBA_BLOCK, dh)
    v_blocks = v.reshape(B, H, nb, MOBA_BLOCK, dh)
    k_mean = jnp.mean(k_blocks, axis=3)
    topk = min(MOBA_TOPK, nb)
    scale = dh ** -0.5
    head_ix = jnp.arange(H)[None, :, None, None, None]
    gather = jax.vmap(jax.vmap(lambda blocks, ix: blocks[ix]))

    def chunk(ci):
        start = ci * MOBA_QCHUNK
        q_c = lax.dynamic_slice_in_dim(q, start, MOBA_QCHUNK, axis=2)
        q_pos = start + jnp.arange(MOBA_QCHUNK)
        cur = start // MOBA_BLOCK
        gate = jnp.einsum('bhqd,bhnd->bhqn', q_c, k_mean)
        gate = jnp.where(jnp.arange(nb) < cur, gate, -jnp.inf)
        _, sel = lax.top_k(gate, topk)
        sel_valid = jnp.arange(topk) < cur
        k_sel = gather(k_blocks, sel)
        v_sel = gather(v_blocks, sel)
        sel_pos = sel[..., None] * MOBA_BLOCK + jnp.arange(MOBA_BLOCK)
        sel_bias = rel_bias[head_ix, rel_bucket(q_pos[:, None, None] - sel_pos)]
        s_sel = jnp.einsum('bhqd,bhqrkd->bhqrk', q_c, k_sel) * scale + sel_bias
        s_sel = jnp.where(sel_valid[:, None], s_sel, -jnp.inf)
        own_start = cur * MOBA_BLOCK
        k_own = lax.dynamic_slice_in_dim(k, own_start, MOBA_BLOCK, axis=2)
        v_own = lax.dynamic_slice_in_dim(v, own_start, MOBA_BLOCK, axis=2)
        rel = q_pos[:, None] - (own_start + jnp.arange(MOBA_BLOCK))[None, :]
        s_own = jnp.einsum('bhqd,bhkd->bhqk', q_c, k_own) * scale + rel_bias[:, rel_bucket(rel)]
        s_own = jnp.where(rel >= 0, s_own, -jnp.inf)
        n_sel = topk * MOBA_BLOCK
        logits = jnp.concatenate([s_sel.reshape(B, H, MOBA_QCHUNK, n_sel), s_own], axis=-1)
        p = jax.nn.softmax(logits, axis=-1)
        p_sel = p[..., :n_sel].reshape(B, H, MOBA_QCHUNK, topk, MOBA_BLOCK)
        p_own = p[..., n_sel:]
        return (jnp.einsum('bhqrk,bhqrkd->bhqd', p_sel, v_sel)
                + jnp.einsum('bhqk,bhkd->bhqd', p_own, v_own))

    out = lax.map(chunk, jnp.arange(S // MOBA_QCHUNK))
    return jnp.transpose(out, (1, 2, 0, 3, 4)).reshape(B, H, S, dh)

def token_mixing(u, w_in, w_gla_lr, b_gla_lr, gla_norm, rel_bias, w_br_gla, w_br_moba, w_out):
    B, S, _ = u.shape
    proj = u @ w_in
    offsets = np.cumsum(IN_SIZES)[:-1].tolist()
    gq, gk, gv, glr, gog, mq, mk, mv, ga, gb = jnp.split(proj, offsets, axis=-1)

    def heads(t, n):
        return t.reshape(B, S, n, -1).transpose(0, 2, 1, 3)

    log_a = jax.nn.log_sigmoid((glr @ w_gla_lr + b_gla_lr).astype(jnp.float32)) / GLA_TAU
    o_a = gla_chunked(heads(gq, GLA_HEADS) * (GLA_DK ** -0.5), heads(gk, GLA_HEADS),
                      heads(gv, GLA_HEADS), heads(log_a, GLA_HEADS))
    o_a = rmsnorm(o_a.transpose(0, 2, 1, 3), gla_norm)
    o_a = o_a * jax.nn.silu(gog.reshape(B, S, GLA_HEADS, GLA_DV).astype(jnp.float32))
    y_a = o_a.reshape(B, S, GLA_V_W).astype(u.dtype) @ w_br_gla

    o_b = moba_attention(heads(mq, MOBA_HEADS), heads(mk, MOBA_HEADS), heads(mv, MOBA_HEADS), rel_bias)
    y_b = o_b.transpose(0, 2, 1, 3).reshape(B, S, MOBA_W).astype(u.dtype) @ w_br_moba

    merged = jax.nn.sigmoid(ga) * y_a + jax.nn.sigmoid(gb) * y_b
    return merged @ w_out

def first_inputs(seed: int = 0) -> dict:
    key = jax.random.key(seed)
    ks = jax.random.split(key, 24)
    L, D, F = DEPTH, D_MODEL, D_FF
    nrm = lambda k, shape, fan_in: jax.random.normal(k, shape, jnp.float32) * (fan_in ** -0.5)
    gain = lambda k, shape: 1.0 + 0.05 * jax.random.normal(k, shape, jnp.float32)
    return {
        "x": jax.random.normal(ks[0], (BATCH, SEQ, D), jnp.float32),
        "c": jax.random.normal(ks[1], (BATCH, D), jnp.float32),
        "w_ada": nrm(ks[2], (L, D, N_MOD * D), D) * 0.5,
        "b_ada": 0.01 * jax.random.normal(ks[3], (L, N_MOD * D), jnp.float32),
        "norm_ff1": gain(ks[4], (L, D)),
        "w_ff1_gate": nrm(ks[5], (L, D, F), D),
        "w_ff1_up": nrm(ks[6], (L, D, F), D),
        "w_ff1_down": nrm(ks[7], (L, F, D), F),
        "norm_mix": gain(ks[8], (L, D)),
        "w_in": nrm(ks[9], (L, D, IN_WIDTH), D),
        "w_gla_lr": nrm(ks[10], (L, GLA_LOWRANK, GLA_QK_W), GLA_LOWRANK),
        "b_gla_lr": 0.1 * jax.random.normal(ks[11], (L, GLA_QK_W), jnp.float32),
        "gla_norm": gain(ks[12], (L, GLA_DV)),
        "rel_bias": 0.5 * jax.random.normal(ks[13], (MOBA_HEADS, NUM_BUCKETS), jnp.float32),
        "w_br_gla": nrm(ks[14], (L, GLA_V_W, D), GLA_V_W),
        "w_br_moba": nrm(ks[15], (L, MOBA_W, D), MOBA_W),
        "w_out": nrm(ks[16], (L, D, D), D),
        "norm_ff2": gain(ks[17], (L, D)),
        "w_ff2_gate": nrm(ks[18], (L, D, F), D),
        "w_ff2_up": nrm(ks[19], (L, D, F), D),
        "w_ff2_down": nrm(ks[20], (L, F, D), F),
        "norm_final": gain(ks[21], (D,)),
    }

def first_block(x, c, w_ada, b_ada, norm_ff1, w_ff1_gate, w_ff1_up, w_ff1_down, norm_mix, w_in,
              w_gla_lr, b_gla_lr, gla_norm, rel_bias, w_br_gla, w_br_moba, w_out, norm_ff2,
              w_ff2_gate, w_ff2_up, w_ff2_down, norm_final):
    h = x
    c_act = jax.nn.silu(c)
    for l in range(DEPTH):
        mod = c_act @ w_ada[l] + b_ada[l]
        sh1, sc1, g1, sh2, sc2, g2, sh3, sc3, g3 = jnp.split(mod, N_MOD, axis=-1)
        u = modulate(rmsnorm(h, norm_ff1[l]), sh1, sc1)
        h = h + FFN_RES * g1[:, None, :] * swiglu(u, w_ff1_gate[l], w_ff1_up[l], w_ff1_down[l])
        u = modulate(rmsnorm(h, norm_mix[l]), sh2, sc2)
        h = h + g2[:, None, :] * token_mixing(u, w_in[l], w_gla_lr[l], b_gla_lr[l], gla_norm[l], rel_bias,
                                              w_br_gla[l], w_br_moba[l], w_out[l])
        u = modulate(rmsnorm(h, norm_ff2[l]), sh3, sc3)
        h = h + FFN_RES * g3[:, None, :] * swiglu(u, w_ff2_gate[l], w_ff2_up[l], w_ff2_down[l])
    return rmsnorm(h, norm_final)


DEPTH_2 = 2

HEAD_DIM = 64
CONV_CH = 256
CONV_WIDTH = 3
HGRN_HEADS = 4
HGRN_DK = 64
HGRN_DV = 64
HGRN_QK = HGRN_HEADS * HGRN_DK
HGRN_WIDTH = HGRN_HEADS * HGRN_DV
CHUNK = 64
FOX_HEADS = 8
FOX_WIDTH = FOX_HEADS * HEAD_DIM
Q_BLOCK = 128
MIX_WIDTH = CONV_CH + HGRN_WIDTH + FOX_WIDTH
MIX_IN_SIZES = (CONV_CH, CONV_CH, CONV_CH,
                HGRN_QK, HGRN_QK, HGRN_WIDTH, HGRN_WIDTH,
                FOX_WIDTH, FOX_WIDTH, FOX_WIDTH, FOX_HEADS)
MIX_IN = sum(MIX_IN_SIZES)
MASK_VALUE = -1e30


def rms_norm(x, gain):
    xf = x.astype(jnp.float32)
    inv = lax.rsqrt(jnp.mean(xf * xf, axis=-1, keepdims=True) + EPS)
    return (xf * inv).astype(x.dtype) * gain

def swiglu_2(h, w_in, w_out):
    gate, up = jnp.split(h @ w_in, 2, axis=-1)
    return (jax.nn.silu(gate) * up) @ w_out

def short_conv_mixer(x_in, b_gate, c_gate, conv_w):
    u = c_gate * x_in
    taps = conv_w[:, None, :].astype(u.dtype)
    y = lax.conv_general_dilated(u, taps, window_strides=(1,),
                                 padding=((CONV_WIDTH - 1, 0),),
                                 dimension_numbers=('NWC', 'WIO', 'NWC'),
                                 feature_group_count=CONV_CH)
    return b_gate * y

def hgrn2_mixer(q, f_logit, v, g, lb, out_gain):
    f32 = jnp.float32
    bsz, seqlen, _ = q.shape
    n_chunks = seqlen // CHUNK
    z = f_logit.astype(f32)
    lb = lb.astype(f32)
    log_f = jax.nn.log_sigmoid(z) + jnp.log1p(lb * jnp.exp(-z))
    k = (1.0 - lb) * jax.nn.sigmoid(-z)

    def to_chunks(t, d):
        return t.astype(f32).reshape(bsz, n_chunks, CHUNK, HGRN_HEADS, d).transpose(1, 0, 3, 2, 4)

    qc, kc, lfc = to_chunks(q, HGRN_DK), to_chunks(k, HGRN_DK), to_chunks(log_f, HGRN_DK)
    vc = to_chunks(v, HGRN_DV)
    causal = jnp.tril(jnp.ones((CHUNK, CHUNK), dtype=bool))[:, :, None]

    def step(state, inp):
        qb, kb, vb, lfb = inp
        bcum = jnp.cumsum(lfb, axis=-2)
        rel = bcum[..., :, None, :] - bcum[..., None, :, :]
        decay = jnp.where(causal, jnp.exp(jnp.where(causal, rel, 0.0)), 0.0)
        scores = jnp.einsum('bhtd,bhsd,bhtsd->bhts', qb, kb, decay)
        o = (jnp.einsum('bhts,bhsv->bhtv', scores, vb)
             + jnp.einsum('bhtd,bhdv->bhtv', qb * jnp.exp(bcum), state))
        b_last = bcum[..., -1:, :]
        state = (jnp.exp(b_last[..., 0, :])[..., None] * state
                 + jnp.einsum('bhsd,bhsv->bhdv', kb * jnp.exp(b_last - bcum), vb))
        return state, o

    s0 = jnp.zeros((bsz, HGRN_HEADS, HGRN_DK, HGRN_DV), f32)
    _, o = lax.scan(step, s0, (qc, kc, vc, lfc))
    o = o.transpose(1, 0, 3, 2, 4).reshape(bsz, seqlen, HGRN_HEADS, HGRN_DV)
    gate = g.astype(f32).reshape(bsz, seqlen, HGRN_HEADS, HGRN_DV)
    o = rms_norm(o, out_gain) * jax.nn.silu(gate)
    return o.reshape(bsz, seqlen, HGRN_WIDTH).astype(q.dtype)

def fox_mixer(q, k, v, f_logit, f_bias, q_gain, k_gain):
    f32 = jnp.float32
    bsz, seqlen, _ = q.shape

    def heads(t):
        return t.reshape(bsz, seqlen, FOX_HEADS, HEAD_DIM).transpose(0, 2, 1, 3)

    qh = rms_norm(heads(q), q_gain) * (HEAD_DIM ** -0.5)
    kh = rms_norm(heads(k), k_gain)
    vh = heads(v)
    log_f = jax.nn.log_sigmoid((f_logit + f_bias).astype(f32))
    cum = jnp.cumsum(log_f, axis=1).transpose(0, 2, 1)
    kpos = jnp.arange(seqlen)

    def block(i):
        start = i * Q_BLOCK
        qb = lax.dynamic_slice_in_dim(qh, start, Q_BLOCK, axis=2)
        cb = lax.dynamic_slice_in_dim(cum, start, Q_BLOCK, axis=2)
        qpos = start + jnp.arange(Q_BLOCK)
        s = (jnp.einsum('bhqd,bhkd->bhqk', qb, kh).astype(f32)
             + (cb[..., :, None] - cum[..., None, :]))
        s = jnp.where(qpos[:, None] >= kpos[None, :], s, MASK_VALUE)
        p = jax.nn.softmax(s, axis=-1)
        return jnp.einsum('bhqk,bhkd->bhqd', p.astype(vh.dtype), vh)

    o = lax.map(block, jnp.arange(seqlen // Q_BLOCK))
    return o.transpose(1, 0, 3, 2, 4).reshape(bsz, seqlen, FOX_WIDTH)

def second_inputs(seed: int = 0) -> dict:
    key = jax.random.key(seed)
    ks = jax.random.split(key, 17)
    nrm = jax.random.normal
    f32 = jnp.float32
    return {
        "x": nrm(ks[0], (BATCH, SEQ, D_MODEL), f32),
        "ffn1_norm": 1.0 + 0.02 * nrm(ks[1], (DEPTH_2, D_MODEL), f32),
        "ffn1_w_in": nrm(ks[2], (DEPTH_2, D_MODEL, 2 * D_FF), f32) * D_MODEL ** -0.5,
        "ffn1_w_out": nrm(ks[3], (DEPTH_2, D_FF, D_MODEL), f32) * D_FF ** -0.5,
        "mix_norm": 1.0 + 0.02 * nrm(ks[4], (DEPTH_2, D_MODEL), f32),
        "w_mix_in": nrm(ks[5], (DEPTH_2, D_MODEL, MIX_IN), f32) * D_MODEL ** -0.5,
        "conv_w": nrm(ks[6], (DEPTH_2, CONV_WIDTH, CONV_CH), f32) * CONV_WIDTH ** -0.5,
        "hgrn_lb_logits": nrm(ks[7], (DEPTH_2, HGRN_QK), f32),
        "hgrn_out_gain": 1.0 + 0.02 * nrm(ks[8], (DEPTH_2, HGRN_DV), f32),
        "fox_q_gain": 1.0 + 0.02 * nrm(ks[9], (DEPTH_2, HEAD_DIM), f32),
        "fox_k_gain": 1.0 + 0.02 * nrm(ks[10], (DEPTH_2, HEAD_DIM), f32),
        "fox_f_bias": 2.0 + 0.5 * nrm(ks[11], (DEPTH_2, FOX_HEADS), f32),
        "w_mix_out": nrm(ks[12], (DEPTH_2, MIX_WIDTH, D_MODEL), f32) * MIX_WIDTH ** -0.5,
        "ffn2_norm": 1.0 + 0.02 * nrm(ks[13], (DEPTH_2, D_MODEL), f32),
        "ffn2_w_in": nrm(ks[14], (DEPTH_2, D_MODEL, 2 * D_FF), f32) * D_MODEL ** -0.5,
        "ffn2_w_out": nrm(ks[15], (DEPTH_2, D_FF, D_MODEL), f32) * D_FF ** -0.5,
    }

def second_block(x, ffn1_norm, ffn1_w_in, ffn1_w_out, mix_norm, w_mix_in, conv_w,
              hgrn_lb_logits, hgrn_out_gain, fox_q_gain, fox_k_gain, fox_f_bias,
              w_mix_out, ffn2_norm, ffn2_w_in, ffn2_w_out):
    lb_soft = jax.nn.softmax(hgrn_lb_logits.astype(jnp.float32), axis=0)
    lower_bounds = jnp.clip(jnp.cumsum(lb_soft, axis=0) - lb_soft[0:1], 0.0, 1.0)
    split_at = [int(s) for s in np.cumsum(MIX_IN_SIZES)[:-1]]
    for l in range(DEPTH_2):
        x = x + 0.5 * swiglu_2(rms_norm(x, ffn1_norm[l]), ffn1_w_in[l], ffn1_w_out[l])
        h = rms_norm(x, mix_norm[l]) @ w_mix_in[l]
        (c_x, c_b, c_c, h_q, h_f, h_i, h_g, f_q, f_k, f_v, f_f) = jnp.split(h, split_at, axis=-1)
        y = jnp.concatenate([
            short_conv_mixer(c_x, c_b, c_c, conv_w[l]),
            hgrn2_mixer(h_q, h_f, h_i, h_g, lower_bounds[l], hgrn_out_gain[l]),
            fox_mixer(f_q, f_k, f_v, f_f, fox_f_bias[l], fox_q_gain[l], fox_k_gain[l]),
        ], axis=-1)
        x = x + y @ w_mix_out[l]
        x = x + 0.5 * swiglu_2(rms_norm(x, ffn2_norm[l]), ffn2_w_in[l], ffn2_w_out[l])
    return x


def setup_inputs(seed=0):
    out = dict(first_inputs(seed))
    for name, value in second_inputs(seed + 1).items():
        if name != "x":
            out[name + "_2"] = value
    return out


def reference(
    x, c, w_ada, b_ada, norm_ff1, w_ff1_gate, w_ff1_up, w_ff1_down, norm_mix, w_in, w_gla_lr,
    b_gla_lr, gla_norm, rel_bias, w_br_gla, w_br_moba, w_out, norm_ff2, w_ff2_gate, w_ff2_up,
    w_ff2_down, norm_final, ffn1_norm_2, ffn1_w_in_2, ffn1_w_out_2, mix_norm_2, w_mix_in_2,
    conv_w_2, hgrn_lb_logits_2, hgrn_out_gain_2, fox_q_gain_2, fox_k_gain_2, fox_f_bias_2,
    w_mix_out_2, ffn2_norm_2, ffn2_w_in_2, ffn2_w_out_2,
):
    x = first_block(
        x, c, w_ada, b_ada, norm_ff1, w_ff1_gate, w_ff1_up, w_ff1_down, norm_mix, w_in,
        w_gla_lr, b_gla_lr, gla_norm, rel_bias, w_br_gla, w_br_moba, w_out, norm_ff2,
        w_ff2_gate, w_ff2_up, w_ff2_down, norm_final,
    )
    return second_block(
        x, ffn1_norm_2, ffn1_w_in_2, ffn1_w_out_2, mix_norm_2, w_mix_in_2, conv_w_2,
        hgrn_lb_logits_2, hgrn_out_gain_2, fox_q_gain_2, fox_k_gain_2, fox_f_bias_2,
        w_mix_out_2, ffn2_norm_2, ffn2_w_in_2, ffn2_w_out_2,
    )


_drawn_inputs = setup_inputs


def setup_inputs(seed=0):
    import zlib

    import numpy as np

    out = dict(_drawn_inputs(seed))
    spreads = {}
    factors = {'b_ada': 4.005,
     'norm_ff1': 4.383,
     'norm_mix': 2.799,
     'b_gla_lr': 5.848,
     'gla_norm': 6.442,
     'norm_ff2': 4.536,
     'ffn1_norm_2': 3.597,
     'hgrn_out_gain_2': 8.0,
     'fox_q_gain_2': 8.0,
     'fox_k_gain_2': 8.0,
     'ffn2_norm_2': 5.39}
    for name, (base, spread) in spreads.items():
        noise = np.random.default_rng([zlib.crc32(name.encode()), seed]).standard_normal(out[name].shape)
        drawn = base * np.exp(spread * noise) if base else spread * noise
        out[name] = __import__('jax').numpy.asarray(drawn.astype(out[name].dtype))
    for name, factor in factors.items():
        out[name] = (out[name] * factor).astype(out[name].dtype)
    return out
```

```python
from contextlib import ExitStack

import concourse.bass as bass
from concourse import mybir
import numpy as np

F32 = mybir.dt.float32
F32R = mybir.dt.float32r
U8 = mybir.dt.uint8
ALU = mybir.AluOpType
ACT = mybir.ActivationFunctionType
AX_X = mybir.AxisListType.X

P = 128
T = 256
TT = T // P
D = 1024
KD = D // P
F = 2816
KF = F // P
RING = 4
SLOT = 2048
LEAD = 2
NMOD = 9
ADA = NMOD * KD
ADA_FIRST = 2 * KD
EPS = 1e-6
NEG = -1e30
LEVELS = [128, 64, 32, 16, 8, 4, 2, 1, 0]
MAX_EXACT, NUM_BUCKETS, MAX_DISTANCE = 16, 32, 128
LIN_FIRST = 3
TAU = 16.0

GLA_CHUNKS = [("lq", 0, "f"), ("lk", 256, "f"), ("lv0", 512, "t"), ("lv1", 768, "t"),
              ("aq0", 1552, "f"), ("aq1", 1808, "f"), ("ak0", 2064, "f"), ("ak1", 2320, "f"),
              ("av0", 2576, "t"), ("av1", 2832, "t"), ("g0", 1040, "f"), ("g2", 1296, "f")] + \
             [(f"g{4 + 2 * i}", 3088 + 256 * i, "f") for i in range(8)]
MIX_CHUNKS = [("g8", 1024, "f"), ("lq", 768, "f"), ("lv0", 1280, "t"),
              ("aq0", 1792, "f"), ("aq1", 2048, "f"), ("ak0", 2304, "f"), ("ak1", 2560, "f"),
              ("av0", 2816, "t"), ("av1", 3072, "t"),
              ("g4", 0, "f"), ("g6", 512, "f"), ("g12", 256, "f"), ("g0", 1536, "f")]
GLR_AT, GLR_N = 1024, 16
FF_AT, FF_N = 3328, 8
IN_CHUNKS = [GLA_CHUNKS, MIX_CHUNKS, MIX_CHUNKS]
ATT_HEADS = [4, 8, 8]
ATT_DH = [128, 64, 64]
ATT_FIRST = [10, 9, 9]
LIN_DV = [128, 64, 64]
LIN_AT = [0, 2, 2]


def chunk_columns():
    cols, first = [], {}

    def add(name, counts):
        first[name] = len(cols)
        cols.extend(counts)

    def ffn(i):
        add(f"up{i}", [SLOT] * KF)
        add(f"down{i}", [KF // 2 * P] * (2 * KD))

    ffn(0)
    add("in0", [SLOT] * len(GLA_CHUNKS))
    add("branch", [KD * P] * KD)
    add("out0", [SLOT] * 4)
    ffn(1)
    for layer in (1, 2):
        ffn(2 * layer)
        add(f"in{layer}", [SLOT] * len(MIX_CHUNKS))
        add(f"out{layer}", [SLOT] * 4)
        ffn(2 * layer + 1)
    return cols, first


def mixer_steps(m):
    return max(len(IN_CHUNKS[m]), LIN_FIRST + len(LEVELS) + 2, ATT_FIRST[m] + ATT_HEADS[m] + 3)


COLS, FIRST = chunk_columns()
UNIT = {}


def count_units():
    n = 0
    names = sorted(FIRST, key=FIRST.get)
    for name in names:
        UNIT[name] = n
        n += {"up": KF, "do": KD, "br": KD, "ou": 4}.get(name[:2], 0)
        if name[:2] == "in":
            n += len(IN_CHUNKS[int(name[2:])])


count_units()
NORMS = ["up0", "in0", "up1", "final", "up2", "in1", "up3", "up4", "in2", "up5"]
SPLITS = ["up0", "in0", "branch", "out0", "up1", "up2", "in1", "out1", "up3", "up4", "in2", "out2", "up5"]

C_IDENT, C_ANTI, C_HEAD, C_CAUSAL = 0, 128, 256, 384
C_N = 512


def shape_constants():
    c = np.zeros((P, C_N), np.float32)
    i = np.arange(P)
    c[:, C_IDENT:C_IDENT + P] = np.eye(P)
    c[:, C_ANTI:C_ANTI + P] = np.eye(P)[::-1]
    c[:, C_HEAD:C_HEAD + P] = (i[:, None] // 64 == i[None, :] // 64)
    c[:, C_CAUSAL:C_CAUSAL + P] = np.where(i[:, None] >= i[None, :], 0.0, NEG)
    dist = (T - 1) - np.arange(384)
    n = np.maximum(dist, 0)
    nf = np.maximum(n, 1).astype(np.float32)
    large = MAX_EXACT + (np.log(nf / np.float32(MAX_EXACT)) / np.float32(np.log(MAX_DISTANCE / MAX_EXACT))
                         * np.float32(NUM_BUCKETS - MAX_EXACT)).astype(np.int32)
    bucket = np.where(n < MAX_EXACT, n, np.minimum(large, NUM_BUCKETS - 1))
    by_distance = np.zeros((NUM_BUCKETS + 4, 384), np.float32)
    by_distance[bucket, np.arange(384)] = 1.0
    by_distance[NUM_BUCKETS:] = np.where(dist >= 0, 0.0, NEG)
    m = np.zeros((P, len(LEVELS) - 1, P), np.float32)
    key, query = i[:, None], i[None, :]
    for n, s in enumerate(LEVELS[1:]):
        if s:
            m[:, n] = (key // (2 * s) == query // (2 * s)) & (key % (2 * s) < s) & (query % (2 * s) >= s)
        else:
            m[:, n] = key == query
    return c, m.reshape(P, -1), by_distance


def build(nc, a, out):
    with ExitStack() as ctx:
        ctx.enter_context(nc.allow_non_contiguous_dma(reason="two vectors of a few elements"))
        def sb(name, shape, dt=F32):
            return ctx.enter_context(nc.sbuf_tensor(name, shape, dt))

        def sem(name):
            return ctx.enter_context(nc.semaphore(name))

        raw = sb("raw", [P, RING, SLOT])
        whi = sb("whi", [P, RING, SLOT], F32R)
        wlo = sb("wlo", [P, RING, SLOT], F32R)
        h = sb("h", [P, KD, T])
        u = sb("u", [P, KD, T])
        uhi = sb("uhi", [P, KD, T], F32R)
        ulo = sb("ulo", [P, KD, T], F32R)
        work = sb("work", [P, 4, T])
        silu, hid = work[:, 0:2], work[:, 2:4]
        dec = work[:].rearrange("p (a b) t -> p a b t", a=2)
        f8 = work[0:8]
        glr = work[0:GLR_N, 2]
        toe_row = work[0:4, 0:2].rearrange("p a t -> p (a t)")[:, 0:384]
        in_turn = sb("in_turn", [P, 2 * KD * P])
        ada_raw = in_turn[:].rearrange("p (a k c) -> p a k c", a=2, k=KD)
        qz = in_turn[:].rearrange("p (a t) -> p a t", t=T)
        ada_acc = sb("ada_acc", [P, 2, P])
        const = sb("const", [P, C_N])
        ones = sb("ones", [P, P])
        vec_a = sb("vec_a", [P, P])
        vec_b = sb("vec_b", [P, P])
        c_act = sb("c_act", [P, KD])
        mod = sb("mod", [P, ADA])
        gain = sb("gain", [P, 3, KD])
        half = sb("half", [P, 2 * KD])
        eps = sb("eps", [P, 1])
        zero8 = sb("zero8", [P, KD])
        half8 = sb("half8", [P, KD])
        sumsq = sb("sumsq", [P, T])
        sq = sb("sq", [P, T])
        stage = sq[:].rearrange("p (a c) -> p a c", a=2)
        rstd = sb("rstd", [P, T])
        wlr = sb("wlr", [P, KD, GLR_N])
        wff = sb("wff", [P, 2, KD, FF_N])
        wgl = sb("wgl", [GLR_N, 256])
        rel = sb("rel", [NUM_BUCKETS, 4])
        fbias = sb("fbias", [8, 2])
        negc = sb("negc", [P, T])
        lb = sb("lb", [P, 8])
        lbt = sb("lbt", [P, 12])
        st_max = sb("st_max", [P, 2, 8])
        scratch = nc.dram_tensor("bias_by_distance", [4, 384], F32)

        intra = sb("intra", [P, 8, P])
        level_mask = sb("level_mask", [P, len(LEVELS) - 1, P], U8)
        toe = sb("toe", [P, 4, T])
        qk_sq = toe

        hidden = ExitStack()
        hhi = hidden.enter_context(nc.sbuf_tensor("hhi", [P, KF, T], F32R))
        hlo = hidden.enter_context(nc.sbuf_tensor("hlo", [P, KF, T], F32R))
        hidden.close()
        lv = sb("lv", [P, TT, 512])
        aq = sb("aq", [P, 4, T])
        ak = sb("ak", [P, 4, T])
        av = sb("av", [P, TT, 512])
        gat = sb("gat", [P, 20, T])
        lq, lk = gat[:, 16:18], gat[:, 18:20]
        mask_in = gat[:].rearrange("p a t -> p (a t)")[:, 0:(len(LEVELS) - 1) * P]
        bcum = sb("bcum", [P, 2, T])
        xqk = sb("xqk", [P, 2, 2, T])
        cross = sb("cross", [P, 4, P])
        prob = sb("prob", [P, 384])
        prob_t = sb("prob_t", [P, 384])

        psum = [ctx.enter_context(nc.psum_tensor(f"bank{i}", [P, 512], F32)) for i in range(4)]
        wide = ctx.enter_context(nc.psum_tensor("wide", [P, 1024], F32))
        ps_score = ctx.enter_context(nc.psum_tensor("ps_score", [P, 512], F32))
        ps_turn = ctx.enter_context(nc.psum_tensor("ps_turn", [P, 512], F32))
        acc = psum[0:2]
        ps_stat, ps_mod = psum[2], psum[3]

        ident = const[:, C_IDENT:C_IDENT + P]
        anti = const[:, C_ANTI:C_ANTI + P]
        same_head = const[:, C_HEAD:C_HEAD + P]
        causal = const[:, C_CAUSAL:C_CAUSAL + P]

        def pick(hd):
            return const[:, C_IDENT + hd:C_IDENT + hd + 1].to_broadcast([P, P])

        landed = [sem(f"landed{i}") for i in range(RING)]
        hi_ready = sem("hi_ready")
        lo_ready = sem("lo_ready")
        chunk_used = sem("chunk_used")
        evacuated = sem("evacuated")
        silu_ready = sem("silu_ready")
        hhi_ready = sem("hhi_ready")
        hlo_ready = sem("hlo_ready")
        ada_landed = [sem(f"ada_landed{i}") for i in range(2)]
        ada_summed = sem("ada_summed")
        mod_ready = sem("mod_ready")
        small = sem("small")
        consts = sem("consts")
        x_in = sem("x_in")
        set_up = sem("set_up")
        turned_a = sem("turned_a")
        vec_ready = sem("vec_ready")
        c_ready = sem("c_ready")
        x_turned = sem("x_turned")
        x_taken = sem("x_taken")
        mods = sem("mods")
        summed = sem("summed")
        stat = sem("stat")
        rms = sem("rms")
        scaled = sem("scaled")
        u_ready = sem("u_ready")
        uhi_ready = sem("uhi_ready")
        ulo_ready = sem("ulo_ready")
        mixed = sem("mixed")
        pe_glr, dve_glr, pe_z = sem("pe_glr"), sem("dve_glr"), sem("pe_z")
        z_ready = sem("z_ready")
        l_ready = sem("l_ready")
        kexp_in, kexp_out = sem("kexp_in"), sem("kexp_out")
        diffs, decays = sem("diffs"), sem("decays")
        xqk_ready, level_ready, level_taken = sem("xqk_ready"), sem("level_ready"), sem("level_taken")
        lin_ready, lin_taken = sem("lin_ready"), sem("lin_taken")
        lin_sq, lin_stat, lin_rms = sem("lin_sq"), sem("lin_stat"), sem("lin_rms")
        gate_sig = sem("gate_sig")
        f_ready, f_taken, f_log, negc_ready = sem("f_ready"), sem("f_taken"), sem("f_log"), sem("negc_ready")
        scores_ready, max_ready, exp_ready = sem("scores_ready"), sem("max_ready"), sem("exp_ready")
        prob_ready, prob_turned, prob_t_ready = sem("prob_ready"), sem("prob_turned"), sem("prob_t_ready")
        att_ready, att_taken = sem("att_ready"), sem("att_taken")
        toe_psum, toe_sb, toe_out, toe_in = sem("toe_psum"), sem("toe_sb"), sem("toe_out"), sem("toe_in")
        qk_squared, qk_summed, qk_root, qk_normed = sem("qk_squared"), sem("qk_summed"), sem("qk_root"), sem("qk_normed")
        lb_in, lb_exp = sem("lb_in"), sem("lb_exp")
        out_turned, out_taken, stored = sem("out_turned"), sem("out_taken"), sem("stored")
        dve_done, act_done, pool_done = sem("dve_done"), sem("act_done"), sem("pool_done")

        A_C, A_FF1, A_MIX, A_FF2, A_FIN, A_ADA = 0, 8, 16, 24, 32, 40
        A_GLAN, A_BGL, A_HG, A_FQ, A_FK = 112, 113, 115, 117, 119
        B_FF1, B_MIX, B_FF2, B_LB, B_CONV = 0, 16, 32, 48, 52
        A_ROWS, B_ROWS = 121, 64

        def rows(ap):
            return ap.rearrange("l (k c) -> (l k) c", c=P)

        small_loads = [
            (stage[A_C:A_C + 8, 0], rows(a["c"])), (stage[A_FF1:A_FF1 + 8, 0], rows(a["norm_ff1"])),
            (stage[A_MIX:A_MIX + 8, 0], rows(a["norm_mix"])), (stage[A_FF2:A_FF2 + 8, 0], rows(a["norm_ff2"])),
            (stage[A_FIN:A_FIN + 8, 0], a["norm_final"].rearrange("(k c) -> k c", c=P)),
            (stage[A_ADA:A_ADA + ADA, 0], rows(a["b_ada"])),
            (stage[A_GLAN:A_GLAN + 1, 0], a["gla_norm"]), (stage[A_BGL:A_BGL + 2, 0], rows(a["b_gla_lr"])),
        ]
        for at, name in ((A_HG, "hgrn_out_gain_2"), (A_FQ, "fox_q_gain_2"), (A_FK, "fox_k_gain_2")):
            small_loads += [(stage[at:at + 2, 0, 64 * i:64 * i + 64], a[name]) for i in range(2)]
        small_loads += [
            (stage[B_FF1:B_FF1 + 16, 1], rows(a["ffn1_norm_2"])), (stage[B_MIX:B_MIX + 16, 1], rows(a["mix_norm_2"])),
            (stage[B_FF2:B_FF2 + 16, 1], rows(a["ffn2_norm_2"])), (stage[B_LB:B_LB + 4, 1], rows(a["hgrn_lb_logits_2"])),
            (stage[B_CONV:B_CONV + 12, 1], a["conv_w_2"].rearrange("l w (k c) -> (l w k) c", c=P)),
            (wgl[:], a["w_gla_lr"][0]),
            (wlr[:], a["w_in"][0, :, GLR_AT:GLR_AT + GLR_N].rearrange("(k p) c -> p k c", p=P)),
            (wff[:, 0], a["w_mix_in_2"][0, :, FF_AT:FF_AT + FF_N].rearrange("(k p) c -> p k c", p=P)),
            (wff[:, 1], a["w_mix_in_2"][1, :, FF_AT:FF_AT + FF_N].rearrange("(k p) c -> p k c", p=P)),
            (rel[:], a["rel_bias"].rearrange("h b -> b h")),
            (fbias[:], a["fox_f_bias_2"].rearrange("l h -> h l")),
        ]

        small_loads += [(prob[0:NUM_BUCKETS, :], a["by_distance"][0:NUM_BUCKETS]),
                        (prob_t[0:4, :], a["by_distance"][NUM_BUCKETS:])]

        w2 = a["ffn1_w_in_2"], a["ffn2_w_in_2"]
        ffn_w = [(a["w_ff1_gate"][0], a["w_ff1_up"][0], a["w_ff1_down"][0]),
                 (a["w_ff2_gate"][0], a["w_ff2_up"][0], a["w_ff2_down"][0])]
        for layer in range(2):
            for n in range(2):
                w = w2[n][layer]
                ffn_w.append((w[:, 0:F], w[:, F:2 * F], a[f"ffn{n + 1}_w_out_2"][layer]))
        in_w = [a["w_in"][0], a["w_mix_in_2"][0], a["w_mix_in_2"][1]]
        out_w = [a["w_out"][0], a["w_mix_out_2"][0], a["w_mix_out_2"][1]]

        def norm_gain(name):
            if name in ("up0", "in0", "up1"):
                j = ("up0", "in0", "up1").index(name)
                return gain[:, j], mod[:, 3 * j * KD:(3 * j + 1) * KD]
            if name == "final":
                return vec_a[:, A_FIN:A_FIN + 8], zero8
            at = {"up2": B_FF1, "in1": B_MIX, "up3": B_FF2, "up4": B_FF1 + 8, "in2": B_MIX + 8, "up5": B_FF2 + 8}[name]
            return vec_b[:, at:at + 8], zero8

        def residual_gate(i):
            return [half[:, 0:8], half[:, 8:16]][i] if i < 2 else half8

        def seg(name):
            return FIRST[name], UNIT[name]

        def kview(tile, slot, k, width):
            return tile[:, slot, 0:k * width].rearrange("p (k c) -> p k c", k=k)

        class Chain:

            def __init__(self, eng, done):
                self.eng, self.done, self.n, self.turn, self.per = eng, done, 0, None, 0

            def __call__(self, ins):
                self.n += 1
                ins.then_inc(self.done, 1)
                self.eng.wait_ge(self.done, self.n if self.turn is None else self.turn * self.per + self.n)

            def loop(self, turn, per):
                self.turn, self.per, self.n0 = turn, per, self.n

            def end(self, turns):
                assert self.n - self.n0 == self.per, (self.n - self.n0, self.per)
                self.n, self.turn = self.n0 + self.per * turns, None

        block = ctx.enter_context(nc.Block())

        @block.sync
        def _(sp):
            def ada_load(t, it=0):
                sp.wait_ge(ada_summed, it * 4 + t + 1)
                sp.dma_start(ada_raw[:, t % 2],
                             a["w_ada"][0, :, bass.ds(it * 4 * P + t * P, P)].rearrange("(k p) c -> p k c", p=P)
                             ).then_inc(ada_landed[t % 2], 16)

            def load(n, parts, it=0):
                sp.wait_ge(lo_ready, it * RING + n + 1)
                for dst, src in parts:
                    sp.dma_start(dst, src).then_inc(landed[n % RING], 16)

            def up_parts(i, n, t, it=0):
                wg, wu, _ = ffn_w[i]
                v = kview(raw, n % RING, KD, 2 * P)
                return [(v[:, :, j * P:(j + 1) * P],
                         w[:, bass.ds(it * RING * P + t * P, P)].rearrange("(k p) c -> p k c", p=P))
                        for j, w in enumerate((wg, wu))]

            def down_parts(i, n, d, it=0):
                wd = ffn_w[i][2]
                v = kview(raw, n % RING, KF // 2, P)
                src = wd[(d % 2) * (F // 2):(d % 2 + 1) * (F // 2), bass.ds(it * 2 * P + d // 2 * P, P)]
                src = src.rearrange("(k p) c -> p k c", p=P)
                return [(v[:, 0:6], src[:, 0:6]), (v[:, 6:11], src[:, 6:11])]

            def ffn(i):
                n0 = FIRST[f"up{i}"]
                with sp.Fori(0, KF // RING) as it:
                    for t in range(RING):
                        load(n0 + t, up_parts(i, n0 + t, t, it), it)
                        if i == 0:
                            ada_load(ADA_FIRST + t, it)
                for t in range(KF // RING * RING, KF):
                    load(n0 + t, up_parts(i, n0 + t, t))
                    if i == 0:
                        ada_load(ADA_FIRST + t)
                n0 = FIRST[f"down{i}"]
                with sp.Fori(0, 2 * KD // RING) as it:
                    for t in range(RING):
                        load(n0 + t, down_parts(i, n0 + t, t, it), it)
                        if i == 0:
                            ada_load(ADA_FIRST + KF + t, it)

            def plain(w, n, at):
                v = kview(raw, n % RING, KD, 256)
                src = w[:, at:at + 256].rearrange("(k p) c -> p k c", p=P)
                return [(v[:, 4 * j:4 * j + 4], src[:, 4 * j:4 * j + 4]) for j in range(2)]

            def mixer(m):
                n0 = FIRST[f"in{m}"]
                for s, (_, at, _) in enumerate(IN_CHUNKS[m]):
                    load(n0 + s, plain(in_w[m], n0 + s, at))
                    if m == 0 and ADA_FIRST + KF + 2 * KD + s < ADA:
                        ada_load(ADA_FIRST + KF + 2 * KD + s)
                if m == 0:
                    n0 = FIRST["branch"]
                    for t in range(KD):
                        v = kview(raw, (n0 + t) % RING, KD, P)
                        load(n0 + t, [(v[:, 4 * j:4 * j + 4],
                                       w[0, :, t * P:(t + 1) * P].rearrange("(k p) c -> p k c", p=P))
                                      for j, w in enumerate((a["w_br_gla"], a["w_br_moba"]))])
                n0 = FIRST[f"out{m}"]
                for t in range(4):
                    load(n0 + t, plain(out_w[m], n0 + t, 256 * t))

            for t in range(ADA_FIRST):
                ada_load(t)
            ffn(0)
            mixer(0)
            ffn(1)
            for layer in (1, 2):
                ffn(2 * layer)
                mixer(layer)
                ffn(2 * layer + 1)
            for tt in range(TT):
                sp.wait_ge(out_taken, 2 * (tt + 1))
                sp.dma_start(out[0, tt * P:(tt + 1) * P], u[:].rearrange("p k t -> p (k t)")[:, tt * D:(tt + 1) * D]
                             ).then_inc(stored, 16)
            sp.wait_ge(stored, 16 * TT)

        @block.gpsimd
        def _(pool):
            link = Chain(pool, pool_done)
            norms = [0]

            def sum_of_squares(tile, ready, at, tiles):
                if norms[0]:
                    pool.wait_ge(stat, norms[0])
                for k in range(KD):
                    if k % tiles == 0:
                        pool.wait_ge(ready, at + k // tiles + 1)
                    if k == 0:
                        link(nc.gpsimd.tensor_tensor(sumsq[:], tile[:, 0], tile[:, 0], ALU.mult))
                        continue
                    link(nc.gpsimd.tensor_tensor(sq[:], tile[:, k], tile[:, k], ALU.mult))
                    ins = nc.gpsimd.tensor_tensor(sumsq[:], sumsq[:], sq[:], ALU.add)
                    if k < KD - 1:
                        link(ins)
                ins.then_inc(summed, 1)
                norms[0] += 1

            def sums_over_units(name, tiles):
                sum_of_squares(h, evacuated, 2 + UNIT[name], tiles)

            def affine(name, dst):
                g, b = norm_gain(name)
                i = NORMS.index(name)
                for kk in range(4):
                    pool.wait_ge(scaled, 4 * i + kk + 1)
                    for k in (2 * kk, 2 * kk + 1):
                        ins = nc.gpsimd.tensor_scalar(dst[:, k], dst[:, k], g[:, k:k + 1], b[:, k:k + 1],
                                                      ALU.mult, ALU.add)
                    ins.then_inc(u_ready, 1)

            pool.dma_start(const[:], a["shape_constants"]).then_inc(consts, 16)
            pool.dma_start(mask_in, a["level_masks"]).then_inc(consts, 16)
            sum_of_squares(h, x_taken, 0, 1)
            affine("up0", u)
            sums_over_units("down0", 1)
            affine("in0", u)
            sums_over_units("out0", 2)
            affine("up1", u)
            sums_over_units("down1", 1)
            affine("final", h)
            sum_of_squares(h, u_ready, 4 * NORMS.index("final"), 2)
            for layer in (1, 2):
                affine(f"up{2 * layer}", u)
                sums_over_units(f"down{2 * layer}", 1)
                affine(f"in{layer}", u)
                sums_over_units(f"out{layer}", 2)
                affine(f"up{2 * layer + 1}", u)
                if layer == 1:
                    sums_over_units(f"down{2 * layer + 1}", 1)

        @block.scalar
        def _(act):
            link = Chain(act, act_done)

            def split_hi(n, it=0):
                cols = COLS[n]
                act.wait_ge(landed[n % RING], it * 32 + 32 * (n // RING + 1))
                act.wait_ge(chunk_used, it * RING + n + 1)
                nc.scalar.copy(whi[:, n % RING, 0:cols], raw[:, n % RING, 0:cols]).then_inc(hi_ready, 1)

            def split_ahead(n, it=0):
                if n + LEAD < len(COLS):
                    split_hi(n + LEAD, it)

            def split_u(name, ready, at):
                for kk in range(4):
                    act.wait_ge(ready, at + kk + 1)
                    nc.scalar.copy(uhi[:, 2 * kk:2 * kk + 2], u[:, 2 * kk:2 * kk + 2]).then_inc(uhi_ready, 1)

            def root_of_mean(name):
                i = NORMS.index(name)
                act.wait_ge(stat, i + 1)
                nc.scalar.activation(rstd[:], ps_stat[:, 0:T], ACT.Sqrt, bias=eps[:], scale=1.0 / D).then_inc(rms, 1)

            def norm(name):
                root_of_mean(name)
                if name != "final":
                    split_u(name, u_ready, 4 * NORMS.index(name))

            def ffn(i):
                n0, e0 = seg(f"up{i}")

                def step(t, it=0):
                    split_ahead(n0 + t, it)
                    act.wait_ge(chunk_used, it * RING + RING + n0 + t + 1)
                    nc.scalar.activation(silu[:, t % 2], acc[(e0 + t) % 2][:, 0:T], ACT.Silu).then_inc(silu_ready, 1)
                    act.wait_ge(evacuated, it * RING + 2 + e0 + t + 1)
                    dst = hhi[:, t] if isinstance(it, int) else hhi[:, bass.ds(it * RING + t, 1)].rearrange("p a t -> p (a t)")
                    nc.scalar.copy(dst, hid[:, t % 2]).then_inc(hhi_ready, 1)

                with act.Fori(0, KF // RING) as it:
                    for t in range(RING):
                        step(t, it)
                for t in range(KF // RING * RING, KF):
                    step(t)
                n0, e0 = seg(f"down{i}")
                with act.Fori(0, 2 * KD // RING - 1) as it:
                    for t in range(RING):
                        split_ahead(n0 + t, it)
                for t in range(2 * KD - RING, 2 * KD):
                    split_ahead(n0 + t)

            def mixer(m):
                n0, e0 = seg(f"in{m}")
                steps = len(IN_CHUNKS[m])
                last = mixer_steps(m)
                z, t_, l_ = gat[:, 8:10], gat[:, 4:6], gat[:, 6:8]
                for s in range(last):
                    if s == 2:
                        if m == 0:
                            act.wait_ge(z_ready, 1)
                        else:
                            act.wait_ge(evacuated, 2 + e0 + 1)
                        link(nc.scalar.activation(t_, z, ACT.Abs))
                        link(nc.scalar.activation(t_, t_, ACT.Exp, scale=-1.0))
                        if m:
                            link(nc.scalar.activation(gat[:, 12:14], z, ACT.Exp, scale=-1.0))
                        nc.scalar.activation(l_, t_, ACT.Ln, bias=1.0).then_inc(l_ready, 1)
                        if m:
                            for hp in range(2):
                                j = 2 * (m - 1) + hp
                                ins = nc.scalar.activation(gat[:, 14 + hp], gat[:, 12 + hp], ACT.Ln, bias=1.0,
                                                           scale=lb[:, j:j + 1])
                            ins.then_inc(l_ready, 1)
                            act.wait_ge(f_taken, m)
                            link(nc.scalar.activation(f8[:, 1], f8[:, 0], ACT.Abs))
                            link(nc.scalar.activation(f8[:, 1], f8[:, 1], ACT.Exp, scale=-1.0))
                            nc.scalar.activation(f8[:, 2], f8[:, 1], ACT.Ln, bias=1.0).then_inc(f_log, 1)
                    if m and s == LIN_FIRST:
                        act.wait_ge(kexp_in, m)
                        nc.scalar.activation(lk, t_, ACT.Exp, scale=-1.0).then_inc(kexp_out, 1)
                    if m and s in (6, 8):
                        c = 2 * (m - 1) + (s == 8)
                        for half_, ps in enumerate((ps_turn, ps_score)):
                            act.wait_ge(qk_summed, 2 * c + half_ + 1)
                            nc.scalar.activation(qk_sq[:, 2 * half_:2 * half_ + 2],
                                                 ps[:].rearrange("p (a t) -> p a t", a=2), ACT.Sqrt, bias=eps[:],
                                                 scale=1.0 / ATT_DH[m]).then_inc(qk_root, 1)
                    l = s - LIN_FIRST
                    if 0 <= l < len(LEVELS) - 1:
                        c = m * (len(LEVELS) - 1) + l + 1
                        act.wait_ge(diffs, c)
                        nc.scalar.activation(dec[:, l % 2], dec[:, l % 2], ACT.Exp,
                                             scale=1.0 / TAU if m == 0 else 1.0).then_inc(decays, 1)
                    t = s - ATT_FIRST[m]
                    if 0 <= t < ATT_HEADS[m]:
                        c = sum(ATT_HEADS[:m]) + t + 1
                        act.wait_ge(max_ready, c)
                        act.wait_ge(prob_turned, c - 1) if c > 1 else None
                        for j, (lo, hi) in enumerate(((0, P), (P, 3 * P))):
                            ins = nc.scalar.activation(prob[:, lo:hi], ps_score[:, lo:hi], ACT.Exp,
                                                       bias=st_max[:, t % 2, 2 + j:3 + j],
                                                       accum_out=st_max[:, t % 2, 4 + j:5 + j])
                            ins.then_inc(exp_ready, 1)
                    if s < steps:
                        split_ahead(n0 + s)
                w = LIN_DV[m] * 4 // P
                lin = u[:, LIN_AT[m]:LIN_AT[m] + w]
                xs = xqk[:].rearrange("p a b t -> p (a b) t")[:, 0:w]
                ds = dec.rearrange("p a b t -> p (a b) t")[:, 0:w]
                act.wait_ge(lin_taken, m + 1)
                nc.scalar.activation(xs, lin, ACT.Square).then_inc(lin_sq, 1)
                act.wait_ge(lin_stat, m + 1)
                nc.scalar.activation(xs, wide[:, 0:w * T].rearrange("p (k t) -> p k t", t=T), ACT.Sqrt, bias=eps[:],
                                     scale=1.0 / LIN_DV[m]).then_inc(lin_rms, 1)
                nc.scalar.activation(ds, gat[:, 0:w], ACT.Sigmoid).then_inc(gate_sig, 1)
                if m == 0:
                    nc.scalar.activation(gat[:, 4:20], gat[:, 4:20], ACT.Sigmoid).then_inc(gate_sig, 1)
                split_u(f"y{m}", mixed, 4 * (m + (m > 0)))
                if m == 0:
                    n0 = FIRST["branch"]
                    for t in range(KD):
                        split_ahead(n0 + t)
                    act.wait_ge(chunk_used, RING + FIRST["out0"])
                    split_u("merged", mixed, 4)
                n0 = FIRST[f"out{m}"]
                for t in range(4):
                    split_ahead(n0 + t)

            act.dma_start(u[:].rearrange("p k t -> p (k t)").rearrange("p (a d) -> p a d", a=TT),
                          a["x"][0].rearrange("(a p) d -> p a d", p=P)).then_inc(x_in, 16)
            for dst, src in small_loads:
                act.dma_start(dst, src).then_inc(small, 16)
            act.wait_ge(vec_ready, 1)
            nc.scalar.activation(c_act[:], vec_a[:, A_C:A_C + 8], ACT.Silu).then_inc(c_ready, 1)
            act.wait_ge(lb_in, 1)
            nc.scalar.activation(lbt[:, 4:8], lbt[:, 0:4], ACT.Exp).then_inc(lb_exp, 1)
            act.wait_ge(toe_sb, 1)
            act.dma_start(scratch[:], toe_row).then_inc(toe_out, 16)
            act.wait_ge(toe_out, 16)
            act.dma_start(toe[:], bass.AP(scratch, 0, [[1, P], [384, 4], [1, T]])).then_inc(toe_in, 16)
            for n in range(LEAD):
                split_hi(n)
            norm("up0")
            ffn(0)
            norm("in0")
            mixer(0)
            norm("up1")
            ffn(1)
            norm("final")
            for layer in (1, 2):
                norm(f"up{2 * layer}")
                ffn(2 * layer)
                norm(f"in{layer}")
                mixer(layer)
                norm(f"up{2 * layer + 1}")
                ffn(2 * layer + 1)

        @block.vector
        def _(dve):
            link = Chain(dve, dve_done)

            def split_lo(n, it=0):
                cols = COLS[n]
                dve.wait_ge(hi_ready, it * RING + n + 1)
                nc.vector.tensor_tensor(wlo[:, n % RING, 0:cols], raw[:, n % RING, 0:cols],
                                        whi[:, n % RING, 0:cols].bitcast(F32), ALU.subtract).then_inc(lo_ready, 1)

            def split_ahead(n, it=0):
                if n + LEAD < len(COLS):
                    split_lo(n + LEAD, it)

            def split_u(name):
                q = SPLITS.index(name)
                for kk in range(4):
                    s = slice(2 * kk, 2 * kk + 2)
                    dve.wait_ge(uhi_ready, 4 * q + kk + 1)
                    nc.vector.tensor_tensor(ulo[:, s], u[:, s], uhi[:, s].bitcast(F32), ALU.subtract
                                            ).then_inc(ulo_ready, 1)

            def norm(name):
                dst = h if name == "final" else u
                dve.wait_ge(rms, NORMS.index(name) + 1)
                link(nc.vector.reciprocal(rstd[:], rstd[:]))
                for kk in range(4):
                    s = slice(2 * kk, 2 * kk + 2)
                    nc.vector.tensor_tensor(dst[:, s], h[:, s], rstd[:].unsqueeze(1).to_broadcast([P, 2, T]),
                                            ALU.mult).then_inc(scaled, 1)
                if name != "final":
                    split_u(name)

            def ada_sum(t, it=0):
                dve.wait_ge(ada_landed[t % 2], it * 32 + 16 * (t // 2 + 1))
                dve.wait_ge(mod_ready, it * RING + t + 1)
                for k in range(KD):
                    w, s = ada_raw[:, t % 2, k], ada_acc[:, t % 2]
                    if k == 0:
                        ins = nc.vector.tensor_scalar(s, w, c_act[:, 0:1], None, ALU.mult)
                    else:
                        ins = nc.vector.scalar_tensor_tensor(out=s, in0=w, scalar=c_act[:, k:k + 1], in1=s,
                                                             op0=ALU.mult, op1=ALU.add)
                    if k < KD - 1:
                        link(ins)
                ins.then_inc(ada_summed, 1)

            def mod_take(lo, hi, made):
                dve.wait_ge(mod_ready, 2 + made)
                link(nc.vector.tensor_tensor(mod[:, lo:hi], ps_mod[:, lo:hi], vec_a[:, A_ADA + lo:A_ADA + hi], ALU.add))

            def gain_make(j, at):
                link(nc.vector.tensor_scalar(gain[:, j], mod[:, (3 * j + 1) * KD:(3 * j + 2) * KD], 1.0, None, ALU.add))
                nc.vector.tensor_tensor(gain[:, j], gain[:, j], vec_a[:, at:at + 8], ALU.mult).then_inc(mods, 1)

            def ffn(i):
                n0, e0 = seg(f"up{i}")

                def step(t, it=0):
                    if i == 0:
                        ada_sum(ADA_FIRST + t, it)
                    split_ahead(n0 + t, it)
                    dve.wait_ge(silu_ready, it * RING + KF * i + t + 1)
                    nc.vector.tensor_tensor(hid[:, t % 2], silu[:, t % 2], acc[(e0 + t) % 2][:, T:2 * T], ALU.mult
                                            ).then_inc(evacuated, 1)
                    dve.wait_ge(hhi_ready, it * RING + KF * i + t + 1)
                    at = t if isinstance(it, int) else bass.ds(it * RING + t, 1)
                    d, s = hlo[:, at], hhi[:, at]
                    if not isinstance(it, int):
                        d, s = d.rearrange("p a t -> p (a t)"), s.rearrange("p a t -> p (a t)")
                    nc.vector.tensor_tensor(d, hid[:, t % 2], s.bitcast(F32), ALU.subtract).then_inc(hlo_ready, 1)

                with dve.Fori(0, KF // RING) as it:
                    if i == 0:
                        link.loop(it, RING * (KD - 1))
                    for t in range(RING):
                        step(t, it)
                if i == 0:
                    link.end(KF // RING)
                for t in range(KF // RING * RING, KF):
                    step(t)
                if i == 0:
                    mod_take(2 * KD, 3 * KD, ADA_FIRST + KF)
                    link(nc.vector.tensor_scalar(half[:, 0:8], mod[:, 2 * KD:3 * KD], 0.5, None, ALU.mult))
                n0, e0 = seg(f"down{i}")
                g = residual_gate(i)

                def down(t, it=0):
                    if i == 0:
                        ada_sum(ADA_FIRST + KF + t, it)
                    split_ahead(n0 + t, it)
                    if t % 2:
                        m = t // 2
                        dve.wait_ge(chunk_used, it * RING + RING + n0 + t + 1)
                        if isinstance(it, int):
                            gm, hm = g[:, m:m + 1], h[:, m]
                        else:
                            gm, hm = g[:, bass.ds(it * 2 + m, 1)], h[:, bass.ds(it * 2 + m, 1)].rearrange("p a t -> p (a t)")
                        nc.vector.scalar_tensor_tensor(out=hm, in0=acc[(e0 + m) % 2][:, 0:T], scalar=gm, in1=hm,
                                                       op0=ALU.mult, op1=ALU.add).then_inc(evacuated, 1)

                turns = 2 * KD // RING - 1
                with dve.Fori(0, turns) as it:
                    if i == 0:
                        link.loop(it, RING * (KD - 1))
                    for t in range(RING):
                        down(t, it)
                if i == 0:
                    link.end(turns)
                for t in range(2 * KD - RING, 2 * KD):
                    down(t)

            def log_gates(m):
                z, l_, la, t_ = gat[:, 8:10], gat[:, 6:8], gat[:, 10:12], gat[:, 4:6]
                dve.wait_ge(l_ready, [1, 3, 5][m])
                link(nc.vector.tensor_scalar(la, z, 0.0, None, ALU.min))
                link(nc.vector.tensor_tensor(la, la, l_, ALU.subtract))
                if m:
                    link(nc.vector.tensor_tensor(la, la, gat[:, 14:16], ALU.add))
                    link(nc.vector.tensor_scalar(t_, z, 0.0, None, ALU.max))
                    nc.vector.tensor_tensor(t_, t_, l_, ALU.add).then_inc(kexp_in, 1)
                for hp in range(2):
                    for tt in range(TT):
                        v = la[:, hp, tt * P:(tt + 1) * P]
                        link(nc.vector.tensor_tensor_scan(bcum[:, hp, tt * P:(tt + 1) * P], v, v, 0.0,
                                                          ALU.add, ALU.bypass))
                if m:
                    dve.wait_ge(kexp_out, m)
                    for hp in range(2):
                        j = 2 * (m - 1) + hp
                        link(nc.vector.tensor_scalar(lk[:, hp], lk[:, hp], lb[:, 4 + j:5 + j], None, ALU.mult))
                    dve.wait_ge(f_log, m)
                    link(nc.vector.tensor_scalar(f8[:, 0], f8[:, 0], 0.0, None, ALU.min))
                    link(nc.vector.tensor_tensor(f8[:, 0], f8[:, 2], f8[:, 0], ALU.subtract))
                    nc.vector.tensor_tensor_scan(negc[0:8], f8[:, 0], f8[:, 0], 0.0, ALU.add, ALU.bypass
                                                 ).then_inc(negc_ready, 1)
                    dve.wait_ge(negc_ready, m)

            def halves(tile, s):
                v = tile.rearrange("p a (n b s) -> p (a n) b s", b=2, s=s)
                return v[:, :, 0], v[:, :, 1]

            def level_diffs(m, l):
                s = LEVELS[l]
                bl, br = halves(bcum[:], s)
                dl, dr = halves(dec[:, l % 2], s)
                if s == P:
                    nc.vector.tensor_copy(dr, br)
                    last = bl[:, :, s - 1:s].to_broadcast([P, 2, s])
                    ins = nc.vector.tensor_tensor(dl, last, bl, ALU.subtract)
                else:
                    last = bl[:, :, s - 1:s].to_broadcast([P, 2 * T // (2 * s), s])
                    nc.vector.tensor_tensor(dr, br, last, ALU.subtract)
                    ins = nc.vector.tensor_tensor(dl, last, bl, ALU.subtract)
                ins.then_inc(diffs, 1)

            def level_scale(m, l):
                s = LEVELS[l]
                dl, dr = halves(dec[:, l % 2], s)
                xl, xr = halves(xqk[:, l % 2], s)
                dve.wait_ge(decays, m * (len(LEVELS) - 1) + l + 1)
                nc.vector.tensor_tensor(xl, halves(lk, s)[0], dl, ALU.mult)
                nc.vector.tensor_tensor(xr, halves(lq, s)[1], dr, ALU.mult).then_inc(xqk_ready, 1)

            def level_take(m, l):
                dve.wait_ge(level_ready, m * len(LEVELS) + l + 1)
                if l == 0:
                    ins = nc.vector.tensor_copy(cross[:], wide[:].rearrange("p (a b c) -> p a b c", b=2, c=P)[:, :, 0])
                else:
                    ins = nc.vector.copy_predicated(intra[:], level_mask[:, l - 1].unsqueeze(1).to_broadcast([P, 8, P]),
                                                    wide[:].rearrange("p (a c) -> p a c", c=P))
                ins.then_inc(level_taken, 1)

            def softmax(m, t):
                c = sum(ATT_HEADS[:m]) + t
                st = st_max[:, t % 2]
                dve.wait_ge(scores_ready, c + 1)
                nc.vector.reduce_max(st[:, 0:1], ps_score[:, 0:P], AX_X)
                link(nc.vector.reduce_max(st[:, 1:2], ps_score[:, P:3 * P], AX_X))
                nc.vector.tensor_scalar(st[:, 2:4], st[:, 0:2], -1.0, None, ALU.mult).then_inc(max_ready, 1)
                dve.wait_ge(exp_ready, 2 * c + 2)
                link(nc.vector.reciprocal(st[:, 6:8], st[:, 4:6]))
                nc.vector.tensor_scalar(prob[:, 0:P], prob[:, 0:P], st[:, 6:7], None, ALU.mult)
                nc.vector.tensor_scalar(prob[:, P:3 * P], prob[:, P:3 * P], st[:, 7:8], None, ALU.mult
                                        ).then_inc(prob_ready, 1)

            def prob_take(m, t):
                c = sum(ATT_HEADS[:m]) + t
                dve.wait_ge(prob_turned, c + 1)
                nc.vector.tensor_copy(prob_t[:], ps_turn[:, 0:3 * P]).then_inc(prob_t_ready, 1)

            def att_take(m, t):
                c = sum(ATT_HEADS[:m]) + t
                dve.wait_ge(att_ready, c + 1)
                if m == 0:
                    ins = nc.vector.tensor_copy(u[:, 4 + t], ps_stat[:, T:2 * T])
                else:
                    q = slice(64 * (t % 2), 64 * (t % 2) + 64)
                    ins = nc.vector.tensor_copy(u[q, 4 + t // 2], ps_stat[q, T:2 * T])
                ins.then_inc(att_taken, 1)

            def qk_square(m, tile):
                nc.vector.tensor_tensor(qk_sq[:, 0:2], tile[:, 0:2], tile[:, 0:2], ALU.mult).then_inc(qk_squared, 1)
                nc.vector.tensor_tensor(qk_sq[:, 2:4], tile[:, 2:4], tile[:, 2:4], ALU.mult).then_inc(qk_squared, 1)

            def qk_norm(m, j):
                dve.wait_ge(qk_root, 4 * (m - 1) + 2 * j + 2)
                link(nc.vector.reciprocal(qk_sq[:], qk_sq[:]))
                at = (A_FQ if j == 0 else A_FK) + m - 1
                if j:
                    link(nc.vector.scalar_tensor_tensor(out=ak[:], in0=ak[:], scalar=vec_a[:, at:at + 1],
                                                        in1=qk_sq[:], op0=ALU.mult, op1=ALU.mult))
                    return
                link(nc.vector.memset(qz, 0.0))
                by_head = qz.rearrange("p (a b) t -> p a b t", b=2)
                for b in range(2):
                    r = slice(64 * b, 64 * b + 64)
                    ins = nc.vector.scalar_tensor_tensor(out=by_head[r, :, b], in0=aq[r], scalar=vec_a[r, at:at + 1],
                                                         in1=qk_sq[r], op0=ALU.mult, op1=ALU.mult)
                    link(ins)

            def take(m, s):
                n0, e0 = seg(f"in{m}")
                name, _, kind = IN_CHUNKS[m][s]
                ps = acc[(e0 + s) % 2][:].rearrange("p (a t) -> p a t", a=2)
                dve.wait_ge(chunk_used, RING + n0 + s + 1)
                v = nc.vector
                if name == "lq":
                    ins = v.tensor_scalar(lq, ps, 0.125 if m == 0 else 1.0, None, ALU.mult)
                elif name == "lk":
                    ins = v.tensor_copy(lk, ps)
                elif name[:2] in ("lv", "av"):
                    dst = lv if name[0] == "l" else av
                    c = 256 * int(name[2])
                    ins = v.tensor_copy(dst[:, :, c:c + 256], ps)
                elif name[:2] in ("aq", "ak"):
                    c = 2 * int(name[2])
                    dst = (aq if name[1] == "q" else ak)[:, c:c + 2]
                    ins = v.tensor_scalar(dst, ps, ATT_DH[0] ** -0.5 if (m == 0 and name[1] == "q") else 1.0,
                                          None, ALU.mult)
                else:
                    c = int(name[1:])
                    ins = v.tensor_copy(gat[:, c:c + 2], ps)
                ins.then_inc(evacuated, 1)

            def conv(m):
                x_, c_, b_, y = gat[:, 4:6], gat[:, 6:8], gat[:, 12:14], u[:, 0:2]
                link(nc.vector.tensor_tensor(x_, x_, c_, ALU.mult))

                def tap(w, hp):
                    at = B_CONV + 6 * (m - 1) + 2 * w + hp
                    return vec_b[:, at:at + 1]

                for hp in range(2):
                    link(nc.vector.tensor_scalar(y[:, hp], x_[:, hp], tap(2, hp), None, ALU.mult))
                for w, back in ((1, 1), (0, 2)):
                    for hp in range(2):
                        link(nc.vector.scalar_tensor_tensor(out=y[:, hp, back:T], in0=x_[:, hp, 0:T - back],
                                                            scalar=tap(w, hp), in1=y[:, hp, back:T],
                                                            op0=ALU.mult, op1=ALU.add))
                link(nc.vector.tensor_tensor(y, y, b_, ALU.mult))

            def mixer(m):
                n0, e0 = seg(f"in{m}")
                steps = len(IN_CHUNKS[m])
                for s in range(mixer_steps(m)):
                    if m == 0 and ADA_FIRST + KF + 2 * KD + s < ADA:
                        ada_sum(ADA_FIRST + KF + 2 * KD + s)
                    if m == 0 and s == 0:
                        dve.wait_ge(pe_glr, 1)
                        nc.vector.tensor_copy(glr, ps_stat[0:GLR_N, T:2 * T]).then_inc(dve_glr, 1)
                    if m and s == 1:
                        dve.wait_ge(f_ready, m)
                        nc.vector.tensor_scalar(f8[:, 0], ps_stat[0:8, T:2 * T], fbias[:, m - 1:m], None, ALU.add
                                                ).then_inc(f_taken, 1)
                    if m == 0 and s == 1:
                        dve.wait_ge(pe_z, 1)
                        for hp in range(2):
                            ins = nc.vector.tensor_scalar(gat[:, 8 + hp], wide[:, hp * T:(hp + 1) * T],
                                                          vec_a[:, A_BGL + hp:A_BGL + hp + 1], None, ALU.add)
                        ins.then_inc(z_ready, 1)
                    if s == LIN_FIRST:
                        log_gates(m)
                    l = s - LIN_FIRST
                    if 2 <= l < len(LEVELS) + 2:
                        level_take(m, l - 2)
                    if 1 <= l < len(LEVELS):
                        level_scale(m, l - 1)
                    if 0 <= l < len(LEVELS) - 1:
                        level_diffs(m, l)
                    if m and s in (5, 7):
                        dve.wait_ge(evacuated, 2 + e0 + s)
                        qk_square(m, aq if s == 5 else ak)
                    if m and s in (6, 8):
                        qk_norm(m, s == 8)
                    t = s - ATT_FIRST[m] - 1
                    if 2 <= t < ATT_HEADS[m] + 2:
                        att_take(m, t - 2)
                    if 1 <= t < ATT_HEADS[m] + 1:
                        prob_take(m, t - 1)
                    t += 1
                    if 0 <= t < ATT_HEADS[m]:
                        softmax(m, t)
                    if s < steps:
                        split_ahead(n0 + s)
                        take(m, s)
                if m:
                    conv(m)
                w = LIN_DV[m] * 4 // P
                lin = u[:, LIN_AT[m]:LIN_AT[m] + w]
                xs = xqk[:].rearrange("p a b t -> p (a b) t")[:, 0:w]
                ds = dec.rearrange("p a b t -> p (a b) t")[:, 0:w]
                dve.wait_ge(lin_ready, m + 1)
                nc.vector.tensor_copy(lin, wide[:, 0:w * T].rearrange("p (k t) -> p k t", t=T)).then_inc(lin_taken, 1)
                at = A_GLAN if m == 0 else A_HG + m - 1
                dve.wait_ge(lin_rms, m + 1)
                link(nc.vector.reciprocal(xs, xs))
                link(nc.vector.scalar_tensor_tensor(out=lin, in0=lin, scalar=vec_a[:, at:at + 1], in1=xs,
                                                    op0=ALU.mult, op1=ALU.mult))
                dve.wait_ge(gate_sig, [1, 3, 4][m])
                link(nc.vector.tensor_tensor(ds, ds, gat[:, 0:w], ALU.mult))
                nc.vector.tensor_tensor(lin, lin, ds, ALU.mult).then_inc(mixed, 4)
                split_u("branch" if m == 0 else f"out{m}")
                if m == 0:
                    n0, e0 = seg("branch")
                    dve.wait_ge(gate_sig, 2)
                    for t in range(KD):
                        split_ahead(n0 + t)
                        ps = acc[(e0 + t) % 2]
                        dve.wait_ge(chunk_used, RING + n0 + t + 1)
                        nc.vector.tensor_tensor(u[:, t], ps[:, 0:T], gat[:, 4 + t], ALU.mult)
                        ins = nc.vector.tensor_tensor(silu[:, t % 2], ps[:, T:2 * T], gat[:, 12 + t], ALU.mult)
                        ins.then_inc(evacuated, 1)
                        dve.wait_ge(evacuated, 2 + e0 + t + 1)
                        ins = nc.vector.tensor_tensor(u[:, t], u[:, t], silu[:, t % 2], ALU.add)
                        if t % 2:
                            ins.then_inc(mixed, 1)
                    split_u("out0")
                n0, e0 = seg(f"out{m}")
                if m == 0:
                    mod_take(6 * KD, 9 * KD, ADA)
                    gain_make(2, A_FF2)
                    link(nc.vector.tensor_scalar(half[:, 8:16], mod[:, 8 * KD:9 * KD], 0.5, None, ALU.mult))
                for t in range(4):
                    split_ahead(n0 + t)
                    dve.wait_ge(chunk_used, RING + n0 + t + 1)
                    ps = acc[(e0 + t) % 2]
                    if m == 0:
                        for j in range(2):
                            g = mod[:, 5 * KD + 2 * t + j:5 * KD + 2 * t + j + 1]
                            ins = nc.vector.scalar_tensor_tensor(out=h[:, 2 * t + j], in0=ps[:, j * T:(j + 1) * T],
                                                                 scalar=g, in1=h[:, 2 * t + j],
                                                                 op0=ALU.mult, op1=ALU.add)
                    else:
                        ins = nc.vector.tensor_tensor(h[:, 2 * t:2 * t + 2], ps[:].rearrange("p (a t) -> p a t", a=2),
                                                      h[:, 2 * t:2 * t + 2], ALU.add)
                    ins.then_inc(evacuated, 1)

            dve.sem_inc(lo_ready, RING)
            dve.sem_inc(evacuated, 2)
            dve.sem_inc(ada_summed, 2)
            for tile, value in ((ones, 1.0), (eps, EPS), (zero8, 0.0), (half8, 0.5), (intra, 0.0), (negc, 0.0)):
                nc.vector.memset(tile[:], value).then_inc(set_up, 1)
            dve.wait_ge(consts, 32)
            nc.vector.tensor_copy(level_mask[:].rearrange("p n c -> p (n c)"), mask_in).then_inc(set_up, 1)
            dve.wait_ge(turned_a, 1)
            nc.vector.tensor_copy(vec_a[:, 0:A_ROWS], ps_score[:, 0:A_ROWS])
            ins = nc.vector.tensor_copy(vec_b[:, 0:B_ROWS], ps_score[:, P:P + B_ROWS])
            ins.then_inc(vec_ready, 1)
            dve.wait_ge(vec_ready, 1)
            link(nc.vector.tensor_scalar(vec_a[:, A_FQ:A_FQ + 2], vec_a[:, A_FQ:A_FQ + 2], ATT_DH[1] ** -0.5, None,
                                         ALU.mult))
            l0, l1 = vec_b[:, B_LB:B_LB + 2], vec_b[:, B_LB + 2:B_LB + 4]
            link(nc.vector.tensor_tensor(lbt[:, 8:10], l0, l1, ALU.max))
            link(nc.vector.tensor_tensor(lbt[:, 0:2], l0, lbt[:, 8:10], ALU.subtract))
            nc.vector.tensor_tensor(lbt[:, 2:4], l1, lbt[:, 8:10], ALU.subtract).then_inc(lb_in, 1)
            dve.wait_ge(lb_exp, 1)
            link(nc.vector.tensor_tensor(lbt[:, 8:10], lbt[:, 4:6], lbt[:, 6:8], ALU.add))
            link(nc.vector.reciprocal(lbt[:, 10:12], lbt[:, 8:10]))
            link(nc.vector.tensor_tensor(lbt[:, 0:2], lbt[:, 4:6], lbt[:, 10:12], ALU.mult))
            link(nc.vector.tensor_tensor(lbt[:, 2:4], lbt[:, 6:8], lbt[:, 10:12], ALU.mult))
            link(nc.vector.tensor_tensor(lb[:, 0:2], lbt[:, 0:2], lbt[:, 0:2], ALU.subtract))
            link(nc.vector.tensor_tensor(lb[:, 2:4], lbt[:, 0:2], lbt[:, 2:4], ALU.add))
            link(nc.vector.tensor_tensor(lb[:, 2:4], lb[:, 2:4], lbt[:, 0:2], ALU.subtract))
            link(nc.vector.tensor_scalar(lb[:, 0:4], lb[:, 0:4], 0.0, 1.0, ALU.max, ALU.min))
            link(nc.vector.tensor_scalar(lb[:, 4:8], lb[:, 0:4], -1.0, 1.0, ALU.mult, ALU.add))
            dve.wait_ge(toe_psum, 1)
            nc.vector.tensor_tensor(toe_row, ps_turn[0:4, 0:384], prob_t[0:4, :], ALU.add
                                    ).then_inc(toe_sb, 1)
            for k in range(KD):
                dve.wait_ge(x_turned, k + 1)
                nc.vector.tensor_copy(h[:, k], wide[:, k % 2 * 512:k % 2 * 512 + T]).then_inc(x_taken, 1)
            dve.wait_ge(c_ready, 1)
            for t in range(ADA_FIRST):
                ada_sum(t)
            for n in range(LEAD):
                split_lo(n)
            mod_take(0, 2 * KD, ADA_FIRST)
            gain_make(0, A_FF1)
            dve.wait_ge(mods, 1)
            norm("up0")
            ffn(0)
            mod_take(3 * KD, 6 * KD, ADA_FIRST + KF + 2 * KD)
            gain_make(1, A_MIX)
            dve.wait_ge(mods, 2)
            norm("in0")
            mixer(0)
            dve.wait_ge(mods, 3)
            norm("up1")
            ffn(1)
            norm("final")
            for layer in (1, 2):
                norm(f"up{2 * layer}")
                ffn(2 * layer)
                norm(f"in{layer}")
                mixer(layer)
                norm(f"up{2 * layer + 1}")
                ffn(2 * layer + 1)
            for c in range(TT * KD // 4):
                dve.wait_ge(out_turned, c + 1)
                nc.vector.tensor_copy(u[:].rearrange("p k t -> p (k t)")[:, c * 512:(c + 1) * 512],
                                      wide[:, c % 2 * 512:(c % 2 + 1) * 512]).then_inc(out_taken, 1)

        @block.tensor
        def _(pe):
            mm = nc.tensor.matmul

            def three(dst, wh, wl, xh, xl, first, last):
                mm(dst, wh, xh, start=first, stop=False)
                mm(dst, wh, xl, start=False, stop=False)
                return mm(dst, wl, xh, start=False, stop=last)

            def chunk_in(n, it=0):
                pe.wait_ge(lo_ready, it * RING + RING + n + 1)

            def bank_free(e, it=0, per=1):
                pe.wait_ge(evacuated, it * per + e + 1)

            def feature_tiles(n, dst, tiles, width, kt, waits=None):
                vh, vl = kview(whi, n % RING, KD, width), kview(wlo, n % RING, KD, width)
                for j in range(tiles):
                    c = slice(j * P, (j + 1) * P)
                    for k in range(kt):
                        if waits is not None and j == 0 and k % 2 == 0:
                            pe.wait_ge(ulo_ready, waits + k // 2 + 1)
                        ins = three(dst[:, j * T:(j + 1) * T], vh[:, k, c], vl[:, k, c], uhi[:, k], ulo[:, k],
                                    k == 0, k == kt - 1)
                return ins

            def token_tiles(n, dst):
                vh, vl = kview(whi, n % RING, KD, 256), kview(wlo, n % RING, KD, 256)
                for tt in range(TT):
                    c = slice(tt * P, (tt + 1) * P)
                    for k in range(KD):
                        d = dst[:, tt * 256:(tt + 1) * 256]
                        mm(d, uhi[:, k, c], vh[:, k], start=k == 0, stop=False)
                        mm(d, uhi[:, k, c], vl[:, k], start=False, stop=False)
                        ins = mm(d, ulo[:, k, c], vh[:, k], start=False, stop=k == KD - 1)
                return ins

            def mod_column(t, it=0):
                pe.wait_ge(ada_summed, it * RING + 2 + t + 1)
                dst = ps_mod[:, t:t + 1] if isinstance(it, int) else ps_mod[:, bass.ds(it * RING + t, 1)]
                mm(dst, ada_acc[:, t % 2], ones[:, 0:1], start=True, stop=True).then_inc(mod_ready, 1)

            def norm(name):
                i = NORMS.index(name)
                pe.wait_ge(summed, i + 1)
                mm(ps_stat[:, 0:T], ones[:], sumsq[:], start=True, stop=True).then_inc(stat, 1)

            def ffn(i):
                n0, e0 = seg(f"up{i}")
                waits = 4 * SPLITS.index(f"up{i}")

                def step(t, it=0):
                    chunk_in(n0 + t, it)
                    bank_free(e0 + t, it, RING)
                    feature_tiles(n0 + t, acc[(e0 + t) % 2], 2, 2 * P, KD, waits if t == 0 else None
                                  ).then_inc(chunk_used, 1)
                    if i == 0:
                        mod_column(ADA_FIRST + t, it)

                with pe.Fori(0, KF // RING) as it:
                    for t in range(RING):
                        step(t, it)
                for t in range(KF // RING * RING, KF):
                    step(t)
                n0, e0 = seg(f"down{i}")
                with pe.Fori(0, 2 * KD // RING) as it:
                    for t in range(RING):
                        m, side = t // 2, t % 2
                        chunk_in(n0 + t, it)
                        if side == 0:
                            bank_free(e0 + m, it, 2)
                        if t < 2:
                            pe.wait_ge(hlo_ready, KF * i + KF // 2 * (side + 1))
                        vh = kview(whi, (n0 + t) % RING, KF // 2, P)
                        vl = kview(wlo, (n0 + t) % RING, KF // 2, P)
                        for k in range(KF // 2):
                            kk = side * (KF // 2) + k
                            ins = three(acc[(e0 + m) % 2][:, 0:T], vh[:, k], vl[:, k], hhi[:, kk], hlo[:, kk],
                                        kk == 0, kk == KF - 1)
                        ins.then_inc(chunk_used, 1)
                        if i == 0:
                            mod_column(ADA_FIRST + KF + t, it)

            def level_column(hd, tt):
                return (4 * (hd % 2) + 2 * (hd // 2) + tt) * P

            def level_scores(m, l):
                s = LEVELS[l]
                c = m * len(LEVELS) + l
                if c:
                    pe.wait_ge(level_taken, c)
                if s:
                    pe.wait_ge(xqk_ready, m * (len(LEVELS) - 1) + l + 1)
                for hd in range(4):
                    r, hp = slice(64 * (hd % 2), 64 * (hd % 2) + 64), hd // 2
                    key = xqk[:, l % 2] if s else lk
                    query = xqk[:, l % 2] if s else lq
                    if l == 0:
                        j = level_column(hd, 0)
                        ins = mm(wide[:, j:j + P], key[r, hp, 0:P], query[r, hp, P:T], start=True, stop=True)
                    else:
                        for tt in range(TT):
                            c = slice(tt * P, (tt + 1) * P)
                            j = level_column(hd, tt)
                            ins = mm(wide[:, j:j + P], key[r, hp, c], query[r, hp, c], start=True, stop=True)
                ins.then_inc(level_ready, 1)

            def lin_out(m):
                dv = LIN_DV[m]
                pe.wait_ge(level_taken, (m + 1) * len(LEVELS))
                for hd in range(4):
                    vals = [lv[:, tt, hd * dv:(hd + 1) * dv] for tt in range(TT)]
                    if m == 0:
                        dst = wide[:, hd * T:(hd + 1) * T]
                    else:
                        dst = wide[64 * (hd % 2):64 * (hd % 2) + 64, hd // 2 * T:(hd // 2 + 1) * T]
                    j = level_column(hd, 0) // P
                    mm(dst[:, 0:P], vals[0], intra[:, j], start=True, stop=True)
                    mm(dst[:, P:T], vals[0], cross[:, j // 2], start=True, stop=False)
                    ins = mm(dst[:, P:T], vals[1], intra[:, j + 1], start=False, stop=True)
                ins.then_inc(lin_ready, 1)

            def lin_norm(m):
                pe.wait_ge(lin_sq, m + 1)
                w = LIN_DV[m] * 4 // P
                xs = xqk[:].rearrange("p a b t -> p (a b t)")
                for j in range(w // 2):
                    ins = mm(wide[:, j * 512:(j + 1) * 512], ones[:] if m == 0 else same_head,
                             xs[:, j * 512:(j + 1) * 512], start=True, stop=True)
                ins.then_inc(lin_stat, 1)

            def att_scores(m, t):
                c = sum(ATT_HEADS[:m]) + t
                if c:
                    pe.wait_ge(exp_ready, 2 * c)
                if m == 0:
                    q, k = aq[:, t], ak[:, t]
                else:
                    q, k = qz[:, t], ak[:, t // 2]
                for dst, qs, n in ((ps_score[:, 0:P], slice(0, P), P), (ps_score[:, P:3 * P], slice(P, T), T)):
                    mm(dst, q[:, qs], k[:, 0:n], start=True, stop=False)
                    if m == 0:
                        ins = mm(dst, anti, toe[:, t, T - n:T], start=False, stop=True)
                    else:
                        if t == 0:
                            pe.wait_ge(negc_ready, m)
                        mm(dst, pick(t), negc[:, 0:n], start=False, stop=False)
                        ins = mm(dst[:, n - P:n], ident, causal, start=False, stop=True)
                ins.then_inc(scores_ready, 1)

            def att_turn(m, t):
                c = sum(ATT_HEADS[:m]) + t
                pe.wait_ge(prob_ready, c + 1)
                for j in range(3):
                    ins = nc.tensor.transpose(ps_turn[:, j * P:(j + 1) * P], prob[:, j * P:(j + 1) * P], ident)
                ins.then_inc(prob_turned, 1)

            def att_out(m, t):
                c = sum(ATT_HEADS[:m]) + t
                dh = ATT_DH[m]
                pe.wait_ge(prob_t_ready, c + 1)
                if c:
                    pe.wait_ge(att_taken, c)
                vals = [av[:, tt, t * dh:(t + 1) * dh] for tt in range(TT)]
                r = slice(0, P) if m == 0 else slice(64 * (t % 2), 64 * (t % 2) + 64)
                dst = ps_stat[r, T:2 * T]
                mm(dst[:, 0:P], vals[0], prob_t[:, 0:P], start=True, stop=True)
                mm(dst[:, P:T], vals[0], prob_t[:, P:2 * P], start=True, stop=False)
                mm(dst[:, P:T], vals[1], prob_t[:, 2 * P:3 * P], start=False, stop=True).then_inc(att_ready, 1)

            def qk_stat(m, j):
                c = 2 * (m - 1) + j
                for half_, ps in enumerate((ps_turn, ps_score)):
                    pe.wait_ge(qk_squared, 2 * c + half_ + 1)
                    mm(ps[:], same_head, qk_sq[:].rearrange("p k t -> p (k t)")[:, 512 * half_:512 * half_ + 512],
                       start=True, stop=True).then_inc(qk_summed, 1)

            def mixer(m):
                n0, e0 = seg(f"in{m}")
                steps = len(IN_CHUNKS[m])
                waits = 4 * SPLITS.index(f"in{m}")
                pe.wait_ge(ulo_ready, waits + 4)
                wn, nn = (wlr, GLR_N) if m == 0 else (wff[:, m - 1], FF_N)
                for k in range(KD):
                    ins = mm(ps_stat[0:nn, T:2 * T], wn[:, k], u[:, k], start=k == 0, stop=k == KD - 1)
                ins.then_inc(pe_glr if m == 0 else f_ready, 1)
                for s in range(mixer_steps(m)):
                    if s < steps:
                        n = n0 + s
                        chunk_in(n)
                        bank_free(e0 + s)
                        dst = acc[(e0 + s) % 2]
                        if IN_CHUNKS[m][s][2] == "t":
                            ins = token_tiles(n, dst)
                        else:
                            ins = feature_tiles(n, dst, 2, 256, KD)
                        ins.then_inc(chunk_used, 1)
                        if m == 0 and ADA_FIRST + KF + 2 * KD + s < ADA:
                            mod_column(ADA_FIRST + KF + 2 * KD + s)
                    if m == 0 and s == 0:
                        pe.wait_ge(dve_glr, 1)
                        for hp in range(2):
                            ins = mm(wide[:, hp * T:(hp + 1) * T], wgl[:, hp * P:(hp + 1) * P], glr,
                                     start=True, stop=True)
                        ins.then_inc(pe_z, 1)
                    l = s - LIN_FIRST - 1
                    if 0 <= l < len(LEVELS):
                        level_scores(m, l)
                    if m and s in (5, 7):
                        qk_stat(m, s == 7)
                    t = s - ATT_FIRST[m]
                    if 2 <= t < ATT_HEADS[m] + 2:
                        att_out(m, t - 2)
                    if 1 <= t < ATT_HEADS[m] + 1:
                        att_turn(m, t - 1)
                    if 0 <= t < ATT_HEADS[m]:
                        att_scores(m, t)
                lin_out(m)
                lin_norm(m)
                if m == 0:
                    n0, e0 = seg("branch")
                    pe.wait_ge(ulo_ready, 4 * SPLITS.index("branch") + 4)
                    for t in range(KD):
                        chunk_in(n0 + t)
                        bank_free(e0 + t)
                        vh, vl = kview(whi, (n0 + t) % RING, KD, P), kview(wlo, (n0 + t) % RING, KD, P)
                        for j in range(2):
                            for k in range(4 * j, 4 * j + 4):
                                ins = three(acc[(e0 + t) % 2][:, j * T:(j + 1) * T], vh[:, k], vl[:, k], uhi[:, k],
                                            ulo[:, k], k % 4 == 0, k % 4 == 3)
                        ins.then_inc(chunk_used, 1)
                n0, e0 = seg(f"out{m}")
                waits = 4 * SPLITS.index(f"out{m}")
                for t in range(4):
                    chunk_in(n0 + t)
                    bank_free(e0 + t)
                    feature_tiles(n0 + t, acc[(e0 + t) % 2], 2, 256, KD, waits if t == 0 else None
                                  ).then_inc(chunk_used, 1)

            pe.sem_inc(chunk_used, RING)
            pe.sem_inc(mod_ready, 2)
            pe.wait_ge(consts, 32)
            pe.wait_ge(small, 16 * len(small_loads))
            nc.tensor.transpose(ps_score[:, 0:A_ROWS], stage[0:A_ROWS, 0], const[0:A_ROWS, C_IDENT:C_IDENT + A_ROWS])
            nc.tensor.transpose(ps_score[:, P:P + B_ROWS], stage[0:B_ROWS, 1],
                                const[0:B_ROWS, C_IDENT:C_IDENT + B_ROWS]).then_inc(turned_a, 1)
            mm(ps_turn[0:4, 0:384], rel[:], prob[0:NUM_BUCKETS, :], start=True, stop=True
               ).then_inc(toe_psum, 1)
            pe.wait_ge(x_in, 16)
            xt = u[:].rearrange("p k t -> p (k t)")
            for k in range(KD):
                if k >= 2:
                    pe.wait_ge(x_taken, k - 1)
                for tt in range(TT):
                    at = k % 2 * 512 + tt * P
                    ins = nc.tensor.transpose(wide[:, at:at + P],
                                              xt[:, tt * D + k * P:tt * D + (k + 1) * P], ident)
                ins.then_inc(x_turned, 1)
            pe.wait_ge(set_up, 7)
            for t in range(ADA_FIRST):
                mod_column(t)
            pe.wait_ge(toe_in, 16)
            norm("up0")
            ffn(0)
            norm("in0")
            mixer(0)
            norm("up1")
            ffn(1)
            norm("final")
            for layer in (1, 2):
                norm(f"up{2 * layer}")
                ffn(2 * layer)
                norm(f"in{layer}")
                mixer(layer)
                norm(f"up{2 * layer + 1}")
                ffn(2 * layer + 1)
            pe.wait_ge(evacuated, 2 + UNIT["down5"] + KD)
            for c in range(TT * KD // 4):
                tt, k0 = c // 2, 4 * (c % 2)
                if c >= 2:
                    pe.wait_ge(out_taken, c - 1)
                for k in range(4):
                    at = c % 2 * 512 + k * P
                    ins = nc.tensor.transpose(wide[:, at:at + P], h[:, k0 + k, tt * P:(tt + 1) * P], ident)
                ins.then_inc(out_turned, 1)


_INS = ["x", "c", "w_ada", "b_ada", "norm_ff1", "w_ff1_gate", "w_ff1_up", "w_ff1_down", "norm_mix", "w_in", "w_gla_lr",
        "b_gla_lr", "gla_norm", "rel_bias", "w_br_gla", "w_br_moba", "w_out", "norm_ff2", "w_ff2_gate", "w_ff2_up",
        "w_ff2_down", "norm_final", "ffn1_norm_2", "ffn1_w_in_2", "ffn1_w_out_2", "mix_norm_2", "w_mix_in_2",
        "conv_w_2", "hgrn_lb_logits_2", "hgrn_out_gain_2", "fox_q_gain_2", "fox_k_gain_2", "fox_f_bias_2",
        "w_mix_out_2", "ffn2_norm_2", "ffn2_w_in_2", "ffn2_w_out_2"]


def kernel(**inputs):
    import concourse.bacc as bacc
    from concourse.bass_utils import run_bass_kernel_spmd

    nc = bacc.Bacc("TRN2", target_bir_lowering=False, num_devices=1)
    arrays, aps = {}, {}
    constants, masks, by_distance = shape_constants()
    given = {name: np.ascontiguousarray(inputs[name]) for name in _INS}
    for name, value in {**given, "shape_constants": constants, "level_masks": masks,
                        "by_distance": by_distance}.items():
        arrays[f"in_{name}"] = value
        aps[name] = nc.dram_tensor(f"in_{name}", value.shape, mybir.dt.from_np(value.dtype), kind="ExternalInput").ap()
    out = nc.dram_tensor("out", (1, T, D), F32, kind="ExternalOutput").ap()
    build(nc, aps, out)
    result = run_bass_kernel_spmd(nc, [arrays], core_ids=[0])
    return result.results[0]["out"]
```

```python
from contextlib import ExitStack

import concourse.bass as bass
from concourse import mybir
import numpy as np

F32 = mybir.dt.float32
F32R = mybir.dt.float32r
U8 = mybir.dt.uint8
ALU = mybir.AluOpType
ACT = mybir.ActivationFunctionType
AX_X = mybir.AxisListType.X

P = 128
T = 256
TT = T // P
D = 1024
KD = D // P
F = 2816
KF = F // P
RING = 4
SLOT = 2048
LEAD = 2
NMOD = 9
ADA = NMOD * KD
ADA_FIRST = 2 * KD
EPS = 1e-6
NEG = -1e30
LEVELS = [128, 64, 32, 16, 8, 4, 2, 1, 0]
MAX_EXACT, NUM_BUCKETS, MAX_DISTANCE = 16, 32, 128
LIN_FIRST = 3
TAU = 16.0

GLA_CHUNKS = [("lq", 0, "f"), ("lk", 256, "f"), ("lv0", 512, "t"), ("lv1", 768, "t"),
              ("aq0", 1552, "f"), ("aq1", 1808, "f"), ("ak0", 2064, "f"), ("ak1", 2320, "f"),
              ("av0", 2576, "t"), ("av1", 2832, "t"), ("g0", 1040, "f"), ("g2", 1296, "f")] + \
             [(f"g{4 + 2 * i}", 3088 + 256 * i, "f") for i in range(8)]
MIX_CHUNKS = [("g8", 1024, "f"), ("lq", 768, "f"), ("aq0", 1792, "f"), ("aq1", 2048, "f"),
              ("ak0", 2304, "f"), ("ak1", 2560, "f"), ("lv0", 1280, "t"), ("av0", 2816, "t"), ("av1", 3072, "t"),
              ("g4", 0, "f"), ("g6", 512, "f"), ("g12", 256, "f"), ("g0", 1536, "f")]
GLR_AT, GLR_N = 1024, 16
FF_AT, FF_N = 3328, 8
IN_CHUNKS = [GLA_CHUNKS, MIX_CHUNKS, MIX_CHUNKS]
ATT_HEADS = [4, 8, 8]
ATT_DH = [128, 64, 64]
ATT_FIRST = [10, 7, 7]
LIN_DV = [128, 64, 64]
Q_AT, K_AT = 4, 6
LIN_AT = [0, 2, 2]


def chunk_columns():
    cols, first = [], {}

    def add(name, counts):
        first[name] = len(cols)
        cols.extend(counts)

    def ffn(i):
        add(f"up{i}", [SLOT] * KF)
        add(f"down{i}", [KF // 2 * P] * (2 * KD))

    ffn(0)
    add("in0", [SLOT] * len(GLA_CHUNKS))
    add("branch", [KD * P] * KD)
    add("out0", [SLOT] * 4)
    ffn(1)
    for layer in (1, 2):
        ffn(2 * layer)
        add(f"in{layer}", [SLOT] * len(MIX_CHUNKS))
        add(f"out{layer}", [SLOT] * 4)
        ffn(2 * layer + 1)
    return cols, first


def mixer_steps(m):
    return max(len(IN_CHUNKS[m]), LIN_FIRST + len(LEVELS) + 2, ATT_FIRST[m] + ATT_HEADS[m] + 3)


COLS, FIRST = chunk_columns()
UNIT = {}


def count_units():
    n = 0
    names = sorted(FIRST, key=FIRST.get)
    for name in names:
        UNIT[name] = n
        n += {"up": KF, "do": KD, "br": KD, "ou": 4}.get(name[:2], 0)
        if name[:2] == "in":
            n += len(IN_CHUNKS[int(name[2:])])


count_units()
STATS = ["up0", "in0", "up1", "in1", "up3", "up4", "in2", "up5"]
FOLLOWS = {"down1": "up2", "down2": "in1", "out1": "up3", "down3": "up4", "down4": "in2", "out2": "up5"}
SPLITS = ["up0", "in0", "branch", "out0", "up1", "up2", "in1", "out1", "up3", "up4", "in2", "out2", "up5"]

C_IDENT, C_ANTI, C_HEAD, C_CAUSAL = 0, 128, 256, 384
C_N = 512


def shape_constants():
    c = np.zeros((P, C_N), np.float32)
    i = np.arange(P)
    c[:, C_IDENT:C_IDENT + P] = np.eye(P)
    c[:, C_ANTI:C_ANTI + P] = np.eye(P)[::-1]
    c[:, C_HEAD:C_HEAD + P] = (i[:, None] // 64 == i[None, :] // 64)
    c[:, C_CAUSAL:C_CAUSAL + P] = np.where(i[:, None] >= i[None, :], 0.0, NEG)
    dist = (T - 1) - np.arange(384)
    n = np.maximum(dist, 0)
    nf = np.maximum(n, 1).astype(np.float32)
    large = MAX_EXACT + (np.log(nf / np.float32(MAX_EXACT)) / np.float32(np.log(MAX_DISTANCE / MAX_EXACT))
                         * np.float32(NUM_BUCKETS - MAX_EXACT)).astype(np.int32)
    bucket = np.where(n < MAX_EXACT, n, np.minimum(large, NUM_BUCKETS - 1))
    by_distance = np.zeros((NUM_BUCKETS + 4, 384), np.float32)
    by_distance[bucket, np.arange(384)] = 1.0
    by_distance[NUM_BUCKETS:] = np.where(dist >= 0, 0.0, NEG)
    m = np.zeros((P, len(LEVELS) - 1, P), np.float32)
    key, query = i[:, None], i[None, :]
    for n, s in enumerate(LEVELS[1:]):
        if s:
            m[:, n] = (key // (2 * s) == query // (2 * s)) & (key % (2 * s) < s) & (query % (2 * s) >= s)
        else:
            m[:, n] = key == query
    return c, m.reshape(P, -1), by_distance


def build(nc, a, out):
    with ExitStack() as ctx:
        ctx.enter_context(nc.allow_non_contiguous_dma(reason="two vectors of a few elements"))
        def sb(name, shape, dt=F32):
            return ctx.enter_context(nc.sbuf_tensor(name, shape, dt))

        def sem(name):
            return ctx.enter_context(nc.semaphore(name))

        raw = sb("raw", [P, RING, SLOT])
        early = ExitStack()
        ada_early = early.enter_context(nc.sbuf_tensor("ada_early", [P, ADA_FIRST // 2, KD, 2 * P], F32))
        early.close()
        whi = sb("whi", [P, RING, SLOT], F32R)
        wlo = sb("wlo", [P, RING, SLOT], F32R)
        h = sb("h", [P, KD, T])
        place_of_u = ExitStack()
        uhi_2 = place_of_u.enter_context(nc.sbuf_tensor("uhi_2", [P, KD, T], F32R))
        place_of_u.close()
        u = sb("u", [P, KD, T])
        uhi = sb("uhi", [P, KD, T], F32R)
        ulo = sb("ulo", [P, KD, T], F32R)
        work = sb("work", [P, 4, T])
        silu, hid = work[:, 0:2], work[:, 2:4]
        gate_up = work[:].rearrange("p (a b) t -> p a b t", a=2)
        dec = work[:].rearrange("p (a b) t -> p a b t", a=2)
        f8 = work[0:8]
        glr = work[0:GLR_N, 2]
        toe_row = work[0:4, 0:2].rearrange("p a t -> p (a t)")[:, 0:384]
        place_of_in_turn = ExitStack()
        ulo_2 = place_of_in_turn.enter_context(nc.sbuf_tensor("ulo_2", [P, KD, T], F32R))
        place_of_in_turn.close()
        in_turn = sb("in_turn", [P, 2 * KD * P])
        ada_raw = in_turn[:].rearrange("p (a k c) -> p a k c", a=2, k=KD)
        qz = in_turn[:].rearrange("p (a t) -> p a t", t=T)
        ada_acc = sb("ada_acc", [P, 2, 2, P])
        const = sb("const", [P, C_N])
        ones = sb("ones", [P, P])
        vec_a = sb("vec_a", [P, P])
        vec_b = sb("vec_b", [P, P])
        c_act = sb("c_act", [P, KD])
        mod = sb("mod", [P, ADA])
        gain = sb("gain", [P, 3, KD])
        half = sb("half", [P, 2 * KD])
        eps = sb("eps", [P, 1])
        zero8 = sb("zero8", [P, KD])
        half8 = sb("half8", [P, KD])
        sumsq = sb("sumsq", [P, T])
        sq = sb("sq", [P, T])
        stage = sq[:].rearrange("p (a c) -> p a c", a=2)
        rstd = sb("rstd", [P, T + TT])
        gain_f = sb("gain_f", [P, KD])
        wlr = sb("wlr", [P, KD, GLR_N])
        wff = sb("wff", [P, 2, KD, FF_N])
        wgl = sb("wgl", [GLR_N, 256])
        rel = sb("rel", [NUM_BUCKETS, 4])
        fbias = sb("fbias", [8, 2])
        negc = ada_acc[:, 0].rearrange("p a c -> p (a c)")
        lb = sb("lb", [P, 8])
        lbt = sb("lbt", [P, 12])
        st_max = sb("st_max", [P, 2, 8])
        scratch = nc.dram_tensor("bias_by_distance", [4, 384], F32)

        intra = sb("intra", [P, 8, P])
        level_mask = sb("level_mask", [P, len(LEVELS) - 1, P], U8)
        toe = sb("toe", [P, 4, T])
        rstd_f, sumsq_f = toe[:, 0], toe[:, 1]
        qk_sq = toe

        hidden = ExitStack()
        hhi = hidden.enter_context(nc.sbuf_tensor("hhi", [P, KF, T], F32R))
        hlo = hidden.enter_context(nc.sbuf_tensor("hlo", [P, KF, T], F32R))
        hidden.close()
        lv = sb("lv", [P, TT, 512])
        aq = sb("aq", [P, 4, T])
        ak = sb("ak", [P, 4, T])
        av = sb("av", [P, TT, 512])
        gat = sb("gat", [P, 20, T])
        lq, lk = gat[:, 16:18], gat[:, 18:20]
        mask_in = gat[:].rearrange("p a t -> p (a t)")[:, 0:(len(LEVELS) - 1) * P]
        bcum = sb("bcum", [P, 2, T])
        xqk = sb("xqk", [P, 2, 2, T])
        cross = sb("cross", [P, 4, P])
        prob = sb("prob", [P, 384])
        prob_t = sb("prob_t", [P, 384])

        psum = [ctx.enter_context(nc.psum_tensor(f"bank{i}", [P, 512], F32)) for i in range(4)]
        wide = ctx.enter_context(nc.psum_tensor("wide", [P, 1024], F32))
        ps_score = ctx.enter_context(nc.psum_tensor("ps_score", [P, 512], F32))
        ps_turn = ctx.enter_context(nc.psum_tensor("ps_turn", [P, 512], F32))
        acc = psum[0:2]
        ps_stat, ps_mod = psum[2], psum[3]

        ident = const[:, C_IDENT:C_IDENT + P]
        anti = const[:, C_ANTI:C_ANTI + P]
        same_head = const[:, C_HEAD:C_HEAD + P]
        causal = const[:, C_CAUSAL:C_CAUSAL + P]

        def pick(hd):
            return const[0:8, C_IDENT + hd:C_IDENT + hd + 1].to_broadcast([8, P])

        landed = [sem(f"landed{i}") for i in range(RING)]
        hi_ready = sem("hi_ready")
        lo_ready = sem("lo_ready")
        chunk_used = sem("chunk_used")
        evacuated = sem("evacuated")
        silu_ready = sem("silu_ready")
        hid_ready = sem("hid_ready")
        hhi_ready = sem("hhi_ready")
        hlo_ready = sem("hlo_ready")
        ada_landed = [sem(f"ada_landed{i}") for i in range(2)]
        early_landed = [sem(f"early_landed{i}") for i in range(ADA_FIRST // 2)]
        wff_ready = sem("wff_ready")
        ada_step = sem("ada_step")
        mod_ready = sem("mod_ready")
        small = sem("small")
        consts = sem("consts")
        x_in = sem("x_in")
        set_up = sem("set_up")
        turned_a = sem("turned_a")
        vec_ready = sem("vec_ready")
        c_ready = sem("c_ready")
        x_turned = sem("x_turned")
        x_taken = sem("x_taken")
        mods = sem("mods")
        summed = sem("summed")
        stat = sem("stat")
        rms = sem("rms")
        scaled = sem("scaled")
        u_ready = sem("u_ready")
        uhi_ready = sem("uhi_ready")
        ulo_ready = sem("ulo_ready")
        mixed = sem("mixed")
        pe_glr, dve_glr, pe_z = sem("pe_glr"), sem("dve_glr"), sem("pe_z")
        z_ready = sem("z_ready")
        bcum_ready = sem("bcum_ready")
        conv_ready, qz_clear = sem("conv_ready"), sem("qz_clear")
        stat_f, rms_f, mean_f = sem("stat_f"), sem("rms_f"), sem("mean_f")
        l_ready = sem("l_ready")
        kexp_in, kexp_out = sem("kexp_in"), sem("kexp_out")
        diffs, decays = sem("diffs"), sem("decays")
        xqk_ready, level_ready, level_taken = sem("xqk_ready"), sem("level_ready"), sem("level_taken")
        lin_ready, lin_taken = sem("lin_ready"), sem("lin_taken")
        lin_sq, lin_stat, lin_rms = sem("lin_sq"), sem("lin_stat"), sem("lin_rms")
        gate_sig = sem("gate_sig")
        f_ready, f_taken, f_log, negc_ready = sem("f_ready"), sem("f_taken"), sem("f_log"), sem("negc_ready")
        scores_ready, max_ready, exp_ready = sem("scores_ready"), sem("max_ready"), sem("exp_ready")
        prob_ready, prob_turned, prob_t_ready = sem("prob_ready"), sem("prob_turned"), sem("prob_t_ready")
        att_ready, att_taken = sem("att_ready"), sem("att_taken")
        toe_psum, toe_sb, toe_out, toe_in = sem("toe_psum"), sem("toe_sb"), sem("toe_out"), sem("toe_in")
        qk_squared, qk_summed, qk_root, qk_normed = sem("qk_squared"), sem("qk_summed"), sem("qk_root"), sem("qk_normed")
        lb_in, lb_exp = sem("lb_in"), sem("lb_exp")
        out_turned, out_taken, stored = sem("out_turned"), sem("out_taken"), sem("stored")
        dve_done, act_done, pool_done = sem("dve_done"), sem("act_done"), sem("pool_done")

        A_C, A_FF1, A_MIX, A_FF2, A_FIN, A_ADA = 0, 8, 16, 24, 32, 40
        A_GLAN, A_BGL, A_HG, A_FQ, A_FK = 112, 113, 115, 117, 119
        B_FF1, B_MIX, B_FF2, B_LB, B_CONV = 0, 16, 32, 48, 52
        A_ROWS, B_ROWS = 121, 64

        def rows(ap):
            return ap.rearrange("l (k c) -> (l k) c", c=P)

        small_loads = [
            (stage[A_C:A_C + 8, 0], rows(a["c"])), (stage[A_FF1:A_FF1 + 8, 0], rows(a["norm_ff1"])),
            (stage[A_MIX:A_MIX + 8, 0], rows(a["norm_mix"])), (stage[A_FF2:A_FF2 + 8, 0], rows(a["norm_ff2"])),
            (stage[A_FIN:A_FIN + 8, 0], a["norm_final"].rearrange("(k c) -> k c", c=P)),
            (stage[A_ADA:A_ADA + ADA, 0], rows(a["b_ada"])),
            (stage[A_GLAN:A_GLAN + 1, 0], a["gla_norm"]), (stage[A_BGL:A_BGL + 2, 0], rows(a["b_gla_lr"])),
        ]
        for at, name in ((A_HG, "hgrn_out_gain_2"), (A_FQ, "fox_q_gain_2"), (A_FK, "fox_k_gain_2")):
            small_loads += [(stage[at:at + 2, 0, 64 * i:64 * i + 64], a[name]) for i in range(2)]
        small_loads += [
            (stage[B_FF1:B_FF1 + 16, 1], rows(a["ffn1_norm_2"])), (stage[B_MIX:B_MIX + 16, 1], rows(a["mix_norm_2"])),
            (stage[B_FF2:B_FF2 + 16, 1], rows(a["ffn2_norm_2"])), (stage[B_LB:B_LB + 4, 1], rows(a["hgrn_lb_logits_2"])),
            (stage[B_CONV:B_CONV + 12, 1], a["conv_w_2"].rearrange("l w (k c) -> (l w k) c", c=P)),
            (wgl[:], a["w_gla_lr"][0]),
            (wlr[:], a["w_in"][0, :, GLR_AT:GLR_AT + GLR_N].rearrange("(k p) c -> p k c", p=P)),
            (wff[:, 0], a["w_mix_in_2"][0, :, FF_AT:FF_AT + FF_N].rearrange("(k p) c -> p k c", p=P)),
            (wff[:, 1], a["w_mix_in_2"][1, :, FF_AT:FF_AT + FF_N].rearrange("(k p) c -> p k c", p=P)),
            (rel[:], a["rel_bias"].rearrange("h b -> b h")),
            (fbias[:], a["fox_f_bias_2"].rearrange("l h -> h l")),
        ]

        small_loads += [(prob[0:NUM_BUCKETS, :], a["by_distance"][0:NUM_BUCKETS]),
                        (prob_t[0:4, :], a["by_distance"][NUM_BUCKETS:])]

        w2 = a["ffn1_w_in_2"], a["ffn2_w_in_2"]
        ffn_w = [(a["w_ff1_gate"][0], a["w_ff1_up"][0], a["w_ff1_down"][0]),
                 (a["w_ff2_gate"][0], a["w_ff2_up"][0], a["w_ff2_down"][0])]
        for layer in range(2):
            for n in range(2):
                w = w2[n][layer]
                ffn_w.append((w[:, 0:F], w[:, F:2 * F], a[f"ffn{n + 1}_w_out_2"][layer]))
        in_w = [a["w_in"][0], a["w_mix_in_2"][0], a["w_mix_in_2"][1]]
        out_w = [a["w_out"][0], a["w_mix_out_2"][0], a["w_mix_out_2"][1]]

        def norm_gain(name):
            if name in ("up0", "in0", "up1"):
                j = ("up0", "in0", "up1").index(name)
                return gain[:, j], mod[:, 3 * j * KD:(3 * j + 1) * KD]
            at = {"up2": B_FF1, "in1": B_MIX, "up3": B_FF2, "up4": B_FF1 + 8, "in2": B_MIX + 8, "up5": B_FF2 + 8}[name]
            return vec_b[:, at:at + 8], zero8

        def next_gain(name):
            if name == "down1":
                return gain_f[:]
            return norm_gain(FOLLOWS[name])[0] if name in FOLLOWS else None

        def tiles_of(tile, m, it=0, per=0):
            if isinstance(it, int):
                return tile[:, m]
            return tile[:, bass.ds(it * per + m, 1)].rearrange("p a t -> p (a t)")

        def column(tile, m, it=0, per=0):
            return tile[:, m:m + 1] if isinstance(it, int) else tile[:, bass.ds(it * per + m, 1)]

        def residual_gate(i):
            return [half[:, 0:8], half[:, 8:16]][i] if i < 2 else half8

        def seg(name):
            return FIRST[name], UNIT[name]

        def kview(tile, slot, k, width):
            return tile[:, slot, 0:k * width].rearrange("p (k c) -> p k c", k=k)

        def score_bank(m, t):
            return ps_mod if m and t % 2 else ps_score

        class Chain:

            def __init__(self, eng, done):
                self.eng, self.done, self.n, self.turn, self.per = eng, done, 0, None, 0

            def __call__(self, ins):
                self.n += 1
                ins.then_inc(self.done, 1)
                self.eng.wait_ge(self.done, self.n if self.turn is None else self.turn * self.per + self.n)

            def loop(self, turn, per):
                self.turn, self.per, self.n0 = turn, per, self.n

            def end(self, turns):
                assert self.n - self.n0 == self.per, (self.n - self.n0, self.per)
                self.n, self.turn = self.n0 + self.per * turns, None

        block = ctx.enter_context(nc.Block())

        @block.sync
        def _(sp):
            def load(n, parts, it=0):
                sp.wait_ge(lo_ready, it * RING + n + 1)
                for dst, src in parts:
                    sp.dma_start(dst, src).then_inc(landed[n % RING], 16)

            def up_parts(i, n, t, it=0):
                wg, wu, _ = ffn_w[i]
                v = kview(raw, n % RING, KD, 2 * P)
                return [(v[:, :, j * P:(j + 1) * P],
                         w[:, bass.ds(it * RING * P + t * P, P)].rearrange("(k p) c -> p k c", p=P))
                        for j, w in enumerate((wg, wu))]

            def down_parts(i, n, d, it=0):
                wd = ffn_w[i][2]
                v = kview(raw, n % RING, KF // 2, P)
                src = wd[(d % 2) * (F // 2):(d % 2 + 1) * (F // 2), bass.ds(it * 2 * P + d // 2 * P, P)]
                src = src.rearrange("(k p) c -> p k c", p=P)
                return [(v[:, 0:6], src[:, 0:6]), (v[:, 6:11], src[:, 6:11])]

            def ffn(i):
                n0 = FIRST[f"up{i}"]
                with sp.Fori(0, KF // RING) as it:
                    for t in range(RING):
                        load(n0 + t, up_parts(i, n0 + t, t, it), it)
                for t in range(KF // RING * RING, KF):
                    load(n0 + t, up_parts(i, n0 + t, t))
                n0 = FIRST[f"down{i}"]
                with sp.Fori(0, 2 * KD // RING) as it:
                    for t in range(RING):
                        load(n0 + t, down_parts(i, n0 + t, t, it), it)

            def plain(w, n, at):
                v = kview(raw, n % RING, KD, 256)
                src = w[:, at:at + 256].rearrange("(k p) c -> p k c", p=P)
                return [(v[:, 4 * j:4 * j + 4], src[:, 4 * j:4 * j + 4]) for j in range(2)]

            def mixer(m):
                n0 = FIRST[f"in{m}"]
                for s, (_, at, _) in enumerate(IN_CHUNKS[m]):
                    load(n0 + s, plain(in_w[m], n0 + s, at))
                if m == 0:
                    n0 = FIRST["branch"]
                    for t in range(KD):
                        v = kview(raw, (n0 + t) % RING, KD, P)
                        load(n0 + t, [(v[:, 4 * j:4 * j + 4],
                                       w[0, :, t * P:(t + 1) * P].rearrange("(k p) c -> p k c", p=P))
                                      for j, w in enumerate((a["w_br_gla"], a["w_br_moba"]))])
                n0 = FIRST[f"out{m}"]
                for t in range(4):
                    load(n0 + t, plain(out_w[m], n0 + t, 256 * t))

            for t in range(ADA_FIRST // 2):
                sp.dma_start(ada_early[:, t], a["w_ada"][0, :, 2 * P * t:2 * P * (t + 1)].rearrange("(k p) c -> p k c", p=P)
                             ).then_inc(early_landed[t], 16)
            ffn(0)
            mixer(0)
            ffn(1)
            for layer in (1, 2):
                ffn(2 * layer)
                mixer(layer)
                ffn(2 * layer + 1)
            for tt in range(TT):
                sp.wait_ge(out_taken, 2 * (tt + 1))
                sp.dma_start(out[0, tt * P:(tt + 1) * P], u[:].rearrange("p k t -> p (k t)")[:, tt * D:(tt + 1) * D]
                             ).then_inc(stored, 16)
            sp.wait_ge(stored, 16 * TT)

        @block.gpsimd
        def _(pool):
            link = Chain(pool, pool_done)
            norms = [0]

            def ada_load(t, it=0):
                if not isinstance(it, int) or t >= ADA_FIRST + 2:
                    pool.wait_ge(ada_step, it * RING * KD + (t - ADA_FIRST - 1) * KD)
                pool.dma_start(ada_raw[:, t % 2],
                               a["w_ada"][0, :, bass.ds(it * RING * P + t * P, P)].rearrange("(k p) c -> p k c", p=P)
                               ).then_inc(ada_landed[t % 2], 16)

            def square_tile(k, first, last):
                if first:
                    link(nc.gpsimd.tensor_tensor(sumsq[:], h[:, k], h[:, k], ALU.mult))
                    return
                link(nc.gpsimd.tensor_tensor(sq[:], h[:, k], h[:, k], ALU.mult))
                ins = nc.gpsimd.tensor_tensor(sumsq[:], sumsq[:], sq[:], ALU.add)
                if last:
                    ins.then_inc(summed, 1)
                    norms[0] += 1
                else:
                    link(ins)

            def sum_of_squares(ready, at, tiles, extra=None):
                if norms[0]:
                    pool.wait_ge(stat, norms[0])
                for k in range(KD):
                    if extra:
                        extra(k)
                    if k % tiles == 0:
                        pool.wait_ge(ready, at + k // tiles + 1)
                    square_tile(k, k == 0, k == KD - 1)

            def sums_over_units(name, tiles, extra=None):
                sum_of_squares(evacuated, 2 + UNIT[name], tiles, extra)

            def final_squares(k):
                pool.wait_ge(evacuated, 2 + UNIT["down1"] + k + 1)
                dst = sumsq_f if k == 0 else sq
                link(nc.gpsimd.tensor_scalar(sq[:], h[:, k], vec_a[:, A_FIN + k:A_FIN + k + 1], 1.0, ALU.mult, ALU.mult))
                link(nc.gpsimd.tensor_tensor(dst[:], sq[:], sq[:], ALU.mult))
                if k:
                    link(nc.gpsimd.tensor_tensor(sumsq_f, sumsq_f, sq[:], ALU.add))

            def halves(tile, s):
                v = tile.rearrange("p a (n b s) -> p (a n) b s", b=2, s=s)
                return v[:, :, 0], v[:, :, 1]

            def level_diffs(m, l):
                s = LEVELS[l]
                bl, br = halves(bcum[:], s)
                dl, dr = halves(dec[:, l % 2], s)
                if l == 0:
                    pool.wait_ge(bcum_ready, m + 1)
                elif l >= 2:
                    pool.wait_ge(xqk_ready, m * (len(LEVELS) - 1) + l - 1)
                if s == P:
                    nc.gpsimd.tensor_copy(dr, br)
                    last = bl[:, :, s - 1:s].to_broadcast([P, 2, s])
                    ins = nc.gpsimd.tensor_tensor(dl, last, bl, ALU.subtract)
                else:
                    last = bl[:, :, s - 1:s].to_broadcast([P, 2 * T // (2 * s), s])
                    nc.gpsimd.tensor_tensor(dr, br, last, ALU.subtract)
                    ins = nc.gpsimd.tensor_tensor(dl, last, bl, ALU.subtract)
                ins.then_inc(diffs, 1)

            def level_scale(m, l):
                s = LEVELS[l]
                dl, dr = halves(dec[:, l % 2], s)
                xl, xr = halves(xqk[:, l % 2], s)
                pool.wait_ge(decays, m * (len(LEVELS) - 1) + l + 1)
                if l >= 2:
                    pool.wait_ge(level_ready, m * len(LEVELS) + l - 1)
                nc.gpsimd.tensor_tensor(xl, halves(lk, s)[0], dl, ALU.mult)
                nc.gpsimd.tensor_tensor(xr, halves(lq, s)[1], dr, ALU.mult).then_inc(xqk_ready, 1)

            def conv(m):
                x_, c_, b_, y, tmp = gat[:, 4:6], gat[:, 6:8], gat[:, 12:14], u[:, 0:2], gat[:, 10:12]
                pool.wait_ge(evacuated, 2 + UNIT[f"in{m}"] + len(MIX_CHUNKS) - 1)
                link(nc.gpsimd.tensor_tensor(x_, x_, c_, ALU.mult))

                def tap(w, hp):
                    at = B_CONV + 6 * (m - 1) + 2 * w + hp
                    return vec_b[:, at:at + 1]

                for hp in range(2):
                    link(nc.gpsimd.tensor_scalar(y[:, hp], x_[:, hp], tap(2, hp), 1.0, ALU.mult, ALU.mult))
                for w, back in ((1, 1), (0, 2)):
                    for hp in range(2):
                        link(nc.gpsimd.tensor_scalar(tmp[:, hp], x_[:, hp], tap(w, hp), 1.0, ALU.mult, ALU.mult))
                    link(nc.gpsimd.tensor_tensor(y[:, :, back:T], y[:, :, back:T], tmp[:, :, 0:T - back], ALU.add))
                nc.gpsimd.tensor_tensor(y, y, b_, ALU.mult).then_inc(conv_ready, 1)

            def mixer(m):
                if m:
                    nc.gpsimd.memset(in_turn[:], 0.0).then_inc(qz_clear, 1)
                for s in range(mixer_steps(m)):
                    if m == 0 and ADA_FIRST + 2 + KF + 2 * KD + s < ADA:
                        ada_load(ADA_FIRST + 2 + KF + 2 * KD + s)
                    l = s - LIN_FIRST
                    if 1 <= l < len(LEVELS):
                        level_scale(m, l - 1)
                    if 0 <= l < len(LEVELS) - 1:
                        level_diffs(m, l)
                if m:
                    conv(m)

            def affine(name, dst):
                g, b = norm_gain(name)
                i = STATS.index(name)
                for kk in range(4):
                    pool.wait_ge(scaled, 4 * i + kk + 1)
                    for k in (2 * kk, 2 * kk + 1):
                        ins = nc.gpsimd.tensor_scalar(dst[:, k], dst[:, k], g[:, k:k + 1], b[:, k:k + 1],
                                                      ALU.mult, ALU.add)
                    ins.then_inc(u_ready, 1)

            pool.dma_start(const[:], a["shape_constants"]).then_inc(consts, 16)
            pool.dma_start(mask_in, a["level_masks"]).then_inc(consts, 16)
            for t in range(2):
                ada_load(ADA_FIRST + t)
            sum_of_squares(x_taken, 0, 1)
            affine("up0", u)
            with pool.Fori(0, KF // RING) as it:
                for t in range(RING):
                    ada_load(ADA_FIRST + 2 + t, it)
            for t in range(KF // RING * RING, KF):
                ada_load(ADA_FIRST + 2 + t)
            first_down = ADA_FIRST + 2 + KF
            sums_over_units("down0", 1, lambda k: [ada_load(first_down + 2 * k + j) for j in range(2)])
            affine("in0", u)
            mixer(0)
            sums_over_units("out0", 2)
            affine("up1", u)
            sums_over_units("down1", 1, final_squares)
            for layer in (1, 2):
                sums_over_units(f"down{2 * layer}", 1)
                mixer(layer)
                sums_over_units(f"out{layer}", 2)
                if layer == 1:
                    sums_over_units("down3", 1)

        @block.scalar
        def _(act):
            link = Chain(act, act_done)

            def split_hi(n, it=0):
                cols = COLS[n]
                act.wait_ge(landed[n % RING], it * 32 + 32 * (n // RING + 1))
                act.wait_ge(chunk_used, it * RING + n + 1)
                nc.scalar.copy(whi[:, n % RING, 0:cols], raw[:, n % RING, 0:cols]).then_inc(hi_ready, 1)

            def split_ahead(n, it=0):
                if n + LEAD < len(COLS):
                    split_hi(n + LEAD, it)

            def split_u(name, ready, at):
                for kk in range(4):
                    act.wait_ge(ready, at + kk + 1)
                    nc.scalar.copy(uhi[:, 2 * kk:2 * kk + 2], u[:, 2 * kk:2 * kk + 2]).then_inc(uhi_ready, 2)

            def root_of_mean(name):
                i = STATS.index(name)
                act.wait_ge(stat, i + 1 + (i > 2))
                w = T if i < 3 else T + TT
                nc.scalar.activation(rstd[:, 0:w], ps_stat[:, 0:w], ACT.Sqrt, bias=eps[:], scale=1.0 / D).then_inc(rms, 1)

            def norm(name):
                root_of_mean(name)
                split_u(name, u_ready, 4 * STATS.index(name))

            def gained_hi(g, e, k, it=0, per=0, per_e=0, dst=uhi):
                act.wait_ge(evacuated, it * per_e + 2 + e + 1)
                nc.scalar.activation(tiles_of(dst, k, it, per), tiles_of(h, k, it, per), ACT.Identity,
                                     scale=column(g, k, it, per)).then_inc(uhi_ready, 1)

            def final_norms():
                act.wait_ge(stat_f, 1)
                nc.scalar.activation(rstd_f, ps_stat[:, 0:T], ACT.Sqrt, bias=eps[:], scale=1.0 / D).then_inc(rms_f, 1)
                act.wait_ge(mean_f, 1)
                nc.scalar.activation(rstd[:, 0:T], sumsq_f, ACT.Sqrt, bias=eps[:], scale=1.0 / D).then_inc(rms_f, 1)

            def ffn(i):
                n0, e0 = seg(f"up{i}")

                def step(t, it=0):
                    split_ahead(n0 + t, it)
                    dst = tiles_of(hhi, t, it, RING)
                    if i < 2:
                        act.wait_ge(chunk_used, it * RING + RING + n0 + t + 1)
                        nc.scalar.activation(silu[:, t % 2], acc[(e0 + t) % 2][:, 0:T], ACT.Silu).then_inc(silu_ready, 1)
                        act.wait_ge(evacuated, it * RING + 2 + e0 + t + 1)
                        nc.scalar.copy(dst, hid[:, t % 2]).then_inc(hhi_ready, 1)
                    else:
                        pair = gate_up[:, t % 2]
                        act.wait_ge(evacuated, it * RING + 2 + e0 + t + 1)
                        nc.scalar.activation(pair[:, 0], pair[:, 0], ACT.Silu).then_inc(silu_ready, 1)
                        act.wait_ge(hid_ready, it * RING + KF * (i - 2) + t + 1)
                        nc.scalar.copy(dst, pair[:, 1]).then_inc(hhi_ready, 1)

                with act.Fori(0, KF // RING) as it:
                    for t in range(RING):
                        step(t, it)
                for t in range(KF // RING * RING, KF):
                    step(t)
                n0, e0 = seg(f"down{i}")
                g = next_gain(f"down{i}")

                def down(t, it=0):
                    split_ahead(n0 + t, it)
                    if t % 2 and g is not None:
                        gained_hi(g, e0 + t // 2, t // 2, it, 2, 2)

                with act.Fori(0, 2 * KD // RING - 1) as it:
                    for t in range(RING):
                        down(t, it)
                for t in range(2 * KD - RING, 2 * KD):
                    down(t)

            def mixer(m):
                n0, e0 = seg(f"in{m}")
                steps = len(IN_CHUNKS[m])
                last = mixer_steps(m)
                z, t_, l_ = gat[:, 8:10], gat[:, 4:6], gat[:, 6:8]
                for s in range(last):
                    if s == 2:
                        if m == 0:
                            act.wait_ge(z_ready, 1)
                        else:
                            act.wait_ge(evacuated, 2 + e0 + 1)
                        link(nc.scalar.activation(t_, z, ACT.Abs))
                        link(nc.scalar.activation(t_, t_, ACT.Exp, scale=-1.0))
                        if m:
                            link(nc.scalar.activation(gat[:, 12:14], z, ACT.Exp, scale=-1.0))
                        nc.scalar.activation(l_, t_, ACT.Ln, bias=1.0).then_inc(l_ready, 1)
                        if m:
                            for hp in range(2):
                                j = 2 * (m - 1) + hp
                                ins = nc.scalar.activation(gat[:, 14 + hp], gat[:, 12 + hp], ACT.Ln, bias=1.0,
                                                           scale=lb[:, j:j + 1])
                            ins.then_inc(l_ready, 1)
                            act.wait_ge(f_taken, m)
                            link(nc.scalar.activation(f8[:, 1], f8[:, 0], ACT.Abs))
                            link(nc.scalar.activation(f8[:, 1], f8[:, 1], ACT.Exp, scale=-1.0))
                            nc.scalar.activation(f8[:, 2], f8[:, 1], ACT.Ln, bias=1.0).then_inc(f_log, 1)
                    if m and s == LIN_FIRST:
                        act.wait_ge(kexp_in, m)
                        nc.scalar.activation(lk, t_, ACT.Exp, scale=-1.0).then_inc(kexp_out, 1)
                    if m and s in (Q_AT + 1, K_AT + 1):
                        c = 2 * (m - 1) + (s == K_AT + 1)
                        for half_, ps in enumerate((ps_turn, ps_score)):
                            act.wait_ge(qk_summed, 2 * c + half_ + 1)
                            link(nc.scalar.activation(qk_sq[:, 2 * half_:2 * half_ + 2],
                                                      ps[:].rearrange("p (a t) -> p a t", a=2), ACT.Ln, bias=eps[:],
                                                      scale=1.0 / ATT_DH[m]))
                        nc.scalar.activation(qk_sq[:], qk_sq[:], ACT.Exp, scale=-0.5).then_inc(qk_root, 1)
                    l = s - LIN_FIRST
                    if 0 <= l < len(LEVELS) - 1:
                        c = m * (len(LEVELS) - 1) + l + 1
                        act.wait_ge(diffs, c)
                        nc.scalar.activation(dec[:, l % 2], dec[:, l % 2], ACT.Exp,
                                             scale=1.0 / TAU if m == 0 else 1.0).then_inc(decays, 1)
                    t = s - ATT_FIRST[m]
                    if 0 <= t < ATT_HEADS[m]:
                        c = sum(ATT_HEADS[:m]) + t + 1
                        act.wait_ge(max_ready, c)
                        act.wait_ge(prob_turned, c - 1) if c > 1 else None
                        for j, (lo, hi) in enumerate(((0, P), (P, 3 * P))):
                            ins = nc.scalar.activation(prob[:, lo:hi], score_bank(m, t)[:, lo:hi], ACT.Exp,
                                                       bias=st_max[:, t % 2, 2 + j:3 + j],
                                                       accum_out=st_max[:, t % 2, 4 + j:5 + j])
                            ins.then_inc(exp_ready, 1)
                    if s < steps:
                        split_ahead(n0 + s)
                w = LIN_DV[m] * 4 // P
                lin = u[:, LIN_AT[m]:LIN_AT[m] + w]
                xs = xqk[:].rearrange("p a b t -> p (a b) t")[:, 0:w]
                ds = dec.rearrange("p a b t -> p (a b) t")[:, 0:w]
                act.wait_ge(lin_taken, m + 1)
                nc.scalar.activation(xs, lin, ACT.Square).then_inc(lin_sq, 1)
                act.wait_ge(lin_stat, m + 1)
                link(nc.scalar.activation(xs, wide[:, 0:w * T].rearrange("p (k t) -> p k t", t=T), ACT.Ln, bias=eps[:],
                                          scale=1.0 / LIN_DV[m]))
                nc.scalar.activation(xs, xs, ACT.Exp, scale=-0.5).then_inc(lin_rms, 1)
                nc.scalar.activation(ds, gat[:, 0:w], ACT.Sigmoid).then_inc(gate_sig, 1)
                if m == 0:
                    nc.scalar.activation(gat[:, 4:20], gat[:, 4:20], ACT.Sigmoid).then_inc(gate_sig, 1)
                if m:
                    act.wait_ge(conv_ready, m)
                split_u(f"y{m}", mixed, 4 * (m + (m > 0)))
                if m == 0:
                    n0 = FIRST["branch"]
                    for t in range(KD):
                        split_ahead(n0 + t)
                    act.wait_ge(chunk_used, RING + FIRST["out0"])
                    split_u("merged", mixed, 4)
                n0, e0 = seg(f"out{m}")
                g = next_gain(f"out{m}")
                for t in range(4):
                    split_ahead(n0 + t)
                    if g is not None:
                        for k in (2 * t, 2 * t + 1):
                            gained_hi(g, e0 + t, k, dst=uhi_2)

            act.dma_start(u[:].rearrange("p k t -> p (k t)").rearrange("p (a d) -> p a d", a=TT),
                          a["x"][0].rearrange("(a p) d -> p a d", p=P)).then_inc(x_in, 16)
            for dst, src in small_loads:
                act.dma_start(dst, src).then_inc(small, 16)
            act.wait_ge(vec_ready, 1)
            nc.scalar.activation(c_act[:], vec_a[:, A_C:A_C + 8], ACT.Silu).then_inc(c_ready, 1)
            act.wait_ge(lb_in, 1)
            nc.scalar.activation(lbt[:, 4:8], lbt[:, 0:4], ACT.Exp).then_inc(lb_exp, 1)
            act.wait_ge(toe_sb, 1)
            act.dma_start(scratch[:], toe_row).then_inc(toe_out, 16)
            act.wait_ge(toe_out, 16)
            act.dma_start(toe[:], bass.AP(scratch, 0, [[1, P], [384, 4], [1, T]])).then_inc(toe_in, 16)
            act.wait_ge(mod_ready, 2 + ADA_FIRST)
            for n in range(LEAD):
                split_hi(n)
            norm("up0")
            ffn(0)
            norm("in0")
            mixer(0)
            norm("up1")
            ffn(1)
            final_norms()
            for layer in (1, 2):
                if layer > 1:
                    root_of_mean(f"up{2 * layer}")
                ffn(2 * layer)
                root_of_mean(f"in{layer}")
                mixer(layer)
                root_of_mean(f"up{2 * layer + 1}")
                ffn(2 * layer + 1)

        @block.vector
        def _(dve):
            link = Chain(dve, dve_done)

            def split_lo(n, it=0):
                cols = COLS[n]
                dve.wait_ge(hi_ready, it * RING + n + 1)
                nc.vector.tensor_tensor(wlo[:, n % RING, 0:cols], raw[:, n % RING, 0:cols],
                                        whi[:, n % RING, 0:cols].bitcast(F32), ALU.subtract).then_inc(lo_ready, 1)

            def split_ahead(n, it=0):
                if n + LEAD < len(COLS):
                    split_lo(n + LEAD, it)

            def split_u(name):
                q = SPLITS.index(name)
                for kk in range(4):
                    s = slice(2 * kk, 2 * kk + 2)
                    dve.wait_ge(uhi_ready, KD * q + 2 * kk + 2)
                    nc.vector.tensor_tensor(ulo[:, s], u[:, s], uhi[:, s].bitcast(F32), ALU.subtract
                                            ).then_inc(ulo_ready, 2)

            def gained_lo(q, g, k, it=0, per=0, hi=uhi, dst=ulo):
                dve.wait_ge(uhi_ready, it * per + KD * q + k + 1)
                nc.vector.scalar_tensor_tensor(out=tiles_of(dst, k, it, per), in0=tiles_of(h, k, it, per),
                                               scalar=column(g, k, it, per),
                                               in1=tiles_of(hi, k, it, per).bitcast(F32),
                                               op0=ALU.mult, op1=ALU.subtract).then_inc(ulo_ready, 1)

            def norm(name):
                dve.wait_ge(rms, STATS.index(name) + 1)
                link(nc.vector.reciprocal(rstd[:, 0:T], rstd[:, 0:T]))
                for kk in range(4):
                    s = slice(2 * kk, 2 * kk + 2)
                    nc.vector.tensor_tensor(u[:, s], h[:, s], by_token(2), ALU.mult).then_inc(scaled, 1)
                split_u(name)

            def by_token(n):
                return rstd[:, 0:T].unsqueeze(1).to_broadcast([P, n, T])

            def scale_of(name):
                dve.wait_ge(rms, STATS.index(name) + 1)
                link(nc.vector.reciprocal(rstd[:], rstd[:]))

            def final_norms():
                dve.wait_ge(rms_f, 1)
                link(nc.vector.reciprocal(rstd_f, rstd_f))
                link(nc.vector.tensor_tensor(sumsq_f, ps_stat[:, T:2 * T], rstd_f, ALU.mult))
                nc.vector.tensor_tensor(sumsq_f, sumsq_f, rstd_f, ALU.mult).then_inc(mean_f, 1)
                dve.wait_ge(rms_f, 2)
                link(nc.vector.reciprocal(rstd[:, 0:T], rstd[:, 0:T]))
                link(nc.vector.tensor_tensor(rstd[:, 0:T], rstd[:, 0:T], rstd_f, ALU.mult))

            def final_residual():
                for k in range(KD):
                    ins = nc.vector.scalar_tensor_tensor(out=h[:, k], in0=h[:, k], scalar=vec_a[:, A_FIN + k:A_FIN + k + 1],
                                                         in1=rstd_f, op0=ALU.mult, op1=ALU.mult)
                link(ins)

            def ada_sum(t, it=0):
                dve.wait_ge(ada_landed[t % 2], it * 32 + 16 * ((t - ADA_FIRST) // 2 + 1))
                dve.wait_ge(mod_ready, it * RING + t + 1)
                for k in range(KD):
                    w, s = ada_raw[:, t % 2, k], ada_acc[:, t % 2, k % 2]
                    if k < 2:
                        ins = nc.vector.tensor_scalar(s, w, c_act[:, k:k + 1], None, ALU.mult)
                    else:
                        dve.wait_ge(ada_step, it * RING * KD + (t - ADA_FIRST) * KD + k - 1)
                        ins = nc.vector.scalar_tensor_tensor(out=s, in0=w, scalar=c_act[:, k:k + 1], in1=s,
                                                             op0=ALU.mult, op1=ALU.add)
                    ins.then_inc(ada_step, 1)

            def mod_take(lo, hi, made):
                dve.wait_ge(mod_ready, 2 + made)
                link(nc.vector.tensor_tensor(mod[:, lo:hi], ps_mod[:, lo:hi], vec_a[:, A_ADA + lo:A_ADA + hi], ALU.add))

            def gain_make(j, at):
                link(nc.vector.tensor_scalar(gain[:, j], mod[:, (3 * j + 1) * KD:(3 * j + 2) * KD], 1.0, None, ALU.add))
                nc.vector.tensor_tensor(gain[:, j], gain[:, j], vec_a[:, at:at + 8], ALU.mult).then_inc(mods, 1)

            def ffn(i):
                n0, e0 = seg(f"up{i}")

                def step(t, it=0):
                    if i == 0:
                        ada_sum(ADA_FIRST + t, it)
                    split_ahead(n0 + t, it)
                    g = it * RING + KF * i + t + 1
                    ps = acc[(e0 + t) % 2]
                    if i < 2:
                        dve.wait_ge(silu_ready, g)
                        nc.vector.tensor_tensor(hid[:, t % 2], silu[:, t % 2], ps[:, T:2 * T], ALU.mult
                                                ).then_inc(evacuated, 1)
                    else:
                        pair = gate_up[:, t % 2]
                        dve.wait_ge(chunk_used, it * RING + RING + n0 + t + 1)
                        nc.vector.tensor_tensor(pair, ps[:].rearrange("p (a t) -> p a t", a=2), by_token(2), ALU.mult
                                                ).then_inc(evacuated, 1)
                        dve.wait_ge(silu_ready, g)
                        nc.vector.tensor_tensor(pair[:, 1], pair[:, 0], pair[:, 1], ALU.mult).then_inc(hid_ready, 1)
                    dve.wait_ge(hhi_ready, g)
                    src = hid[:, t % 2] if i < 2 else gate_up[:, t % 2, 1]
                    nc.vector.tensor_tensor(tiles_of(hlo, t, it, RING), src, tiles_of(hhi, t, it, RING).bitcast(F32),
                                            ALU.subtract).then_inc(hlo_ready, 1)

                with dve.Fori(0, KF // RING) as it:
                    for t in range(RING):
                        step(t, it)
                for t in range(KF // RING * RING, KF):
                    step(t)
                if i == 0:
                    mod_take(2 * KD, 3 * KD, ADA_FIRST + KF)
                    link(nc.vector.tensor_scalar(half[:, 0:8], mod[:, 2 * KD:3 * KD], 0.5, None, ALU.mult))
                n0, e0 = seg(f"down{i}")
                g = residual_gate(i)
                after = next_gain(f"down{i}")
                if i == 2:
                    final_residual()

                def down(t, it=0):
                    if i == 0:
                        ada_sum(ADA_FIRST + KF + t, it)
                    split_ahead(n0 + t, it)
                    if t % 2:
                        m = t // 2
                        dve.wait_ge(chunk_used, it * RING + RING + n0 + t + 1)
                        gm, hm = column(g, m, it, 2), tiles_of(h, m, it, 2)
                        nc.vector.scalar_tensor_tensor(out=hm, in0=acc[(e0 + m) % 2][:, 0:T], scalar=gm, in1=hm,
                                                       op0=ALU.mult, op1=ALU.add).then_inc(evacuated, 1)
                        if after is not None:
                            gained_lo(SPLITS.index(FOLLOWS[f"down{i}"]), after, m, it, 2)

                turns = 2 * KD // RING - 1
                with dve.Fori(0, turns) as it:
                    for t in range(RING):
                        down(t, it)
                for t in range(2 * KD - RING, 2 * KD):
                    down(t)

            def log_gates(m):
                z, l_, la, t_ = gat[:, 8:10], gat[:, 6:8], gat[:, 10:12], gat[:, 4:6]
                dve.wait_ge(l_ready, [1, 3, 5][m])
                link(nc.vector.tensor_scalar(la, z, 0.0, None, ALU.min))
                link(nc.vector.tensor_tensor(la, la, l_, ALU.subtract))
                if m:
                    link(nc.vector.tensor_tensor(la, la, gat[:, 14:16], ALU.add))
                    link(nc.vector.tensor_scalar(t_, z, 0.0, None, ALU.max))
                    nc.vector.tensor_tensor(t_, t_, l_, ALU.add).then_inc(kexp_in, 1)
                for hp in range(2):
                    for tt in range(TT):
                        v = la[:, hp, tt * P:(tt + 1) * P]
                        link(nc.vector.tensor_tensor_scan(bcum[:, hp, tt * P:(tt + 1) * P], v, v, 0.0,
                                                          ALU.add, ALU.bypass))
                if m:
                    dve.wait_ge(kexp_out, m)
                    for hp in range(2):
                        j = 2 * (m - 1) + hp
                        link(nc.vector.tensor_scalar(lk[:, hp], lk[:, hp], lb[:, 4 + j:5 + j], None, ALU.mult))
                    dve.wait_ge(f_log, m)
                    link(nc.vector.tensor_scalar(f8[:, 0], f8[:, 0], 0.0, None, ALU.min))
                    link(nc.vector.tensor_tensor(f8[:, 0], f8[:, 2], f8[:, 0], ALU.subtract))
                    nc.vector.tensor_tensor_scan(negc[0:8], f8[:, 0], f8[:, 0], 0.0, ALU.add, ALU.bypass
                                                 ).then_inc(negc_ready, 1)
                    dve.wait_ge(negc_ready, m)
                nc.vector.tensor_copy(st_max[:, 0, 0:1], bcum[:, 0, 0:1]).then_inc(bcum_ready, 1)

            def level_take(m, l):
                dve.wait_ge(level_ready, m * len(LEVELS) + l + 1)
                if l == 0:
                    ins = nc.vector.tensor_copy(cross[:], wide[:].rearrange("p (a b c) -> p a b c", b=2, c=P)[:, :, 0])
                else:
                    ins = nc.vector.copy_predicated(intra[:], level_mask[:, l - 1].unsqueeze(1).to_broadcast([P, 8, P]),
                                                    wide[:].rearrange("p (a c) -> p a c", c=P))
                ins.then_inc(level_taken, 1)

            def softmax(m, t):
                c = sum(ATT_HEADS[:m]) + t
                st = st_max[:, t % 2]
                ps = score_bank(m, t)
                dve.wait_ge(scores_ready, c + 1)
                nc.vector.reduce_max(st[:, 0:1], ps[:, 0:P], AX_X)
                link(nc.vector.reduce_max(st[:, 1:2], ps[:, P:3 * P], AX_X))
                nc.vector.tensor_scalar(st[:, 2:4], st[:, 0:2], -1.0, None, ALU.mult).then_inc(max_ready, 1)
                dve.wait_ge(exp_ready, 2 * c + 2)
                link(nc.vector.reciprocal(st[:, 6:8], st[:, 4:6]))
                nc.vector.tensor_scalar(prob[:, 0:P], prob[:, 0:P], st[:, 6:7], None, ALU.mult)
                nc.vector.tensor_scalar(prob[:, P:3 * P], prob[:, P:3 * P], st[:, 7:8], None, ALU.mult
                                        ).then_inc(prob_ready, 1)

            def prob_take(m, t):
                c = sum(ATT_HEADS[:m]) + t
                dve.wait_ge(prob_turned, c + 1)
                nc.vector.tensor_copy(prob_t[:], ps_turn[:, 0:3 * P]).then_inc(prob_t_ready, 1)

            def att_take(m, t):
                c = sum(ATT_HEADS[:m]) + t
                dve.wait_ge(att_ready, c + 1)
                if m == 0:
                    ins = nc.vector.tensor_copy(u[:, 4 + t], ps_stat[:, T:2 * T])
                else:
                    q = slice(64 * (t % 2), 64 * (t % 2) + 64)
                    ins = nc.vector.tensor_copy(u[q, 4 + t // 2], ps_stat[q, T:2 * T])
                ins.then_inc(att_taken, 1)

            def qk_square(m, tile):
                nc.vector.tensor_tensor(qk_sq[:, 0:2], tile[:, 0:2], tile[:, 0:2], ALU.mult).then_inc(qk_squared, 1)
                nc.vector.tensor_tensor(qk_sq[:, 2:4], tile[:, 2:4], tile[:, 2:4], ALU.mult).then_inc(qk_squared, 1)

            def qk_norm(m, j):
                dve.wait_ge(qk_root, 2 * (m - 1) + j + 1)
                at = (A_FQ if j == 0 else A_FK) + m - 1
                if j:
                    nc.vector.scalar_tensor_tensor(out=ak[:], in0=ak[:], scalar=vec_a[:, at:at + 1], in1=qk_sq[:],
                                                   op0=ALU.mult, op1=ALU.mult).then_inc(qk_normed, 1)
                    return
                dve.wait_ge(qz_clear, m)
                by_head = qz.rearrange("p (a b) t -> p a b t", b=2)
                for b in range(2):
                    r = slice(64 * b, 64 * b + 64)
                    ins = nc.vector.scalar_tensor_tensor(out=by_head[r, :, b], in0=aq[r], scalar=vec_a[r, at:at + 1],
                                                         in1=qk_sq[r], op0=ALU.mult, op1=ALU.mult)
                    link(ins)

            def take(m, s):
                n0, e0 = seg(f"in{m}")
                name, _, kind = IN_CHUNKS[m][s]
                ps = acc[(e0 + s) % 2][:].rearrange("p (a t) -> p a t", a=2)
                dve.wait_ge(chunk_used, RING + n0 + s + 1)
                v = nc.vector
                if name == "lq":
                    dst = lq
                elif name == "lk":
                    dst = lk
                elif name[:2] in ("lv", "av"):
                    c = 256 * int(name[2])
                    dst = (lv if name[0] == "l" else av)[:, :, c:c + 256]
                elif name[:2] in ("aq", "ak"):
                    c = 2 * int(name[2])
                    dst = (aq if name[1] == "q" else ak)[:, c:c + 2]
                else:
                    c = int(name[1:])
                    dst = gat[:, c:c + 2]
                if m == 0:
                    factor = {"lq": 64 ** -0.5, "aq": ATT_DH[0] ** -0.5}.get(name[:2], 1.0)
                    ins = v.tensor_scalar(dst, ps, factor, None, ALU.mult)
                elif kind == "f":
                    ins = v.tensor_tensor(dst, ps, by_token(2), ALU.mult)
                else:
                    for tt in range(TT):
                        ins = v.tensor_scalar(dst[:, tt], ps[:, tt], rstd[:, T + tt:T + tt + 1], None, ALU.mult)
                ins.then_inc(evacuated, 1)

            def mixer(m):
                n0, e0 = seg(f"in{m}")
                steps = len(IN_CHUNKS[m])
                for s in range(mixer_steps(m)):
                    if m == 0 and ADA_FIRST + KF + 2 * KD + s < ADA:
                        ada_sum(ADA_FIRST + KF + 2 * KD + s)
                    if m == 0 and s == 0:
                        dve.wait_ge(pe_glr, 1)
                        nc.vector.tensor_copy(glr, ps_stat[0:GLR_N, T:2 * T]).then_inc(dve_glr, 1)
                    if m and s == 1:
                        dve.wait_ge(f_ready, m)
                        link(nc.vector.tensor_tensor(f8[:, 0], ps_score[0:8, 0:T], rstd[0:8, 0:T], ALU.mult))
                        nc.vector.tensor_scalar(f8[:, 0], f8[:, 0], fbias[:, m - 1:m], None, ALU.add
                                                ).then_inc(f_taken, 1)
                    if m == 0 and s == 1:
                        dve.wait_ge(pe_z, 1)
                        for hp in range(2):
                            ins = nc.vector.tensor_scalar(gat[:, 8 + hp], wide[:, hp * T:(hp + 1) * T],
                                                          vec_a[:, A_BGL + hp:A_BGL + hp + 1], None, ALU.add)
                        ins.then_inc(z_ready, 1)
                    if s == LIN_FIRST:
                        log_gates(m)
                    l = s - LIN_FIRST
                    if 2 <= l < len(LEVELS) + 2:
                        level_take(m, l - 2)
                    if m and s in (Q_AT, K_AT):
                        dve.wait_ge(evacuated, 2 + e0 + s)
                        qk_square(m, aq if s == Q_AT else ak)
                    if m and s in (Q_AT + 1, K_AT + 1):
                        qk_norm(m, s == K_AT + 1)
                    t = s - ATT_FIRST[m] - 1
                    if 2 <= t < ATT_HEADS[m] + 2:
                        att_take(m, t - 2)
                    if 1 <= t < ATT_HEADS[m] + 1:
                        prob_take(m, t - 1)
                    t += 1
                    if 0 <= t < ATT_HEADS[m]:
                        softmax(m, t)
                    if s < steps:
                        split_ahead(n0 + s)
                        take(m, s)
                w = LIN_DV[m] * 4 // P
                lin = u[:, LIN_AT[m]:LIN_AT[m] + w]
                xs = xqk[:].rearrange("p a b t -> p (a b) t")[:, 0:w]
                ds = dec.rearrange("p a b t -> p (a b) t")[:, 0:w]
                dve.wait_ge(lin_ready, m + 1)
                nc.vector.tensor_copy(lin, wide[:, 0:w * T].rearrange("p (k t) -> p k t", t=T)).then_inc(lin_taken, 1)
                at = A_GLAN if m == 0 else A_HG + m - 1
                dve.wait_ge(lin_rms, m + 1)
                link(nc.vector.scalar_tensor_tensor(out=lin, in0=lin, scalar=vec_a[:, at:at + 1], in1=xs,
                                                    op0=ALU.mult, op1=ALU.mult))
                dve.wait_ge(gate_sig, [1, 3, 4][m])
                link(nc.vector.tensor_tensor(ds, ds, gat[:, 0:w], ALU.mult))
                nc.vector.tensor_tensor(lin, lin, ds, ALU.mult).then_inc(mixed, 4)
                split_u("branch" if m == 0 else f"out{m}")
                if m == 0:
                    n0, e0 = seg("branch")
                    dve.wait_ge(gate_sig, 2)
                    for t in range(KD):
                        split_ahead(n0 + t)
                        ps = acc[(e0 + t) % 2]
                        dve.wait_ge(chunk_used, RING + n0 + t + 1)
                        nc.vector.tensor_tensor(u[:, t], ps[:, 0:T], gat[:, 4 + t], ALU.mult)
                        ins = nc.vector.tensor_tensor(silu[:, t % 2], ps[:, T:2 * T], gat[:, 12 + t], ALU.mult)
                        ins.then_inc(evacuated, 1)
                        dve.wait_ge(evacuated, 2 + e0 + t + 1)
                        ins = nc.vector.tensor_tensor(u[:, t], u[:, t], silu[:, t % 2], ALU.add)
                        if t % 2:
                            ins.then_inc(mixed, 1)
                    split_u("out0")
                n0, e0 = seg(f"out{m}")
                if m == 0:
                    mod_take(6 * KD, 9 * KD, ADA)
                    gain_make(2, A_FF2)
                    link(nc.vector.tensor_scalar(half[:, 8:16], mod[:, 8 * KD:9 * KD], 0.5, None, ALU.mult))
                for t in range(4):
                    split_ahead(n0 + t)
                    dve.wait_ge(chunk_used, RING + n0 + t + 1)
                    ps = acc[(e0 + t) % 2]
                    if m == 0:
                        for j in range(2):
                            g = mod[:, 5 * KD + 2 * t + j:5 * KD + 2 * t + j + 1]
                            ins = nc.vector.scalar_tensor_tensor(out=h[:, 2 * t + j], in0=ps[:, j * T:(j + 1) * T],
                                                                 scalar=g, in1=h[:, 2 * t + j],
                                                                 op0=ALU.mult, op1=ALU.add)
                    else:
                        ins = nc.vector.tensor_tensor(h[:, 2 * t:2 * t + 2], ps[:].rearrange("p (a t) -> p a t", a=2),
                                                      h[:, 2 * t:2 * t + 2], ALU.add)
                    ins.then_inc(evacuated, 1)
                    if m:
                        for k in (2 * t, 2 * t + 1):
                            gained_lo(SPLITS.index(FOLLOWS[f"out{m}"]), next_gain(f"out{m}"), k,
                                      hi=uhi_2, dst=ulo_2)

            dve.sem_inc(lo_ready, RING)
            dve.sem_inc(evacuated, 2)
            for tile, value in ((ones, 1.0), (eps, EPS), (zero8, 0.0), (half8, 0.5), (intra, 0.0)):
                nc.vector.memset(tile[:], value).then_inc(set_up, 1)
            dve.wait_ge(consts, 32)
            nc.vector.tensor_copy(level_mask[:].rearrange("p n c -> p (n c)"), mask_in).then_inc(set_up, 1)
            dve.wait_ge(turned_a, 1)
            nc.vector.tensor_copy(vec_a[:, 0:A_ROWS], ps_score[:, 0:A_ROWS])
            ins = nc.vector.tensor_copy(vec_b[:, 0:B_ROWS], ps_score[:, P:P + B_ROWS])
            ins.then_inc(vec_ready, 1)
            dve.wait_ge(vec_ready, 1)
            link(nc.vector.tensor_scalar(vec_a[:, A_FQ:A_FQ + 2], vec_a[:, A_FQ:A_FQ + 2], ATT_DH[1] ** -0.5, None,
                                         ALU.mult))
            l0, l1 = vec_b[:, B_LB:B_LB + 2], vec_b[:, B_LB + 2:B_LB + 4]
            link(nc.vector.tensor_tensor(lbt[:, 8:10], l0, l1, ALU.max))
            link(nc.vector.tensor_tensor(lbt[:, 0:2], l0, lbt[:, 8:10], ALU.subtract))
            nc.vector.tensor_tensor(lbt[:, 2:4], l1, lbt[:, 8:10], ALU.subtract).then_inc(lb_in, 1)
            dve.wait_ge(lb_exp, 1)
            link(nc.vector.tensor_tensor(lbt[:, 8:10], lbt[:, 4:6], lbt[:, 6:8], ALU.add))
            link(nc.vector.reciprocal(lbt[:, 10:12], lbt[:, 8:10]))
            link(nc.vector.tensor_tensor(lbt[:, 0:2], lbt[:, 4:6], lbt[:, 10:12], ALU.mult))
            link(nc.vector.tensor_tensor(lbt[:, 2:4], lbt[:, 6:8], lbt[:, 10:12], ALU.mult))
            link(nc.vector.tensor_tensor(lb[:, 0:2], lbt[:, 0:2], lbt[:, 0:2], ALU.subtract))
            link(nc.vector.tensor_tensor(lb[:, 2:4], lbt[:, 0:2], lbt[:, 2:4], ALU.add))
            link(nc.vector.tensor_tensor(lb[:, 2:4], lb[:, 2:4], lbt[:, 0:2], ALU.subtract))
            link(nc.vector.tensor_scalar(lb[:, 0:4], lb[:, 0:4], 0.0, 1.0, ALU.max, ALU.min))
            link(nc.vector.tensor_scalar(lb[:, 4:8], lb[:, 0:4], -1.0, 1.0, ALU.mult, ALU.add))
            dve.wait_ge(toe_psum, 1)
            nc.vector.tensor_tensor(toe_row, ps_turn[0:4, 0:384], prob_t[0:4, :], ALU.add
                                    ).then_inc(toe_sb, 1)
            for k in range(KD):
                dve.wait_ge(x_turned, k + 1)
                nc.vector.tensor_copy(h[:, k], wide[:, k % 2 * 512:k % 2 * 512 + T]).then_inc(x_taken, 1)
            dve.wait_ge(c_ready, 1)
            link(nc.vector.tensor_tensor(gain_f[:], vec_a[:, A_FIN:A_FIN + 8], vec_b[:, B_FF1:B_FF1 + 8], ALU.mult))
            for l in range(2):
                g = vec_b[:, B_MIX + 8 * l:B_MIX + 8 * l + 8].unsqueeze(2).to_broadcast([P, KD, FF_N])
                nc.vector.tensor_tensor(wff[:, l], wff[:, l], g, ALU.mult).then_inc(wff_ready, 1)
            for n in range(LEAD):
                split_lo(n)
            mod_take(0, 2 * KD, ADA_FIRST)
            gain_make(0, A_FF1)
            dve.wait_ge(mods, 1)
            norm("up0")
            ffn(0)
            mod_take(3 * KD, 6 * KD, ADA_FIRST + KF + 2 * KD)
            gain_make(1, A_MIX)
            dve.wait_ge(mods, 2)
            norm("in0")
            mixer(0)
            dve.wait_ge(mods, 3)
            norm("up1")
            ffn(1)
            final_norms()
            for layer in (1, 2):
                if layer > 1:
                    scale_of(f"up{2 * layer}")
                ffn(2 * layer)
                scale_of(f"in{layer}")
                mixer(layer)
                scale_of(f"up{2 * layer + 1}")
                ffn(2 * layer + 1)
            for c in range(TT * KD // 4):
                dve.wait_ge(out_turned, c + 1)
                nc.vector.tensor_copy(u[:].rearrange("p k t -> p (k t)")[:, c * 512:(c + 1) * 512],
                                      wide[:, c % 2 * 512:(c % 2 + 1) * 512]).then_inc(out_taken, 1)

        @block.tensor
        def _(pe):
            mm = nc.tensor.matmul

            def three(dst, wh, wl, xh, xl, first, last):
                mm(dst, wh, xh, start=first, stop=False)
                mm(dst, wh, xl, start=False, stop=False)
                return mm(dst, wl, xh, start=False, stop=last)

            def chunk_in(n, it=0):
                pe.wait_ge(lo_ready, it * RING + RING + n + 1)

            def bank_free(e, it=0, per=1):
                pe.wait_ge(evacuated, it * per + e + 1)

            def feature_tiles(n, dst, tiles, width, kt, waits=None, x=(uhi, ulo)):
                vh, vl = kview(whi, n % RING, KD, width), kview(wlo, n % RING, KD, width)
                for j in range(tiles):
                    c = slice(j * P, (j + 1) * P)
                    for k in range(kt):
                        if waits is not None and j == 0 and k % 2 == 0:
                            pe.wait_ge(ulo_ready, waits + k + 2)
                        ins = three(dst[:, j * T:(j + 1) * T], vh[:, k, c], vl[:, k, c], x[0][:, k], x[1][:, k],
                                    k == 0, k == kt - 1)
                return ins

            def token_tiles(n, dst):
                vh, vl = kview(whi, n % RING, KD, 256), kview(wlo, n % RING, KD, 256)
                for tt in range(TT):
                    c = slice(tt * P, (tt + 1) * P)
                    for k in range(KD):
                        d = dst[:, tt * 256:(tt + 1) * 256]
                        mm(d, uhi[:, k, c], vh[:, k], start=k == 0, stop=False)
                        mm(d, uhi[:, k, c], vl[:, k], start=False, stop=False)
                        ins = mm(d, ulo[:, k, c], vh[:, k], start=False, stop=k == KD - 1)
                return ins

            def mod_column(t, it=0):
                pe.wait_ge(ada_step, it * RING * KD + (t - ADA_FIRST + 1) * KD)
                dst = column(ps_mod, t, it, RING)
                mm(dst, ada_acc[:, t % 2, 0], ones[:, 0:1], start=True, stop=False)
                mm(dst, ada_acc[:, t % 2, 1], ones[:, 0:1], start=False, stop=True).then_inc(mod_ready, 1)

            def mod_columns_early(t):
                pe.wait_ge(early_landed[t], 16)
                for j in range(2):
                    for k in range(KD):
                        ins = mm(ps_mod[:, 2 * t + j:2 * t + j + 1], ada_early[:, t, k, j * P:(j + 1) * P],
                                 c_act[:, k:k + 1], start=k == 0, stop=k == KD - 1)
                    if j == 0:
                        ins.then_inc(mod_ready, 1)
                ins.then_inc(mod_ready, 1)

            def norm(name):
                i = STATS.index(name)
                pe.wait_ge(summed, i + 1 + (i > 2))
                ins = mm(ps_stat[:, 0:T], ones[:], sumsq[:], start=True, stop=True)
                if i > 2:
                    for tt in range(TT):
                        ins = mm(ps_stat[:, T + tt:T + tt + 1], sumsq[:, tt * P:(tt + 1) * P], ones[:, 0:1],
                                 start=True, stop=True)
                ins.then_inc(stat, 1)

            def final_norms():
                pe.wait_ge(summed, 4)
                mm(ps_stat[:, 0:T], ones[:], sumsq[:], start=True, stop=True).then_inc(stat, 1)
                mm(ps_stat[:, T:2 * T], ones[:], sumsq_f, start=True, stop=True).then_inc(stat_f, 1)

            def ffn(i):
                n0, e0 = seg(f"up{i}")
                waits = KD * SPLITS.index(f"up{i}")

                def step(t, it=0):
                    chunk_in(n0 + t, it)
                    bank_free(e0 + t, it, RING)
                    feature_tiles(n0 + t, acc[(e0 + t) % 2], 2, 2 * P, KD, waits if t == 0 else None,
                                  (uhi_2, ulo_2) if i in (3, 5) else (uhi, ulo)).then_inc(chunk_used, 1)
                    if i == 0:
                        mod_column(ADA_FIRST + t, it)

                with pe.Fori(0, KF // RING) as it:
                    for t in range(RING):
                        step(t, it)
                for t in range(KF // RING * RING, KF):
                    step(t)
                n0, e0 = seg(f"down{i}")
                with pe.Fori(0, 2 * KD // RING) as it:
                    for t in range(RING):
                        m, side = t // 2, t % 2
                        chunk_in(n0 + t, it)
                        if side == 0:
                            bank_free(e0 + m, it, 2)
                        if t < 2:
                            pe.wait_ge(hlo_ready, KF * i + KF // 2 * (side + 1))
                        vh = kview(whi, (n0 + t) % RING, KF // 2, P)
                        vl = kview(wlo, (n0 + t) % RING, KF // 2, P)
                        for k in range(KF // 2):
                            kk = side * (KF // 2) + k
                            ins = three(acc[(e0 + m) % 2][:, 0:T], vh[:, k], vl[:, k], hhi[:, kk], hlo[:, kk],
                                        kk == 0, kk == KF - 1)
                        ins.then_inc(chunk_used, 1)
                        if i == 0:
                            mod_column(ADA_FIRST + KF + t, it)

            def level_column(hd, tt):
                return (4 * (hd % 2) + 2 * (hd // 2) + tt) * P

            def level_scores(m, l):
                s = LEVELS[l]
                c = m * len(LEVELS) + l
                if c:
                    pe.wait_ge(level_taken, c)
                if s:
                    pe.wait_ge(xqk_ready, m * (len(LEVELS) - 1) + l + 1)
                for hd in range(4):
                    r, hp = slice(64 * (hd % 2), 64 * (hd % 2) + 64), hd // 2
                    key = xqk[:, l % 2] if s else lk
                    query = xqk[:, l % 2] if s else lq
                    if l == 0:
                        j = level_column(hd, 0)
                        ins = mm(wide[:, j:j + P], key[r, hp, 0:P], query[r, hp, P:T], start=True, stop=True)
                    else:
                        for tt in range(TT):
                            c = slice(tt * P, (tt + 1) * P)
                            j = level_column(hd, tt)
                            ins = mm(wide[:, j:j + P], key[r, hp, c], query[r, hp, c], start=True, stop=True)
                ins.then_inc(level_ready, 1)

            def lin_out(m):
                dv = LIN_DV[m]
                pe.wait_ge(level_taken, (m + 1) * len(LEVELS))
                for hd in range(4):
                    vals = [lv[:, tt, hd * dv:(hd + 1) * dv] for tt in range(TT)]
                    if m == 0:
                        dst = wide[:, hd * T:(hd + 1) * T]
                    else:
                        dst = wide[64 * (hd % 2):64 * (hd % 2) + 64, hd // 2 * T:(hd // 2 + 1) * T]
                    j = level_column(hd, 0) // P
                    mm(dst[:, 0:P], vals[0], intra[:, j], start=True, stop=True)
                    mm(dst[:, P:T], vals[0], cross[:, j // 2], start=True, stop=False)
                    ins = mm(dst[:, P:T], vals[1], intra[:, j + 1], start=False, stop=True)
                ins.then_inc(lin_ready, 1)

            def lin_norm(m):
                pe.wait_ge(lin_sq, m + 1)
                w = LIN_DV[m] * 4 // P
                xs = xqk[:].rearrange("p a b t -> p (a b t)")
                for j in range(w // 2):
                    ins = mm(wide[:, j * 512:(j + 1) * 512], ones[:] if m == 0 else same_head,
                             xs[:, j * 512:(j + 1) * 512], start=True, stop=True)
                ins.then_inc(lin_stat, 1)

            def att_scores(m, t):
                c = sum(ATT_HEADS[:m]) + t
                if c:
                    pe.wait_ge(exp_ready, 2 * c if t == 0 or m == 0 else 2 * c - 2)
                if m == 0:
                    q, k = aq[:, t], ak[:, t]
                else:
                    q, k = qz[:, t], ak[:, t // 2]
                ps = score_bank(m, t)
                if m and t == 0:
                    pe.wait_ge(qk_normed, m)
                    pe.wait_ge(negc_ready, m)
                for dst, qs, n in ((ps[:, 0:P], slice(0, P), P), (ps[:, P:3 * P], slice(P, T), T)):
                    mm(dst, q[:, qs], k[:, 0:n], start=True, stop=False)
                    if m == 0:
                        ins = mm(dst, anti, toe[:, t, T - n:T], start=False, stop=True)
                    else:
                        mm(dst, pick(t), negc[0:8, 0:n], start=False, stop=False)
                        ins = mm(dst[:, n - P:n], ident, causal, start=False, stop=True)
                ins.then_inc(scores_ready, 1)

            def att_turn(m, t):
                c = sum(ATT_HEADS[:m]) + t
                pe.wait_ge(prob_ready, c + 1)
                if c:
                    pe.wait_ge(prob_t_ready, c)
                for j in range(3):
                    ins = nc.tensor.transpose(ps_turn[:, j * P:(j + 1) * P], prob[:, j * P:(j + 1) * P], ident)
                ins.then_inc(prob_turned, 1)

            def att_out(m, t):
                c = sum(ATT_HEADS[:m]) + t
                dh = ATT_DH[m]
                pe.wait_ge(prob_t_ready, c + 1)
                if c:
                    pe.wait_ge(att_taken, c)
                vals = [av[:, tt, t * dh:(t + 1) * dh] for tt in range(TT)]
                r = slice(0, P) if m == 0 else slice(64 * (t % 2), 64 * (t % 2) + 64)
                dst = ps_stat[r, T:2 * T]
                mm(dst[:, 0:P], vals[0], prob_t[:, 0:P], start=True, stop=True)
                mm(dst[:, P:T], vals[0], prob_t[:, P:2 * P], start=True, stop=False)
                mm(dst[:, P:T], vals[1], prob_t[:, 2 * P:3 * P], start=False, stop=True).then_inc(att_ready, 1)

            def qk_stat(m, j):
                c = 2 * (m - 1) + j
                for half_, ps in enumerate((ps_turn, ps_score)):
                    pe.wait_ge(qk_squared, 2 * c + half_ + 1)
                    mm(ps[:], same_head, qk_sq[:].rearrange("p k t -> p (k t)")[:, 512 * half_:512 * half_ + 512],
                       start=True, stop=True).then_inc(qk_summed, 1)

            def mixer(m):
                n0, e0 = seg(f"in{m}")
                steps = len(IN_CHUNKS[m])
                waits = KD * SPLITS.index(f"in{m}")
                pe.wait_ge(ulo_ready, waits + KD)
                if m == 0:
                    for k in range(KD):
                        ins = mm(ps_stat[0:GLR_N, T:2 * T], wlr[:, k], u[:, k], start=k == 0, stop=k == KD - 1)
                    ins.then_inc(pe_glr, 1)
                else:
                    pe.wait_ge(wff_ready, 2)
                    for k in range(KD):
                        ins = mm(ps_score[0:FF_N, 0:T], wff[:, m - 1, k], h[:, k], start=k == 0, stop=k == KD - 1)
                    ins.then_inc(f_ready, 1)
                for s in range(mixer_steps(m)):
                    if s < steps:
                        n = n0 + s
                        chunk_in(n)
                        bank_free(e0 + s)
                        dst = acc[(e0 + s) % 2]
                        if IN_CHUNKS[m][s][2] == "t":
                            ins = token_tiles(n, dst)
                        else:
                            ins = feature_tiles(n, dst, 2, 256, KD)
                        ins.then_inc(chunk_used, 1)
                        if m == 0 and ADA_FIRST + KF + 2 * KD + s < ADA:
                            mod_column(ADA_FIRST + KF + 2 * KD + s)
                    if m == 0 and s == 0:
                        pe.wait_ge(dve_glr, 1)
                        for hp in range(2):
                            ins = mm(wide[:, hp * T:(hp + 1) * T], wgl[:, hp * P:(hp + 1) * P], glr,
                                     start=True, stop=True)
                        ins.then_inc(pe_z, 1)
                    l = s - LIN_FIRST - 1
                    if 0 <= l < len(LEVELS):
                        level_scores(m, l)
                    if m and s in (Q_AT, K_AT):
                        qk_stat(m, s == K_AT)
                    t = s - ATT_FIRST[m]
                    if 0 <= t < ATT_HEADS[m]:
                        att_scores(m, t)
                    if 1 <= t < ATT_HEADS[m] + 1:
                        att_turn(m, t - 1)
                    if 2 <= t < ATT_HEADS[m] + 2:
                        att_out(m, t - 2)
                lin_out(m)
                lin_norm(m)
                if m == 0:
                    n0, e0 = seg("branch")
                    pe.wait_ge(ulo_ready, KD * SPLITS.index("branch") + KD)
                    for t in range(KD):
                        chunk_in(n0 + t)
                        bank_free(e0 + t)
                        vh, vl = kview(whi, (n0 + t) % RING, KD, P), kview(wlo, (n0 + t) % RING, KD, P)
                        for j in range(2):
                            for k in range(4 * j, 4 * j + 4):
                                ins = three(acc[(e0 + t) % 2][:, j * T:(j + 1) * T], vh[:, k], vl[:, k], uhi[:, k],
                                            ulo[:, k], k % 4 == 0, k % 4 == 3)
                        ins.then_inc(chunk_used, 1)
                n0, e0 = seg(f"out{m}")
                waits = KD * SPLITS.index(f"out{m}")
                for t in range(4):
                    chunk_in(n0 + t)
                    bank_free(e0 + t)
                    feature_tiles(n0 + t, acc[(e0 + t) % 2], 2, 256, KD, waits if t == 0 else None
                                  ).then_inc(chunk_used, 1)

            pe.sem_inc(chunk_used, RING)
            pe.sem_inc(mod_ready, 2)
            pe.wait_ge(consts, 32)
            pe.wait_ge(small, 16 * len(small_loads))
            nc.tensor.transpose(ps_score[:, 0:A_ROWS], stage[0:A_ROWS, 0], const[0:A_ROWS, C_IDENT:C_IDENT + A_ROWS])
            nc.tensor.transpose(ps_score[:, P:P + B_ROWS], stage[0:B_ROWS, 1],
                                const[0:B_ROWS, C_IDENT:C_IDENT + B_ROWS]).then_inc(turned_a, 1)
            mm(ps_turn[0:4, 0:384], rel[:], prob[0:NUM_BUCKETS, :], start=True, stop=True
               ).then_inc(toe_psum, 1)
            pe.wait_ge(x_in, 16)
            xt = u[:].rearrange("p k t -> p (k t)")
            for k in range(KD):
                if k >= 2:
                    pe.wait_ge(x_taken, k - 1)
                for tt in range(TT):
                    at = k % 2 * 512 + tt * P
                    ins = nc.tensor.transpose(wide[:, at:at + P],
                                              xt[:, tt * D + k * P:tt * D + (k + 1) * P], ident)
                ins.then_inc(x_turned, 1)
            pe.wait_ge(set_up, 6)
            pe.wait_ge(c_ready, 1)
            for t in range(ADA_FIRST // 2):
                mod_columns_early(t)
            pe.wait_ge(toe_in, 16)
            norm("up0")
            ffn(0)
            norm("in0")
            mixer(0)
            norm("up1")
            ffn(1)
            final_norms()
            for layer in (1, 2):
                if layer > 1:
                    norm(f"up{2 * layer}")
                ffn(2 * layer)
                norm(f"in{layer}")
                mixer(layer)
                norm(f"up{2 * layer + 1}")
                ffn(2 * layer + 1)
            pe.wait_ge(evacuated, 2 + UNIT["down5"] + KD)
            for c in range(TT * KD // 4):
                tt, k0 = c // 2, 4 * (c % 2)
                if c >= 2:
                    pe.wait_ge(out_taken, c - 1)
                for k in range(4):
                    at = c % 2 * 512 + k * P
                    ins = nc.tensor.transpose(wide[:, at:at + P], h[:, k0 + k, tt * P:(tt + 1) * P], ident)
                ins.then_inc(out_turned, 1)


_INS = ["x", "c", "w_ada", "b_ada", "norm_ff1", "w_ff1_gate", "w_ff1_up", "w_ff1_down", "norm_mix", "w_in", "w_gla_lr",
        "b_gla_lr", "gla_norm", "rel_bias", "w_br_gla", "w_br_moba", "w_out", "norm_ff2", "w_ff2_gate", "w_ff2_up",
        "w_ff2_down", "norm_final", "ffn1_norm_2", "ffn1_w_in_2", "ffn1_w_out_2", "mix_norm_2", "w_mix_in_2",
        "conv_w_2", "hgrn_lb_logits_2", "hgrn_out_gain_2", "fox_q_gain_2", "fox_k_gain_2", "fox_f_bias_2",
        "w_mix_out_2", "ffn2_norm_2", "ffn2_w_in_2", "ffn2_w_out_2"]


def kernel(**inputs):
    import concourse.bacc as bacc
    from concourse.bass_utils import run_bass_kernel_spmd

    nc = bacc.Bacc("TRN2", target_bir_lowering=False, num_devices=1)
    arrays, aps = {}, {}
    constants, masks, by_distance = shape_constants()
    given = {name: np.ascontiguousarray(inputs[name]) for name in _INS}
    for name, value in {**given, "shape_constants": constants, "level_masks": masks,
                        "by_distance": by_distance}.items():
        arrays[f"in_{name}"] = value
        aps[name] = nc.dram_tensor(f"in_{name}", value.shape, mybir.dt.from_np(value.dtype), kind="ExternalInput").ap()
    out = nc.dram_tensor("out", (1, T, D), F32, kind="ExternalOutput").ap()
    build(nc, aps, out)
    result = run_bass_kernel_spmd(nc, [arrays], core_ids=[0])
    return result.results[0]["out"]
```

```python
from contextlib import ExitStack

import concourse.bass as bass
from concourse import mybir
import numpy as np

F32 = mybir.dt.float32
F32R = mybir.dt.float32r
U8 = mybir.dt.uint8
ALU = mybir.AluOpType
ACT = mybir.ActivationFunctionType
AX_X = mybir.AxisListType.X

P = 128
T = 256
TT = T // P
D = 1024
KD = D // P
F = 2816
KF = F // P
RING = 4
SLOT = 2048
HI_LEAD = 3
LO_LEAD = 2
NMOD = 9
ADA = NMOD * KD
ADA_FIRST = 2 * KD
GROUPS = NMOD - 2
PIECE = D
DIRECT = 3
EPS = 1e-6
NEG = -1e30
LEVELS = [128, 64, 32, 16, 8, 4, 2, 1, 0]
MAX_EXACT, NUM_BUCKETS, MAX_DISTANCE = 16, 32, 128
LIN_FIRST = [3, 2, 2]
TAU = 16.0

GLA_CHUNKS = [("lq", 0, "f"), ("lk", 256, "f"), ("lv0", 512, "t"), ("lv1", 768, "t"),
              ("aq0", 1552, "f"), ("aq1", 1808, "f"), ("ak0", 2064, "f"), ("ak1", 2320, "f"),
              ("av0", 2576, "t"), ("av1", 2832, "t"), ("g0", 1040, "f"), ("g2", 1296, "f")] + \
             [(f"g{4 + 2 * i}", 3088 + 256 * i, "f") for i in range(8)]
MIX_CHUNKS = [("g8", 1024, "f"), ("lq", 768, "f"), ("aq0", 1792, "f"), ("aq1", 2048, "f"),
              ("ak0", 2304, "f"), ("ak1", 2560, "f"), ("av0", 2816, "t"), ("g4", 0, "f"), ("av1", 3072, "t"),
              ("g6", 512, "f"), ("g12", 256, "f"), ("lv0", 1280, "t"), ("g0", 1536, "f")]
GLR_AT, GLR_N = 1024, 16
FF_AT, FF_N = 3328, 8
IN_CHUNKS = [GLA_CHUNKS, MIX_CHUNKS, MIX_CHUNKS]
ATT_HEADS = [4, 8, 8]
ATT_DH = [128, 64, 64]
ATT_FIRST = [10, 7, 7]
LIN_DV = [128, 64, 64]
Q_AT, K_AT = 4, 6
LIN_AT = [0, 2, 2]


def chunk_columns():
    cols, first = [], {}

    def add(name, counts):
        first[name] = len(cols)
        cols.extend(counts)

    def ffn(i):
        add(f"up{i}", [SLOT] * KF)
        add(f"down{i}", [KF // 2 * P] * (2 * KD))

    ffn(0)
    add("in0", [SLOT] * len(GLA_CHUNKS))
    add("branch", [KD * P] * KD)
    add("out0", [SLOT] * 4)
    ffn(1)
    for layer in (1, 2):
        ffn(2 * layer)
        add(f"in{layer}", [SLOT] * len(MIX_CHUNKS))
        add(f"out{layer}", [SLOT] * 4)
        ffn(2 * layer + 1)
    return cols, first


def att_slot(m, s, side):
    if m == 0:
        return s - ATT_FIRST[m] if side else None
    return 2 * (s - ATT_FIRST[m]) + side


STEPS = [len(chunks) for chunks in IN_CHUNKS]
LIN_OUT = [13, 12, 12]
PAIRS = [[0, 1, 2, 3], [2, 3, 0, 1], [2, 3, 0, 1]]


COLS, FIRST = chunk_columns()
UNIT = {}


def count_units():
    n = 0
    names = sorted(FIRST, key=FIRST.get)
    for name in names:
        UNIT[name] = n
        n += {"up": KF, "do": KD, "br": KD, "ou": 4}.get(name[:2], 0)
        if name[:2] == "in":
            n += len(IN_CHUNKS[int(name[2:])])


count_units()
STATS = ["up0", "in0", "up1", "in1", "up3", "up4", "in2", "up5"]
FOLLOWS = {"down1": "up2", "down2": "in1", "out1": "up3", "down3": "up4", "down4": "in2", "out2": "up5"}
SPLITS = ["up0", "in0", "branch", "out0", "up1", "up2", "in1", "out1", "up3", "up4", "in2", "out2", "up5"]

C_IDENT, C_ANTI, C_HEAD, C_CAUSAL = 0, 128, 256, 384
C_N = 512


def shape_constants():
    c = np.zeros((P, C_N), np.float32)
    i = np.arange(P)
    c[:, C_IDENT:C_IDENT + P] = np.eye(P)
    c[:, C_ANTI:C_ANTI + P] = np.eye(P)[::-1]
    c[:, C_HEAD:C_HEAD + P] = (i[:, None] // 64 == i[None, :] // 64)
    c[:, C_CAUSAL:C_CAUSAL + P] = np.where(i[:, None] >= i[None, :], 0.0, NEG)
    dist = (T - 1) - np.arange(384)
    n = np.maximum(dist, 0)
    nf = np.maximum(n, 1).astype(np.float32)
    large = MAX_EXACT + (np.log(nf / np.float32(MAX_EXACT)) / np.float32(np.log(MAX_DISTANCE / MAX_EXACT))
                         * np.float32(NUM_BUCKETS - MAX_EXACT)).astype(np.int32)
    bucket = np.where(n < MAX_EXACT, n, np.minimum(large, NUM_BUCKETS - 1))
    by_distance = np.zeros((NUM_BUCKETS + 4, 384), np.float32)
    by_distance[bucket, np.arange(384)] = 1.0
    by_distance[NUM_BUCKETS:] = np.where(dist >= 0, 0.0, NEG)
    m = np.zeros((P, len(LEVELS) - 1, P), np.float32)
    key, query = i[:, None], i[None, :]
    for n, s in enumerate(LEVELS[1:]):
        if s:
            m[:, n] = (key // (2 * s) == query // (2 * s)) & (key % (2 * s) < s) & (query % (2 * s) >= s)
        else:
            m[:, n] = key == query
    return c, m.reshape(P, -1), by_distance


def build(nc, a, out):
    with ExitStack() as ctx:
        ctx.enter_context(nc.allow_non_contiguous_dma(reason="two vectors of a few elements"))
        def sb(name, shape, dt=F32):
            return ctx.enter_context(nc.sbuf_tensor(name, shape, dt))

        def sem(name):
            return ctx.enter_context(nc.semaphore(name))

        raw = sb("raw", [P, RING, SLOT])
        early = ExitStack()
        ada_early = early.enter_context(nc.sbuf_tensor("ada_early", [P, KD, 2 * D], F32))
        early.close()
        whi = sb("whi", [P, RING, SLOT], F32R)
        wlo = sb("wlo", [P, RING, SLOT], F32R)
        h = sb("h", [P, KD, T])
        u = sb("u", [P, KD, T])
        uhi = sb("uhi", [P, KD, T], F32R)
        ulo = sb("ulo", [P, KD, T], F32R)
        work = sb("work", [P, 4, T])
        silu, hid = work[:, 0:2], work[:, 2:4]
        gate_up = work[:].rearrange("p (a b) t -> p a b t", a=2)
        dec = work[:].rearrange("p (a b) t -> p a b t", a=2)
        f8 = work[0:8]
        glr = work[0:GLR_N, 2]
        place_of_in_turn = ExitStack()
        mix_lo = place_of_in_turn.enter_context(nc.sbuf_tensor("mix_lo", [P, KD, T], F32R))
        place_of_in_turn.close()
        in_turn = sb("in_turn", [P, 2 * PIECE])
        ada_raw = in_turn[:].rearrange("p (a c) -> p a c", a=2)
        qz = in_turn[:].rearrange("p (a t) -> p a t", t=T)
        const = sb("const", [P, C_N])
        ones = sb("ones", [P, P])
        vec_a = sb("vec_a", [P, P])
        vec_b = sb("vec_b", [P, P])
        c_act = sb("c_act", [P, KD])
        mod = sb("mod", [P, ADA])
        gain = sb("gain", [P, 3, KD])
        half = sb("half", [P, 2 * KD])
        eps = sb("eps", [P, 1])
        zero8 = sb("zero8", [P, KD])
        half8 = sb("half8", [P, KD])
        sumsq = sb("sumsq", [P, T])
        sq = sb("sq", [P, T])
        stage = sq[:].rearrange("p (a c) -> p a c", a=2)
        rstd = sb("rstd", [P, T + TT])
        gain_f = sb("gain_f", [P, KD])
        wlr = sb("wlr", [P, KD, GLR_N])
        wff = sb("wff", [P, 2, KD, FF_N])
        wgl = sb("wgl", [GLR_N, 256])
        rel = sb("rel", [NUM_BUCKETS, 4])
        fbias = sb("fbias", [8, 2])
        negc = sb("negc", [8, T])
        toe_row = sb("toe_row", [4, 384])
        lb = sb("lb", [P, 8])
        lbt = sb("lbt", [P, 12])
        st_max = sb("st_max", [P, 2, 8])
        scratch = nc.dram_tensor("bias_by_distance", [4, 384], F32)

        intra = sb("intra", [P, 8, P])
        level_mask = sb("level_mask", [P, len(LEVELS) - 1, P], U8)
        toe = sb("toe", [P, 4, T])
        rstd_f, sumsq_f = toe[:, 0], toe[:, 1]
        qk_sq = toe

        hidden = ExitStack()
        hhi = hidden.enter_context(nc.sbuf_tensor("hhi", [P, KF, T], F32R))
        hlo = hidden.enter_context(nc.sbuf_tensor("hlo", [P, KF, T], F32R))
        hidden.close()
        lv = sb("lv", [P, TT, 512])
        place_of_aq_ak = ExitStack()
        mix_hi = place_of_aq_ak.enter_context(nc.sbuf_tensor("mix_hi", [P, KD, T], F32R))
        place_of_aq_ak.close()
        aq = sb("aq", [P, 4, T])
        ak = sb("ak", [P, 4, T])
        av = sb("av", [P, TT, 512])
        gat = sb("gat", [P, 20, T])
        lq, lk = gat[:, 16:18], gat[:, 18:20]
        mask_in = gat[:].rearrange("p a t -> p (a t)")[:, 0:(len(LEVELS) - 1) * P]
        early_sum = gat[:, 4:12].rearrange("p a t -> p (a t)")
        piece_sums = [intra[:].rearrange("p a c -> p (a c)")] * 5 + [gat[:, 12:16].rearrange("p a t -> p (a t)")] * 2
        bcum = sb("bcum", [P, 2, T])
        xqk = sb("xqk", [P, 2, 2, T])
        cross = sb("cross", [P, 4, P])
        prob = sb("prob", [P, 384])
        prob_t = sb("prob_t", [P, 384])

        psum = [ctx.enter_context(nc.psum_tensor(f"bank{i}", [P, 512], F32)) for i in range(4)]
        wide = ctx.enter_context(nc.psum_tensor("wide", [P, 1024], F32))
        ps_score = ctx.enter_context(nc.psum_tensor("ps_score", [P, 512], F32))
        ps_turn = ctx.enter_context(nc.psum_tensor("ps_turn", [P, 512], F32))
        acc = psum[0:2]
        ps_stat, ps_mod = psum[2], psum[3]

        ident = const[:, C_IDENT:C_IDENT + P]
        anti = const[:, C_ANTI:C_ANTI + P]
        same_head = const[:, C_HEAD:C_HEAD + P]
        causal = const[:, C_CAUSAL:C_CAUSAL + P]

        def pick(hd):
            return const[0:8, C_IDENT + hd:C_IDENT + hd + 1].to_broadcast([8, P])

        landed = [sem(f"landed{i}") for i in range(RING)]
        hi_ready = sem("hi_ready")
        lo_ready = sem("lo_ready")
        chunk_used = sem("chunk_used")
        evacuated = sem("evacuated")
        silu_ready = sem("silu_ready")
        hid_ready = sem("hid_ready")
        hhi_ready = sem("hhi_ready")
        hlo_ready = sem("hlo_ready")
        ada_landed = [sem(f"ada_landed{i}") for i in range(2)]
        early_landed = [sem(f"early_landed{i}") for i in range(KD + 1)]
        early_direct = sem("early_direct")
        early_step = sem("early_step")
        masks_in, later, intra_clear = sem("masks_in"), sem("later"), sem("intra_clear")
        wff_ready = sem("wff_ready")
        ada_step = sem("ada_step")
        mod_ready = sem("mod_ready")
        mod_taken = sem("mod_taken")
        small = sem("small")
        consts = sem("consts")
        x_in = sem("x_in")
        set_up = sem("set_up")
        turned_a = sem("turned_a")
        vec_ready = sem("vec_ready")
        c_ready = sem("c_ready")
        x_turned = sem("x_turned")
        x_taken = sem("x_taken")
        mods = sem("mods")
        summed = sem("summed")
        stat = sem("stat")
        rms = sem("rms")
        scaled = sem("scaled")
        u_ready = sem("u_ready")
        uhi_ready = sem("uhi_ready")
        ulo_ready = sem("ulo_ready")
        mixed = sem("mixed")
        pe_glr, dve_glr, pe_z = sem("pe_glr"), sem("dve_glr"), sem("pe_z")
        z_ready = sem("z_ready")
        bcum_ready = sem("bcum_ready")
        conv_ready, qz_clear = sem("conv_ready"), sem("qz_clear")
        lin_mixed = sem("lin_mixed")
        stat_f, rms_f, mean_f = sem("stat_f"), sem("rms_f"), sem("mean_f")
        l_ready = sem("l_ready")
        kexp_in, kexp_out = sem("kexp_in"), sem("kexp_out")
        diffs, decays = sem("diffs"), sem("decays")
        xqk_ready, level_ready, level_taken = sem("xqk_ready"), sem("level_ready"), sem("level_taken")
        lin_ready, lin_taken = sem("lin_ready"), sem("lin_taken")
        lin_sq, lin_stat, lin_rms = sem("lin_sq"), sem("lin_stat"), sem("lin_rms")
        gate_sig = sem("gate_sig")
        f_ready, f_taken, f_log, negc_ready = sem("f_ready"), sem("f_taken"), sem("f_log"), sem("negc_ready")
        scores_ready, max_ready, exp_ready = sem("scores_ready"), sem("max_ready"), sem("exp_ready")
        prob_ready, prob_turned, prob_t_ready = sem("prob_ready"), sem("prob_turned"), sem("prob_t_ready")
        att_ready, att_taken = sem("att_ready"), sem("att_taken")
        toe_psum, toe_sb, toe_out, toe_in = sem("toe_psum"), sem("toe_sb"), sem("toe_out"), sem("toe_in")
        qk_squared, qk_summed, qk_root, qk_normed = sem("qk_squared"), sem("qk_summed"), sem("qk_root"), sem("qk_normed")
        lb_in, lb_exp = sem("lb_in"), sem("lb_exp")
        out_turned, out_taken, stored = sem("out_turned"), sem("out_taken"), sem("stored")
        dve_done, act_done, pool_done = sem("dve_done"), sem("act_done"), sem("pool_done")

        A_C, A_FF1, A_MIX, A_FF2, A_FIN, A_ADA = 0, 8, 16, 24, 32, 40
        A_GLAN, A_BGL, A_HG, A_FQ, A_FK = 112, 113, 115, 117, 119
        B_FF1, B_MIX, B_FF2, B_LB, B_CONV = 0, 16, 32, 48, 52
        A_ROWS, B_ROWS = 121, 64

        def rows(ap):
            return ap.rearrange("l (k c) -> (l k) c", c=P)

        small_loads = [
            (stage[A_C:A_C + 8, 0], rows(a["c"])), (stage[A_FF1:A_FF1 + 8, 0], rows(a["norm_ff1"])),
            (stage[A_MIX:A_MIX + 8, 0], rows(a["norm_mix"])), (stage[A_FF2:A_FF2 + 8, 0], rows(a["norm_ff2"])),
            (stage[A_FIN:A_FIN + 8, 0], a["norm_final"].rearrange("(k c) -> k c", c=P)),
            (stage[A_ADA:A_ADA + ADA, 0], rows(a["b_ada"])),
            (stage[A_GLAN:A_GLAN + 1, 0], a["gla_norm"]), (stage[A_BGL:A_BGL + 2, 0], rows(a["b_gla_lr"])),
        ]
        for at, name in ((A_HG, "hgrn_out_gain_2"), (A_FQ, "fox_q_gain_2"), (A_FK, "fox_k_gain_2")):
            small_loads += [(stage[at:at + 2, 0, 64 * i:64 * i + 64], a[name]) for i in range(2)]
        small_loads += [
            (stage[B_FF1:B_FF1 + 16, 1], rows(a["ffn1_norm_2"])), (stage[B_MIX:B_MIX + 16, 1], rows(a["mix_norm_2"])),
            (stage[B_FF2:B_FF2 + 16, 1], rows(a["ffn2_norm_2"])), (stage[B_LB:B_LB + 4, 1], rows(a["hgrn_lb_logits_2"])),
            (stage[B_CONV:B_CONV + 12, 1], a["conv_w_2"].rearrange("l w (k c) -> (l w k) c", c=P)),
        ]
        later_loads = [
            (wgl[:], a["w_gla_lr"][0]),
            (wlr[:], a["w_in"][0, :, GLR_AT:GLR_AT + GLR_N].rearrange("(k p) c -> p k c", p=P)),
            (wff[:, 0], a["w_mix_in_2"][0, :, FF_AT:FF_AT + FF_N].rearrange("(k p) c -> p k c", p=P)),
            (wff[:, 1], a["w_mix_in_2"][1, :, FF_AT:FF_AT + FF_N].rearrange("(k p) c -> p k c", p=P)),
            (rel[:], a["rel_bias"].rearrange("h b -> b h")),
            (fbias[:], a["fox_f_bias_2"].rearrange("l h -> h l")),
        ]

        later_loads += [(prob[0:NUM_BUCKETS, :], a["by_distance"][0:NUM_BUCKETS]),
                        (prob_t[0:4, :], a["by_distance"][NUM_BUCKETS:])]

        w2 = a["ffn1_w_in_2"], a["ffn2_w_in_2"]
        ffn_w = [(a["w_ff1_gate"][0], a["w_ff1_up"][0], a["w_ff1_down"][0]),
                 (a["w_ff2_gate"][0], a["w_ff2_up"][0], a["w_ff2_down"][0])]
        for layer in range(2):
            for n in range(2):
                w = w2[n][layer]
                ffn_w.append((w[:, 0:F], w[:, F:2 * F], a[f"ffn{n + 1}_w_out_2"][layer]))
        in_w = [a["w_in"][0], a["w_mix_in_2"][0], a["w_mix_in_2"][1]]
        out_w = [a["w_out"][0], a["w_mix_out_2"][0], a["w_mix_out_2"][1]]

        def norm_gain(name):
            if name in ("up0", "in0", "up1"):
                j = ("up0", "in0", "up1").index(name)
                return gain[:, j], mod[:, 3 * j * KD:(3 * j + 1) * KD]
            at = {"up2": B_FF1, "in1": B_MIX, "up3": B_FF2, "up4": B_FF1 + 8, "in2": B_MIX + 8, "up5": B_FF2 + 8}[name]
            return vec_b[:, at:at + 8], zero8

        def next_gain(name):
            if name == "down1":
                return gain_f[:]
            return norm_gain(FOLLOWS[name])[0] if name in FOLLOWS else None

        def tiles_of(tile, m, it=0, per=0):
            if isinstance(it, int):
                return tile[:, m]
            return tile[:, bass.ds(it * per + m, 1)].rearrange("p a t -> p (a t)")

        def column(tile, m, it=0, per=0):
            return tile[:, m:m + 1] if isinstance(it, int) else tile[:, bass.ds(it * per + m, 1)]

        def residual_gate(i):
            return [half[:, 0:8], half[:, 8:16]][i] if i < 2 else half8

        def seg(name):
            return FIRST[name], UNIT[name]

        def kview(tile, slot, k, width):
            return tile[:, slot, 0:k * width].rearrange("p (k c) -> p k c", k=k)

        def score_bank(m, t):
            return ps_mod if m and t % 2 else ps_score

        def up_turns(eng, i, step, after_first=None):
            wide_ = 2 if i == 0 else 1
            turns = (KF - HI_LEAD) // RING
            if after_first:
                for t in range(RING):
                    step(t)
                    if t == 0:
                        after_first()
            with eng.Fori(1 if after_first else 0, turns, wide_) as it:
                for t in range(wide_ * RING):
                    step(t, it)
            for t in range(turns * RING, KF):
                step(t)

        class Chain:

            def __init__(self, eng, done):
                self.eng, self.done, self.n, self.turn, self.per = eng, done, 0, None, 0

            def __call__(self, ins):
                self.n += 1
                ins.then_inc(self.done, 1)
                self.eng.wait_ge(self.done, self.n if self.turn is None else self.turn * self.per + self.n)

            def loop(self, turn, per):
                self.turn, self.per, self.n0 = turn, per, self.n

            def end(self, turns):
                assert self.n - self.n0 == self.per, (self.n - self.n0, self.per)
                self.n, self.turn = self.n0 + self.per * turns, None

        block = ctx.enter_context(nc.Block())

        @block.sync
        def _(sp):
            def load(n, parts, it=0):
                sp.wait_ge(lo_ready, it * RING + n + 1)
                for dst, src in parts:
                    sp.dma_start(dst, src).then_inc(landed[n % RING], 16)

            def up_parts(i, n, t, it=0):
                wg, wu, _ = ffn_w[i]
                v = kview(raw, n % RING, KD, 2 * P)
                return [(v[:, :, j * P:(j + 1) * P],
                         w[:, bass.ds(it * RING * P + t * P, P)].rearrange("(k p) c -> p k c", p=P))
                        for j, w in enumerate((wg, wu))]

            def down_parts(i, n, d, it=0):
                wd = ffn_w[i][2]
                v = kview(raw, n % RING, KF // 2, P)
                src = wd[(d % 2) * (F // 2):(d % 2 + 1) * (F // 2), bass.ds(it * 2 * P + d // 2 * P, P)]
                src = src.rearrange("(k p) c -> p k c", p=P)
                return [(v[:, 0:6], src[:, 0:6]), (v[:, 6:11], src[:, 6:11])]

            def ffn(i):
                n0 = FIRST[f"up{i}"]
                if i == 0:
                    for t in range(1, RING):
                        load(n0 + t, up_parts(i, n0 + t, t))
                with sp.Fori(1 if i == 0 else 0, KF // RING) as it:
                    for t in range(RING):
                        load(n0 + t, up_parts(i, n0 + t, t, it), it)
                for t in range(KF // RING * RING, KF):
                    load(n0 + t, up_parts(i, n0 + t, t))
                n0 = FIRST[f"down{i}"]
                with sp.Fori(0, 2 * KD // RING) as it:
                    for t in range(RING):
                        load(n0 + t, down_parts(i, n0 + t, t, it), it)

            def plain(w, n, at):
                v = kview(raw, n % RING, KD, 256)
                src = w[:, at:at + 256].rearrange("(k p) c -> p k c", p=P)
                return [(v[:, 4 * j:4 * j + 4], src[:, 4 * j:4 * j + 4]) for j in range(2)]

            def mixer(m):
                n0 = FIRST[f"in{m}"]
                for s, (_, at, _) in enumerate(IN_CHUNKS[m]):
                    load(n0 + s, plain(in_w[m], n0 + s, at))
                if m == 0:
                    n0 = FIRST["branch"]
                    for t in range(KD):
                        v = kview(raw, (n0 + t) % RING, KD, P)
                        load(n0 + t, [(v[:, 4 * j:4 * j + 4],
                                       w[0, :, t * P:(t + 1) * P].rearrange("(k p) c -> p k c", p=P))
                                      for j, w in enumerate((a["w_br_gla"], a["w_br_moba"]))])
                n0 = FIRST[f"out{m}"]
                for t in range(4):
                    load(n0 + t, plain(out_w[m], n0 + t, 256 * t))

            for dst, src in small_loads[len(small_loads) // 2:]:
                sp.dma_start(dst, src).then_inc(small, 16)
            sp.wait_ge(consts, 16)
            sp.wait_ge(small, 16 * len(small_loads))
            for k in range(KD):
                if k == KD - 2:
                    load(0, up_parts(0, 0, 0))
                parts = [slice(0, 2 * D)] if k < KD - 1 else [slice(0, D), slice(D, 2 * D)]
                for j, c in enumerate(parts):
                    sp.dma_start(ada_early[:, k, c], a["w_ada"][0, k * P:(k + 1) * P, c]
                                 ).then_inc(early_landed[k + j], 16)
            for dst, src in later_loads:
                sp.dma_start(dst, src).then_inc(later, 16)
            ffn(0)
            mixer(0)
            ffn(1)
            for layer in (1, 2):
                ffn(2 * layer)
                mixer(layer)
                ffn(2 * layer + 1)
            for tt in range(TT):
                sp.wait_ge(out_taken, 2 * (tt + 1))
                sp.dma_start(out[0, tt * P:(tt + 1) * P], u[:].rearrange("p k t -> p (k t)")[:, tt * D:(tt + 1) * D]
                             ).then_inc(stored, 16)
            sp.wait_ge(stored, 16 * TT)

        @block.gpsimd
        def _(pool):
            link = Chain(pool, pool_done)
            norms = [0]

            def ada_load(j, it=0):
                if j >= 2:
                    pool.wait_ge(ada_step, it * RING + j - 1)
                k, at = j % KD, (2 + j // KD) * D
                src = a["w_ada"][0, k * P:(k + 1) * P, at:at + D] if isinstance(it, int) else \
                    a["w_ada"][0, k * P:(k + 1) * P, bass.ds(it * (RING * D // KD) + at, D)]
                pool.dma_start(ada_raw[:, j % 2], src).then_inc(ada_landed[j % 2], 16)

            def square_tile(k, first, last):
                if first:
                    link(nc.gpsimd.tensor_tensor(sumsq[:], h[:, k], h[:, k], ALU.mult))
                    return
                link(nc.gpsimd.tensor_tensor(sq[:], h[:, k], h[:, k], ALU.mult))
                ins = nc.gpsimd.tensor_tensor(sumsq[:], sumsq[:], sq[:], ALU.add)
                if last:
                    ins.then_inc(summed, 1)
                    norms[0] += 1
                else:
                    link(ins)

            def sum_of_squares(ready, at, tiles, extra=None):
                if norms[0]:
                    pool.wait_ge(stat, norms[0])
                for k in range(KD):
                    if extra:
                        extra(k)
                    if k % tiles == 0:
                        pool.wait_ge(ready, at + k // tiles + 1)
                    square_tile(k, k == 0, k == KD - 1)

            def sums_over_units(name, tiles, extra=None):
                sum_of_squares(evacuated, 2 + UNIT[name], tiles, extra)

            def final_squares(k):
                pool.wait_ge(evacuated, 2 + UNIT["down1"] + k + 1)
                dst = sumsq_f if k == 0 else sq
                link(nc.gpsimd.tensor_scalar(sq[:], h[:, k], vec_a[:, A_FIN + k:A_FIN + k + 1], 1.0, ALU.mult, ALU.mult))
                link(nc.gpsimd.tensor_tensor(dst[:], sq[:], sq[:], ALU.mult))
                if k:
                    link(nc.gpsimd.tensor_tensor(sumsq_f, sumsq_f, sq[:], ALU.add))

            def halves(tile, s):
                v = tile.rearrange("p a (n b s) -> p (a n) b s", b=2, s=s)
                return v[:, :, 0], v[:, :, 1]

            def level_diffs(m, l):
                s = LEVELS[l]
                bl, br = halves(bcum[:], s)
                dl, dr = halves(dec[:, l % 2], s)
                if l == 0:
                    pool.wait_ge(bcum_ready, m + 1)
                elif l >= 2:
                    pool.wait_ge(xqk_ready, m * (len(LEVELS) - 1) + l - 1)
                if s == P:
                    nc.gpsimd.tensor_copy(dr, br)
                    last = bl[:, :, s - 1:s].to_broadcast([P, 2, s])
                    ins = nc.gpsimd.tensor_tensor(dl, last, bl, ALU.subtract)
                else:
                    last = bl[:, :, s - 1:s].to_broadcast([P, 2 * T // (2 * s), s])
                    nc.gpsimd.tensor_tensor(dr, br, last, ALU.subtract)
                    ins = nc.gpsimd.tensor_tensor(dl, last, bl, ALU.subtract)
                ins.then_inc(diffs, 1)

            def level_scale(m, l):
                s = LEVELS[l]
                dl, dr = halves(dec[:, l % 2], s)
                xl, xr = halves(xqk[:, l % 2], s)
                pool.wait_ge(decays, m * (len(LEVELS) - 1) + l + 1)
                if l >= 2:
                    pool.wait_ge(level_ready, m * len(LEVELS) + l - 1)
                nc.gpsimd.tensor_tensor(xl, halves(lk, s)[0], dl, ALU.mult)
                nc.gpsimd.tensor_tensor(xr, halves(lq, s)[1], dr, ALU.mult).then_inc(xqk_ready, 1)

            def conv(m):
                x_, c_, b_, y, tmp = gat[:, 4:6], gat[:, 6:8], gat[:, 12:14], u[:, 0:2], gat[:, 10:12]
                pool.wait_ge(evacuated, 2 + UNIT[f"in{m}"] + [name for name, _, _ in MIX_CHUNKS].index("g12") + 1)
                link(nc.gpsimd.tensor_tensor(x_, x_, c_, ALU.mult))

                def tap(w, hp):
                    at = B_CONV + 6 * (m - 1) + 2 * w + hp
                    return vec_b[:, at:at + 1]

                for hp in range(2):
                    link(nc.gpsimd.tensor_scalar(y[:, hp], x_[:, hp], tap(2, hp), 1.0, ALU.mult, ALU.mult))
                for w, back in ((1, 1), (0, 2)):
                    for hp in range(2):
                        link(nc.gpsimd.tensor_scalar(tmp[:, hp], x_[:, hp], tap(w, hp), 1.0, ALU.mult, ALU.mult))
                    link(nc.gpsimd.tensor_tensor(y[:, :, back:T], y[:, :, back:T], tmp[:, :, 0:T - back], ALU.add))
                nc.gpsimd.tensor_tensor(y, y, b_, ALU.mult).then_inc(conv_ready, 1)

            def mixer(m):
                if m:
                    nc.gpsimd.memset(in_turn[:], 0.0).then_inc(qz_clear, 1)
                for s in range(STEPS[m]):
                    if m == 0 and s == 2:
                        pool.wait_ge(mod_ready, 2 * (4 + 3))
                        nc.gpsimd.memset(intra[:], 0.0).then_inc(intra_clear, 1)
                    if m == 0 and s < KD - 1:
                        ada_load(5 * KD + 2 + 2 * s)
                        ada_load(5 * KD + 3 + 2 * s)
                    l = s - LIN_FIRST[m]
                    if 1 <= l < len(LEVELS):
                        level_scale(m, l - 1)
                    if 0 <= l < len(LEVELS) - 1:
                        level_diffs(m, l)
                if m:
                    conv(m)

            def affine(name, dst):
                g, b = norm_gain(name)
                i = STATS.index(name)
                for kk in range(4):
                    pool.wait_ge(scaled, 4 * i + kk + 1)
                    for k in (2 * kk, 2 * kk + 1):
                        ins = nc.gpsimd.tensor_scalar(dst[:, k], dst[:, k], g[:, k:k + 1], b[:, k:k + 1],
                                                      ALU.mult, ALU.add)
                    ins.then_inc(u_ready, 1)

            pool.dma_start(const[:], a["shape_constants"]).then_inc(consts, 16)
            sum_of_squares(x_taken, 0, 1)
            pool.wait_ge(early_step, KD - 2 - DIRECT)
            ada_load(0)
            ada_load(1)
            pool.dma_start(mask_in, a["level_masks"]).then_inc(masks_in, 16)
            pool.wait_ge(mods, 1)
            affine("up0", u)
            ada_load(2)
            ada_load(3)
            with pool.Fori(0, 4, 2) as it:
                for t in range(KD):
                    ada_load(4 + t, it)
            for t in range(2 * KD, KF):
                ada_load(4 + t)
            sums_over_units("down0", 1, lambda k: [ada_load(4 + KF + 2 * k + j) for j in range(2 if k < KD - 1 else 0)])
            for j in range(2):
                ada_load(4 + KF + 2 * KD - 2 + j)
            affine("in0", u)
            mixer(0)
            sums_over_units("out0", 2)
            affine("up1", u)
            sums_over_units("down1", 1, final_squares)
            for layer in (1, 2):
                sums_over_units(f"down{2 * layer}", 1)
                mixer(layer)
                sums_over_units(f"out{layer}", 2)
                if layer == 1:
                    sums_over_units("down3", 1)

        @block.scalar
        def _(act):
            link = Chain(act, act_done)

            def split_hi(n, it=0):
                cols = COLS[n]
                act.wait_ge(landed[n % RING], it * 32 + 32 * (n // RING + 1))
                act.wait_ge(chunk_used, it * RING + n + 1)
                nc.scalar.copy(whi[:, n % RING, 0:cols], raw[:, n % RING, 0:cols]).then_inc(hi_ready, 1)

            def split_ahead(n, it=0):
                if n + HI_LEAD < len(COLS):
                    split_hi(n + HI_LEAD, it)

            def split_u(name, ready, at):
                for kk in range(4):
                    act.wait_ge(ready, at + kk + 1)
                    nc.scalar.copy(uhi[:, 2 * kk:2 * kk + 2], u[:, 2 * kk:2 * kk + 2]).then_inc(uhi_ready, 2)

            def root_of_mean(name):
                i = STATS.index(name)
                act.wait_ge(stat, i + 1 + (i > 2))
                w = T if i < 3 else T + TT
                nc.scalar.activation(rstd[:, 0:w], ps_stat[:, 0:w], ACT.Sqrt, bias=eps[:], scale=1.0 / D).then_inc(rms, 1)

            def norm(name):
                root_of_mean(name)
                split_u(name, u_ready, 4 * STATS.index(name))

            def gained_hi(g, e, k, it=0, per=0, per_e=0):
                act.wait_ge(evacuated, it * per_e + 2 + e + 1)
                nc.scalar.activation(tiles_of(uhi, k, it, per), tiles_of(h, k, it, per), ACT.Identity,
                                     scale=column(g, k, it, per)).then_inc(uhi_ready, 1)

            def final_norms():
                act.wait_ge(stat_f, 1)
                nc.scalar.activation(rstd_f, ps_stat[:, 0:T], ACT.Sqrt, bias=eps[:], scale=1.0 / D).then_inc(rms_f, 1)
                act.wait_ge(mean_f, 1)
                nc.scalar.activation(rstd[:, 0:T], sumsq_f, ACT.Sqrt, bias=eps[:], scale=1.0 / D).then_inc(rms_f, 1)

            def ffn(i):
                n0, e0 = seg(f"up{i}")

                def step(t, it=0):
                    dst = tiles_of(hhi, t, it, RING)
                    if i < 2:
                        act.wait_ge(chunk_used, it * RING + RING + n0 + t + 1)
                        nc.scalar.activation(silu[:, t % 2], acc[(e0 + t) % 2][:, 0:T], ACT.Silu).then_inc(silu_ready, 1)
                        split_ahead(n0 + t, it)
                        act.wait_ge(evacuated, it * RING + 2 + e0 + t + 1)
                        nc.scalar.copy(dst, hid[:, t % 2]).then_inc(hhi_ready, 1)
                    else:
                        pair = gate_up[:, t % 2]
                        act.wait_ge(evacuated, it * RING + 2 + e0 + t + 1)
                        nc.scalar.activation(pair[:, 0], pair[:, 0], ACT.Silu).then_inc(silu_ready, 1)
                        split_ahead(n0 + t, it)
                        act.wait_ge(hid_ready, it * RING + KF * (i - 2) + t + 1)
                        nc.scalar.copy(dst, pair[:, 1]).then_inc(hhi_ready, 1)

                up_turns(act, i, step)
                n0, e0 = seg(f"down{i}")
                g = next_gain(f"down{i}")

                def down(t, it=0):
                    split_ahead(n0 + t, it)
                    if t % 2 and g is not None:
                        gained_hi(g, e0 + t // 2, t // 2, it, 2, 2)

                with act.Fori(0, 2 * KD // RING - 1) as it:
                    for t in range(RING):
                        down(t, it)
                for t in range(2 * KD - RING, 2 * KD):
                    down(t)

            def att_exp(m, t):
                if t is None or not 0 <= t < ATT_HEADS[m]:
                    return
                c = sum(ATT_HEADS[:m]) + t + 1
                act.wait_ge(max_ready, c)
                if c > 1:
                    act.wait_ge(prob_turned, c - 1)
                for j, (lo, hi) in enumerate(((0, P), (P, 3 * P))):
                    nc.scalar.activation(prob[:, lo:hi], score_bank(m, t)[:, lo:hi], ACT.Exp,
                                         bias=st_max[:, t % 2, 2 + j:3 + j],
                                         accum_out=st_max[:, t % 2, 4 + j:5 + j]).then_inc(exp_ready, 1)

            def lin_root(m, xs, w):
                act.wait_ge(lin_stat, m + 1)
                link(nc.scalar.activation(xs, wide[:, 0:w * T].rearrange("p (k t) -> p k t", t=T), ACT.Ln, bias=eps[:],
                                          scale=1.0 / LIN_DV[m]))
                nc.scalar.activation(xs, xs, ACT.Exp, scale=-0.5).then_inc(lin_rms, 1)

            def split_mixed_hi(m, pairs=range(4)):
                for kk in pairs:
                    if m and kk == 0:
                        act.wait_ge(conv_ready, m)
                    elif kk < 2:
                        act.wait_ge(lin_mixed, m + 1)
                    else:
                        act.wait_ge(att_taken, sum(ATT_HEADS[:m + 1]))
                    nc.scalar.copy(mix_hi[:, 2 * kk:2 * kk + 2], u[:, 2 * kk:2 * kk + 2]).then_inc(uhi_ready, 2)

            def mixer(m):
                n0, e0 = seg(f"in{m}")
                steps = STEPS[m]
                z, t_, l_ = gat[:, 8:10], gat[:, 4:6], gat[:, 6:8]
                w = LIN_DV[m] * 4 // P
                lin = u[:, LIN_AT[m]:LIN_AT[m] + w]
                xs = xqk[:].rearrange("p a b t -> p (a b) t")[:, 0:w]
                ds = dec.rearrange("p a b t -> p (a b) t")[:, 0:w]
                for s in range(steps):
                    if s == LIN_FIRST[m] - 1:
                        if m == 0:
                            act.wait_ge(z_ready, 1)
                        else:
                            act.wait_ge(evacuated, 2 + e0 + 1)
                        link(nc.scalar.activation(t_, z, ACT.Abs))
                        link(nc.scalar.activation(t_, t_, ACT.Exp, scale=-1.0))
                        if m:
                            link(nc.scalar.activation(gat[:, 12:14], z, ACT.Exp, scale=-1.0))
                        nc.scalar.activation(l_, t_, ACT.Ln, bias=1.0).then_inc(l_ready, 1)
                        if m:
                            for hp in range(2):
                                j = 2 * (m - 1) + hp
                                ins = nc.scalar.activation(gat[:, 14 + hp], gat[:, 12 + hp], ACT.Ln, bias=1.0,
                                                           scale=lb[:, j:j + 1])
                            ins.then_inc(l_ready, 1)
                            act.wait_ge(f_taken, m)
                            link(nc.scalar.activation(f8[:, 1], f8[:, 0], ACT.Abs))
                            link(nc.scalar.activation(f8[:, 1], f8[:, 1], ACT.Exp, scale=-1.0))
                            nc.scalar.activation(f8[:, 2], f8[:, 1], ACT.Ln, bias=1.0).then_inc(f_log, 1)
                    if m and s == LIN_FIRST[m]:
                        act.wait_ge(kexp_in, m)
                        nc.scalar.activation(lk, t_, ACT.Exp, scale=-1.0).then_inc(kexp_out, 1)
                    if m and s in (Q_AT + 1, K_AT + 1):
                        c = 2 * (m - 1) + (s == K_AT + 1)
                        for half_, ps in enumerate((ps_turn, ps_score)):
                            act.wait_ge(qk_summed, 2 * c + half_ + 1)
                            link(nc.scalar.activation(qk_sq[:, 2 * half_:2 * half_ + 2],
                                                      ps[:].rearrange("p (a t) -> p a t", a=2), ACT.Ln, bias=eps[:],
                                                      scale=1.0 / ATT_DH[m]))
                        nc.scalar.activation(qk_sq[:], qk_sq[:], ACT.Exp, scale=-0.5).then_inc(qk_root, 1)
                    l = s - LIN_FIRST[m]
                    if 0 <= l < len(LEVELS) - 1:
                        c = m * (len(LEVELS) - 1) + l + 1
                        act.wait_ge(diffs, c)
                        nc.scalar.activation(dec[:, l % 2], dec[:, l % 2], ACT.Exp,
                                             scale=1.0 / TAU if m == 0 else 1.0).then_inc(decays, 1)
                    for side in range(2):
                        att_exp(m, att_slot(m, s, side))
                        if side == 0 and s == LIN_OUT[m] + (m == 0):
                            act.wait_ge(lin_taken, m + 1)
                            nc.scalar.activation(xs, lin, ACT.Square).then_inc(lin_sq, 1)
                    if s < steps:
                        split_ahead(n0 + s)
                    if m == 0 and s == LIN_OUT[m] + 2:
                        nc.scalar.activation(ds, gat[:, 0:w], ACT.Sigmoid).then_inc(gate_sig, 1)
                        lin_root(m, xs, w)
                    if m == 0 and s == STEPS[m] - 2:
                        split_mixed_hi(m)
                if m == 0:
                    act.wait_ge(evacuated, 2 + e0 + steps)
                    nc.scalar.activation(gat[:, 4:20], gat[:, 4:20], ACT.Sigmoid).then_inc(gate_sig, 1)
                else:
                    split_mixed_hi(m, PAIRS[m][:2])
                    act.wait_ge(evacuated, 2 + e0 + steps)
                    nc.scalar.activation(ds, gat[:, 0:w], ACT.Sigmoid).then_inc(gate_sig, 1)
                    split_mixed_hi(m, PAIRS[m][2:3])
                    lin_root(m, xs, w)
                    split_mixed_hi(m, PAIRS[m][3:])
                if m == 0:
                    n0 = FIRST["branch"]
                    for t in range(KD):
                        split_ahead(n0 + t)
                    split_u("merged", mixed, 0)
                n0, e0 = seg(f"out{m}")
                g = next_gain(f"out{m}")
                for t in range(4):
                    split_ahead(n0 + t)
                    if g is not None:
                        for k in (2 * t, 2 * t + 1):
                            gained_hi(g, e0 + t, k)

            for dst, src in small_loads[:len(small_loads) // 2]:
                act.dma_start(dst, src).then_inc(small, 16)
            act.dma_start(u[:].rearrange("p k t -> p (k t)").rearrange("p (a d) -> p a d", a=TT),
                          a["x"][0].rearrange("(a p) d -> p a d", p=P)).then_inc(x_in, 16)
            act.wait_ge(vec_ready, 1)
            nc.scalar.activation(c_act[:], vec_a[:, A_C:A_C + 8], ACT.Silu).then_inc(c_ready, 1)
            act.wait_ge(lb_in, 1)
            nc.scalar.activation(lbt[:, 4:8], lbt[:, 0:4], ACT.Exp).then_inc(lb_exp, 1)
            root_of_mean("up0")
            act.wait_ge(early_direct, 1)
            split_hi(0)
            split_u("up0", u_ready, 0)
            act.wait_ge(early_direct, DIRECT)
            act.wait_ge(early_step, KD + 1 - DIRECT)
            for n in range(1, HI_LEAD):
                split_hi(n)
            act.wait_ge(toe_sb, 1)
            act.dma_start(scratch[:], toe_row[:]).then_inc(toe_out, 16)
            ffn(0)
            act.wait_ge(toe_out, 16)
            act.dma_start(toe[:], bass.AP(scratch, 0, [[1, P], [384, 4], [1, T]])).then_inc(toe_in, 16)
            norm("in0")
            mixer(0)
            norm("up1")
            ffn(1)
            final_norms()
            for layer in (1, 2):
                if layer > 1:
                    root_of_mean(f"up{2 * layer}")
                ffn(2 * layer)
                root_of_mean(f"in{layer}")
                mixer(layer)
                root_of_mean(f"up{2 * layer + 1}")
                ffn(2 * layer + 1)

        @block.vector
        def _(dve):
            link = Chain(dve, dve_done)

            def split_lo(n, it=0):
                cols = COLS[n]
                dve.wait_ge(hi_ready, it * RING + n + 1)
                nc.vector.tensor_tensor(wlo[:, n % RING, 0:cols], raw[:, n % RING, 0:cols],
                                        whi[:, n % RING, 0:cols].bitcast(F32), ALU.subtract).then_inc(lo_ready, 1)

            def split_ahead(n, it=0):
                if n + LO_LEAD < len(COLS):
                    split_lo(n + LO_LEAD, it)

            def split_u(name):
                q = SPLITS.index(name)
                for kk in range(4):
                    s = slice(2 * kk, 2 * kk + 2)
                    dve.wait_ge(uhi_ready, KD * q + 2 * kk + 2)
                    nc.vector.tensor_tensor(ulo[:, s], u[:, s], uhi[:, s].bitcast(F32), ALU.subtract
                                            ).then_inc(ulo_ready, 2)

            def gained_lo(q, g, k, it=0, per=0):
                dve.wait_ge(uhi_ready, it * per + KD * q + k + 1)
                nc.vector.scalar_tensor_tensor(out=tiles_of(ulo, k, it, per), in0=tiles_of(h, k, it, per),
                                               scalar=column(g, k, it, per),
                                               in1=tiles_of(uhi, k, it, per).bitcast(F32),
                                               op0=ALU.mult, op1=ALU.subtract).then_inc(ulo_ready, 1)

            def scale_u(name):
                dve.wait_ge(rms, STATS.index(name) + 1)
                link(nc.vector.reciprocal(rstd[:, 0:T], rstd[:, 0:T]))
                for kk in range(4):
                    s = slice(2 * kk, 2 * kk + 2)
                    nc.vector.tensor_tensor(u[:, s], h[:, s], by_token(2), ALU.mult).then_inc(scaled, 1)

            def norm(name):
                scale_u(name)
                split_u(name)

            def by_token(n):
                return rstd[:, 0:T].unsqueeze(1).to_broadcast([P, n, T])

            def scale_of(name):
                dve.wait_ge(rms, STATS.index(name) + 1)
                link(nc.vector.reciprocal(rstd[:], rstd[:]))

            def final_norms():
                dve.wait_ge(rms_f, 1)
                link(nc.vector.reciprocal(rstd_f, rstd_f))
                link(nc.vector.tensor_tensor(sumsq_f, ps_stat[:, T:2 * T], rstd_f, ALU.mult))
                nc.vector.tensor_tensor(sumsq_f, sumsq_f, rstd_f, ALU.mult).then_inc(mean_f, 1)
                dve.wait_ge(rms_f, 2)
                link(nc.vector.reciprocal(rstd[:, 0:T], rstd[:, 0:T]))
                link(nc.vector.tensor_tensor(rstd[:, 0:T], rstd[:, 0:T], rstd_f, ALU.mult))

            def final_residual():
                for k in range(KD):
                    ins = nc.vector.scalar_tensor_tensor(out=h[:, k], in0=h[:, k], scalar=vec_a[:, A_FIN + k:A_FIN + k + 1],
                                                         in1=rstd_f, op0=ALU.mult, op1=ALU.mult)
                link(ins)

            def early_sum_step(k, half_=None):
                c = slice(0, 2 * D) if half_ is None else slice(half_ * D, (half_ + 1) * D)
                dve.wait_ge(early_landed[k + (half_ or 0)], 16)
                if k == DIRECT:
                    ins = nc.vector.tensor_scalar(early_sum[:, c], ada_early[:, k, c], c_act[:, k:k + 1], None, ALU.mult)
                else:
                    dve.wait_ge(early_step, k - DIRECT)
                    ins = nc.vector.scalar_tensor_tensor(out=early_sum[:, c], in0=ada_early[:, k, c],
                                                         scalar=c_act[:, k:k + 1], in1=early_sum[:, c],
                                                         op0=ALU.mult, op1=ALU.add)
                ins.then_inc(early_step, 1)

            def ada_sum(j, it=0):
                k, g = j % KD, j // KD
                dst, w = piece_sums[g], ada_raw[:, j % 2]
                dve.wait_ge(ada_landed[j % 2], it * (16 * RING // 2) + 16 * (j // 2 + 1))
                if k == 0:
                    if g:
                        group_take(g - 1, it)
                    ins = nc.vector.tensor_scalar(dst, w, c_act[:, k:k + 1], None, ALU.mult)
                else:
                    dve.wait_ge(ada_step, it * RING + j)
                    ins = nc.vector.scalar_tensor_tensor(out=dst, in0=w, scalar=c_act[:, k:k + 1], in1=dst,
                                                         op0=ALU.mult, op1=ALU.add)
                ins.then_inc(ada_step, 1)

            def group_take(g, it=0):
                lo = (2 + g) * KD
                if isinstance(it, int):
                    dst, bias = mod[:, lo:lo + KD], vec_a[:, A_ADA + lo:A_ADA + lo + KD]
                else:
                    dst = mod[:, bass.ds(it * RING + lo, KD)]
                    bias = vec_a[:, bass.ds(it * RING + A_ADA + lo, KD)]
                dve.wait_ge(mod_ready, it + 2 * (g + 3))
                nc.vector.tensor_tensor(dst, ps_mod[:, 0:KD], bias, ALU.add).then_inc(mod_taken, 1)

            def gain_make(j, at):
                link(nc.vector.tensor_scalar(gain[:, j], mod[:, (3 * j + 1) * KD:(3 * j + 2) * KD], 1.0, None, ALU.add))
                nc.vector.tensor_tensor(gain[:, j], gain[:, j], vec_a[:, at:at + 8], ALU.mult).then_inc(mods, 1)

            def ffn(i):
                n0, e0 = seg(f"up{i}")

                def step(t, it=0):
                    g = it * RING + KF * i + t + 1
                    ps = acc[(e0 + t) % 2]
                    if i < 2:
                        dve.wait_ge(silu_ready, g)
                        nc.vector.tensor_tensor(hid[:, t % 2], silu[:, t % 2], ps[:, T:2 * T], ALU.mult
                                                ).then_inc(evacuated, 1)
                        split_ahead(n0 + t, it)
                        if i == 0:
                            ada_sum(2 + t, it)
                    else:
                        pair = gate_up[:, t % 2]
                        dve.wait_ge(chunk_used, it * RING + RING + n0 + t + 1)
                        nc.vector.tensor_tensor(pair, ps[:].rearrange("p (a t) -> p a t", a=2), by_token(2), ALU.mult
                                                ).then_inc(evacuated, 1)
                        split_ahead(n0 + t, it)
                        dve.wait_ge(silu_ready, g)
                        nc.vector.tensor_tensor(pair[:, 1], pair[:, 0], pair[:, 1], ALU.mult).then_inc(hid_ready, 1)
                    dve.wait_ge(hhi_ready, g)
                    src = hid[:, t % 2] if i < 2 else gate_up[:, t % 2, 1]
                    nc.vector.tensor_tensor(tiles_of(hlo, t, it, RING), src, tiles_of(hhi, t, it, RING).bitcast(F32),
                                            ALU.subtract).then_inc(hlo_ready, 1)

                up_turns(dve, i, step)
                if i == 0:
                    dve.wait_ge(mod_taken, 1)
                    link(nc.vector.tensor_scalar(half[:, 0:8], mod[:, 2 * KD:3 * KD], 0.5, None, ALU.mult))
                n0, e0 = seg(f"down{i}")
                g = residual_gate(i)
                after = next_gain(f"down{i}")
                if i == 2:
                    final_residual()

                def down(t, it=0):
                    if t % 2 == 0:
                        split_ahead(n0 + t, it)
                        if i == 0:
                            ada_sum(2 + KF + t, it)
                    else:
                        m = t // 2
                        dve.wait_ge(chunk_used, it * RING + RING + n0 + t + 1)
                        gm, hm = column(g, m, it, 2), tiles_of(h, m, it, 2)
                        nc.vector.scalar_tensor_tensor(out=hm, in0=acc[(e0 + m) % 2][:, 0:T], scalar=gm, in1=hm,
                                                       op0=ALU.mult, op1=ALU.add).then_inc(evacuated, 1)
                        if after is not None:
                            gained_lo(SPLITS.index(FOLLOWS[f"down{i}"]), after, m, it, 2)
                        split_ahead(n0 + t, it)
                        if i == 0:
                            ada_sum(2 + KF + t, it)

                turns = 2 * KD // RING - 1 if i else 0
                if turns:
                    with dve.Fori(0, turns) as it:
                        for t in range(RING):
                            down(t, it)
                for t in range(turns * RING, 2 * KD):
                    down(t)

            def log_gates(m):
                z, l_, la, t_ = gat[:, 8:10], gat[:, 6:8], gat[:, 10:12], gat[:, 4:6]
                dve.wait_ge(l_ready, [1, 3, 5][m])
                link(nc.vector.tensor_scalar(la, z, 0.0, None, ALU.min))
                link(nc.vector.tensor_tensor(la, la, l_, ALU.subtract))
                if m:
                    link(nc.vector.tensor_tensor(la, la, gat[:, 14:16], ALU.add))
                    link(nc.vector.tensor_scalar(t_, z, 0.0, None, ALU.max))
                    nc.vector.tensor_tensor(t_, t_, l_, ALU.add).then_inc(kexp_in, 1)
                for hp in range(2):
                    for tt in range(TT):
                        v = la[:, hp, tt * P:(tt + 1) * P]
                        link(nc.vector.tensor_tensor_scan(bcum[:, hp, tt * P:(tt + 1) * P], v, v, 0.0,
                                                          ALU.add, ALU.bypass))
                if m:
                    dve.wait_ge(kexp_out, m)
                    for hp in range(2):
                        j = 2 * (m - 1) + hp
                        link(nc.vector.tensor_scalar(lk[:, hp], lk[:, hp], lb[:, 4 + j:5 + j], None, ALU.mult))
                    dve.wait_ge(f_log, m)
                    link(nc.vector.tensor_scalar(f8[:, 0], f8[:, 0], 0.0, None, ALU.min))
                    link(nc.vector.tensor_tensor(f8[:, 0], f8[:, 2], f8[:, 0], ALU.subtract))
                    nc.vector.tensor_tensor_scan(negc[:], f8[:, 0], f8[:, 0], 0.0, ALU.add, ALU.bypass
                                                 ).then_inc(negc_ready, 1)
                    dve.wait_ge(negc_ready, m)
                nc.vector.tensor_copy(st_max[:, 0, 0:1], bcum[:, 0, 0:1]).then_inc(bcum_ready, 1)

            def level_take(m, l):
                dve.wait_ge(level_ready, m * len(LEVELS) + l + 1)
                if m == 0 and l == 1:
                    dve.wait_ge(intra_clear, 1)
                if l == 0:
                    ins = nc.vector.tensor_copy(cross[:], wide[:].rearrange("p (a b c) -> p a b c", b=2, c=P)[:, :, 0])
                else:
                    ins = nc.vector.copy_predicated(intra[:], level_mask[:, l - 1].unsqueeze(1).to_broadcast([P, 8, P]),
                                                    wide[:].rearrange("p (a c) -> p a c", c=P))
                ins.then_inc(level_taken, 1)

            def softmax(m, t):
                c = sum(ATT_HEADS[:m]) + t
                st = st_max[:, t % 2]
                ps = score_bank(m, t)
                dve.wait_ge(scores_ready, c + 1)
                nc.vector.reduce_max(st[:, 0:1], ps[:, 0:P], AX_X)
                link(nc.vector.reduce_max(st[:, 1:2], ps[:, P:3 * P], AX_X))
                nc.vector.tensor_scalar(st[:, 2:4], st[:, 0:2], -1.0, None, ALU.mult).then_inc(max_ready, 1)
                dve.wait_ge(exp_ready, 2 * c + 2)
                link(nc.vector.reciprocal(st[:, 6:8], st[:, 4:6]))
                nc.vector.tensor_scalar(prob[:, 0:P], prob[:, 0:P], st[:, 6:7], None, ALU.mult)
                nc.vector.tensor_scalar(prob[:, P:3 * P], prob[:, P:3 * P], st[:, 7:8], None, ALU.mult
                                        ).then_inc(prob_ready, 1)

            def prob_take(m, t):
                c = sum(ATT_HEADS[:m]) + t
                dve.wait_ge(prob_turned, c + 1)
                nc.vector.tensor_copy(prob_t[:], ps_turn[:, 0:3 * P]).then_inc(prob_t_ready, 1)

            def att_take(m, t):
                c = sum(ATT_HEADS[:m]) + t
                dve.wait_ge(att_ready, c + 1)
                if m == 0:
                    ins = nc.vector.tensor_copy(u[:, 4 + t], ps_stat[:, T:2 * T])
                else:
                    q = slice(64 * (t % 2), 64 * (t % 2) + 64)
                    ins = nc.vector.tensor_copy(u[q, 4 + t // 2], ps_stat[q, T:2 * T])
                ins.then_inc(att_taken, 1)

            def qk_square(m, tile):
                nc.vector.tensor_tensor(qk_sq[:, 0:2], tile[:, 0:2], tile[:, 0:2], ALU.mult).then_inc(qk_squared, 1)
                nc.vector.tensor_tensor(qk_sq[:, 2:4], tile[:, 2:4], tile[:, 2:4], ALU.mult).then_inc(qk_squared, 1)

            def qk_norm(m, j):
                dve.wait_ge(qk_root, 2 * (m - 1) + j + 1)
                at = (A_FQ if j == 0 else A_FK) + m - 1
                if j:
                    nc.vector.scalar_tensor_tensor(out=ak[:], in0=ak[:], scalar=vec_a[:, at:at + 1], in1=qk_sq[:],
                                                   op0=ALU.mult, op1=ALU.mult).then_inc(qk_normed, 1)
                    return
                dve.wait_ge(qz_clear, m)
                by_head = qz.rearrange("p (a b) t -> p a b t", b=2)
                for b in range(2):
                    r = slice(64 * b, 64 * b + 64)
                    ins = nc.vector.scalar_tensor_tensor(out=by_head[r, :, b], in0=aq[r], scalar=vec_a[r, at:at + 1],
                                                         in1=qk_sq[r], op0=ALU.mult, op1=ALU.mult)
                    link(ins)

            def take(m, s):
                n0, e0 = seg(f"in{m}")
                name, _, kind = IN_CHUNKS[m][s]
                ps = acc[(e0 + s) % 2][:].rearrange("p (a t) -> p a t", a=2)
                dve.wait_ge(chunk_used, RING + n0 + s + 1)
                v = nc.vector
                if name == "lq":
                    dst = lq
                elif name == "lk":
                    dst = lk
                elif name[:2] in ("lv", "av"):
                    c = 256 * int(name[2])
                    dst = (lv if name[0] == "l" else av)[:, :, c:c + 256]
                elif name[:2] in ("aq", "ak"):
                    c = 2 * int(name[2])
                    dst = (aq if name[1] == "q" else ak)[:, c:c + 2]
                else:
                    c = int(name[1:])
                    dst = gat[:, c:c + 2]
                if m == 0:
                    factor = {"lq": 64 ** -0.5, "aq": ATT_DH[0] ** -0.5}.get(name[:2], 1.0)
                    ins = v.tensor_scalar(dst, ps, factor, None, ALU.mult)
                elif kind == "f":
                    ins = v.tensor_tensor(dst, ps, by_token(2), ALU.mult)
                else:
                    for tt in range(TT):
                        ins = v.tensor_scalar(dst[:, tt], ps[:, tt], rstd[:, T + tt:T + tt + 1], None, ALU.mult)
                ins.then_inc(evacuated, 1)

            def att_phase(m, t):
                if t is None:
                    return
                if 3 <= t < ATT_HEADS[m] + 3:
                    att_take(m, t - 3)
                if 2 <= t < ATT_HEADS[m] + 2:
                    prob_take(m, t - 2)
                if 0 <= t < ATT_HEADS[m]:
                    softmax(m, t)

            def lin_gate(m, lin, xs, ds):
                at = A_GLAN if m == 0 else A_HG + m - 1
                dve.wait_ge(gate_sig, [1, 3, 4][m])
                link(nc.vector.tensor_tensor(ds, ds, gat[:, 0:LIN_DV[m] * 4 // P], ALU.mult))
                dve.wait_ge(lin_rms, m + 1)
                link(nc.vector.scalar_tensor_tensor(out=lin, in0=lin, scalar=vec_a[:, at:at + 1], in1=xs,
                                                    op0=ALU.mult, op1=ALU.mult))
                nc.vector.tensor_tensor(lin, lin, ds, ALU.mult).then_inc(lin_mixed, 1)

            def split_mixed_lo(m, pairs):
                q = SPLITS.index("branch" if m == 0 else f"out{m}")
                for kk in pairs:
                    c = slice(2 * kk, 2 * kk + 2)
                    dve.wait_ge(uhi_ready, KD * q + 2 * PAIRS[m].index(kk) + 2)
                    nc.vector.tensor_tensor(mix_lo[:, c], u[:, c], mix_hi[:, c].bitcast(F32), ALU.subtract
                                            ).then_inc(ulo_ready, 2)

            def mixer(m):
                n0, e0 = seg(f"in{m}")
                w = LIN_DV[m] * 4 // P
                lin = u[:, LIN_AT[m]:LIN_AT[m] + w]
                xs = xqk[:].rearrange("p a b t -> p (a b) t")[:, 0:w]
                ds = dec.rearrange("p a b t -> p (a b) t")[:, 0:w]
                for s in range(STEPS[m]):
                    if m == 0 and s < KD:
                        ada_sum(5 * KD + 2 * s)
                        ada_sum(5 * KD + 2 * s + 1)
                    if m == 0 and s == 0:
                        dve.wait_ge(pe_glr, 1)
                        nc.vector.tensor_copy(glr, ps_stat[0:GLR_N, T:2 * T]).then_inc(dve_glr, 1)
                    if m and s == 0:
                        dve.wait_ge(f_ready, m)
                        link(nc.vector.tensor_tensor(f8[:, 0], ps_score[0:8, 0:T], rstd[0:8, 0:T], ALU.mult))
                        nc.vector.tensor_scalar(f8[:, 0], f8[:, 0], fbias[:, m - 1:m], None, ALU.add
                                                ).then_inc(f_taken, 1)
                    if m == 0 and s == 1:
                        dve.wait_ge(pe_z, 1)
                        for hp in range(2):
                            ins = nc.vector.tensor_scalar(gat[:, 8 + hp], wide[:, hp * T:(hp + 1) * T],
                                                          vec_a[:, A_BGL + hp:A_BGL + hp + 1], None, ALU.add)
                        ins.then_inc(z_ready, 1)
                    if s == LIN_FIRST[m]:
                        log_gates(m)
                    if m and s in (Q_AT, K_AT):
                        dve.wait_ge(evacuated, 2 + e0 + s)
                        qk_square(m, aq if s == Q_AT else ak)
                    if m and s in (Q_AT + 1, K_AT + 1):
                        qk_norm(m, s == K_AT + 1)
                    for side in range(2):
                        att_phase(m, att_slot(m, s, side))
                        if side == 0 and s == LIN_OUT[m] + (m == 0):
                            dve.wait_ge(lin_ready, m + 1)
                            nc.vector.tensor_copy(lin, wide[:, 0:w * T].rearrange("p (k t) -> p k t", t=T)
                                                  ).then_inc(lin_taken, 1)
                    take(m, s)
                    l = s - LIN_FIRST[m] - 1
                    if 0 <= l < len(LEVELS):
                        level_take(m, l)
                    split_ahead(n0 + s)
                    if m == 0 and s == LIN_OUT[m] + 2:
                        lin_gate(m, lin, xs, ds)
                    if m == 0 and s == STEPS[m] - 2:
                        split_mixed_lo(m, range(4))
                if m:
                    split_mixed_lo(m, PAIRS[m][:3])
                    lin_gate(m, lin, xs, ds)
                    split_mixed_lo(m, PAIRS[m][3:])
                if m == 0:
                    n0, e0 = seg("branch")
                    dve.wait_ge(gate_sig, 2)
                    for t in range(KD):
                        split_ahead(n0 + t)
                        ps = acc[(e0 + t) % 2]
                        dve.wait_ge(chunk_used, RING + n0 + t + 1)
                        nc.vector.tensor_tensor(u[:, t], ps[:, 0:T], gat[:, 4 + t], ALU.mult)
                        ins = nc.vector.tensor_tensor(silu[:, t % 2], ps[:, T:2 * T], gat[:, 12 + t], ALU.mult)
                        ins.then_inc(evacuated, 1)
                        dve.wait_ge(evacuated, 2 + e0 + t + 1)
                        ins = nc.vector.tensor_tensor(u[:, t], u[:, t], silu[:, t % 2], ALU.add)
                        if t % 2:
                            ins.then_inc(mixed, 1)
                    split_u("out0")
                n0, e0 = seg(f"out{m}")
                if m == 0:
                    group_take(GROUPS - 1)
                    dve.wait_ge(mod_taken, GROUPS)
                    gain_make(2, A_FF2)
                    link(nc.vector.tensor_scalar(half[:, 8:16], mod[:, 8 * KD:9 * KD], 0.5, None, ALU.mult))
                for t in range(4):
                    split_ahead(n0 + t)
                    dve.wait_ge(chunk_used, RING + n0 + t + 1)
                    ps = acc[(e0 + t) % 2]
                    if m == 0:
                        for j in range(2):
                            g = mod[:, 5 * KD + 2 * t + j:5 * KD + 2 * t + j + 1]
                            ins = nc.vector.scalar_tensor_tensor(out=h[:, 2 * t + j], in0=ps[:, j * T:(j + 1) * T],
                                                                 scalar=g, in1=h[:, 2 * t + j],
                                                                 op0=ALU.mult, op1=ALU.add)
                    else:
                        ins = nc.vector.tensor_tensor(h[:, 2 * t:2 * t + 2], ps[:].rearrange("p (a t) -> p a t", a=2),
                                                      h[:, 2 * t:2 * t + 2], ALU.add)
                    ins.then_inc(evacuated, 1)
                    if m:
                        for k in (2 * t, 2 * t + 1):
                            gained_lo(SPLITS.index(FOLLOWS[f"out{m}"]), next_gain(f"out{m}"), k)

            dve.sem_inc(lo_ready, RING)
            dve.sem_inc(evacuated, 2)
            for tile, value in ((ones, 1.0), (eps, EPS), (zero8, 0.0), (half8, 0.5)):
                nc.vector.memset(tile[:], value).then_inc(set_up, 1)
            dve.wait_ge(turned_a, 1)
            nc.vector.tensor_copy(vec_a[:, 0:A_ROWS], ps_score[:, 0:A_ROWS])
            ins = nc.vector.tensor_copy(vec_b[:, 0:B_ROWS], ps_score[:, P:P + B_ROWS])
            ins.then_inc(vec_ready, 1)
            dve.wait_ge(vec_ready, 1)
            link(nc.vector.tensor_scalar(vec_a[:, A_FQ:A_FQ + 2], vec_a[:, A_FQ:A_FQ + 2], ATT_DH[1] ** -0.5, None,
                                         ALU.mult))
            for k in range(KD):
                dve.wait_ge(x_turned, k + 1)
                nc.vector.tensor_copy(h[:, k], wide[:, k % 2 * 512:k % 2 * 512 + T]).then_inc(x_taken, 1)
            l0, l1 = vec_b[:, B_LB:B_LB + 2], vec_b[:, B_LB + 2:B_LB + 4]
            link(nc.vector.tensor_tensor(lbt[:, 8:10], l0, l1, ALU.max))
            link(nc.vector.tensor_tensor(lbt[:, 0:2], l0, lbt[:, 8:10], ALU.subtract))
            nc.vector.tensor_tensor(lbt[:, 2:4], l1, lbt[:, 8:10], ALU.subtract).then_inc(lb_in, 1)
            dve.wait_ge(lb_exp, 1)
            link(nc.vector.tensor_tensor(lbt[:, 8:10], lbt[:, 4:6], lbt[:, 6:8], ALU.add))
            link(nc.vector.reciprocal(lbt[:, 10:12], lbt[:, 8:10]))
            link(nc.vector.tensor_tensor(lbt[:, 0:2], lbt[:, 4:6], lbt[:, 10:12], ALU.mult))
            link(nc.vector.tensor_tensor(lbt[:, 2:4], lbt[:, 6:8], lbt[:, 10:12], ALU.mult))
            link(nc.vector.tensor_tensor(lb[:, 0:2], lbt[:, 0:2], lbt[:, 0:2], ALU.subtract))
            link(nc.vector.tensor_tensor(lb[:, 2:4], lbt[:, 0:2], lbt[:, 2:4], ALU.add))
            link(nc.vector.tensor_tensor(lb[:, 2:4], lb[:, 2:4], lbt[:, 0:2], ALU.subtract))
            link(nc.vector.tensor_scalar(lb[:, 0:4], lb[:, 0:4], 0.0, 1.0, ALU.max, ALU.min))
            link(nc.vector.tensor_scalar(lb[:, 4:8], lb[:, 0:4], -1.0, 1.0, ALU.mult, ALU.add))
            link(nc.vector.tensor_tensor(gain_f[:], vec_a[:, A_FIN:A_FIN + 8], vec_b[:, B_FF1:B_FF1 + 8], ALU.mult))
            dve.wait_ge(c_ready, 1)
            for k in range(DIRECT, KD - 3):
                early_sum_step(k)
            scale_u("up0")
            for k in range(KD - 3, KD - 1):
                early_sum_step(k)
            early_sum_step(KD - 1, 0)
            early_sum_step(KD - 1, 1)
            split_lo(0)
            dve.wait_ge(mod_ready, 4)
            link(nc.vector.tensor_tensor(mod[:, 0:2 * KD], ps_mod[:, 0:2 * KD], vec_a[:, A_ADA:A_ADA + 2 * KD], ALU.add))
            gain_make(0, A_FF1)
            split_u("up0")
            split_lo(1)
            ada_sum(0)
            ada_sum(1)
            dve.wait_ge(masks_in, 16)
            nc.vector.tensor_copy(level_mask[:].rearrange("p n c -> p (n c)"), mask_in)
            dve.wait_ge(toe_psum, 1)
            nc.vector.tensor_tensor(toe_row[:], ps_turn[0:4, 0:384], prob_t[0:4, :], ALU.add
                                    ).then_inc(toe_sb, 1)
            dve.wait_ge(later, 16 * len(later_loads))
            for l in range(2):
                g = vec_b[:, B_MIX + 8 * l:B_MIX + 8 * l + 8].unsqueeze(2).to_broadcast([P, KD, FF_N])
                nc.vector.tensor_tensor(wff[:, l], wff[:, l], g, ALU.mult).then_inc(wff_ready, 1)
            ffn(0)
            dve.wait_ge(mod_taken, 3)
            gain_make(1, A_MIX)
            dve.wait_ge(mods, 2)
            norm("in0")
            mixer(0)
            dve.wait_ge(mods, 3)
            norm("up1")
            ffn(1)
            final_norms()
            for layer in (1, 2):
                if layer > 1:
                    scale_of(f"up{2 * layer}")
                ffn(2 * layer)
                scale_of(f"in{layer}")
                mixer(layer)
                scale_of(f"up{2 * layer + 1}")
                ffn(2 * layer + 1)
            for c in range(TT * KD // 4):
                dve.wait_ge(out_turned, c + 1)
                nc.vector.tensor_copy(u[:].rearrange("p k t -> p (k t)")[:, c * 512:(c + 1) * 512],
                                      wide[:, c % 2 * 512:(c % 2 + 1) * 512]).then_inc(out_taken, 1)

        @block.tensor
        def _(pe):
            mm = nc.tensor.matmul

            def three(dst, wh, wl, xh, xl, first, last):
                mm(dst, wh, xh, start=first, stop=False)
                mm(dst, wh, xl, start=False, stop=False)
                return mm(dst, wl, xh, start=False, stop=last)

            def chunk_in(n, it=0):
                pe.wait_ge(lo_ready, it * RING + RING + n + 1)

            def bank_free(e, it=0, per=1):
                pe.wait_ge(evacuated, it * per + e + 1)

            def feature_tiles(n, dst, tiles, width, kt, waits=None):
                vh, vl = kview(whi, n % RING, KD, width), kview(wlo, n % RING, KD, width)
                for j in tiles:
                    c = slice(j * P, (j + 1) * P)
                    for k in range(kt):
                        if waits is not None and j == 0 and k % 2 == 0:
                            pe.wait_ge(ulo_ready, waits + k + 2)
                        ins = three(dst[:, j * T:(j + 1) * T], vh[:, k, c], vl[:, k, c], uhi[:, k], ulo[:, k],
                                    k == 0, k == kt - 1)
                return ins

            def token_tiles(n, dst, tiles):
                vh, vl = kview(whi, n % RING, KD, 256), kview(wlo, n % RING, KD, 256)
                for tt in tiles:
                    c = slice(tt * P, (tt + 1) * P)
                    for k in range(KD):
                        d = dst[:, tt * 256:(tt + 1) * 256]
                        mm(d, uhi[:, k, c], vh[:, k], start=k == 0, stop=False)
                        mm(d, uhi[:, k, c], vl[:, k], start=False, stop=False)
                        ins = mm(d, ulo[:, k, c], vh[:, k], start=False, stop=k == KD - 1)
                return ins

            def mod_vector(sums):
                for j in range(KD):
                    ins = mm(ps_mod[:, j:j + 1], sums[:, j * P:(j + 1) * P], ones[:, 0:1], start=True, stop=True)
                ins.then_inc(mod_ready, 2)

            def early_tile(k):
                pe.wait_ge(early_landed[k], 16)
                for j in range(2 * KD):
                    ins = mm(ps_mod[:, j:j + 1], ada_early[:, k, j * P:(j + 1) * P], c_act[:, k:k + 1],
                             start=k == 0 and j == 0, stop=False)
                ins.then_inc(early_direct, 1)

            def group_sum(g, it=0):
                pe.wait_ge(ada_step, it * RING + (g + 1) * KD)
                mod_vector(piece_sums[g])

            def norm(name):
                i = STATS.index(name)
                pe.wait_ge(summed, i + 1 + (i > 2))
                ins = mm(ps_stat[:, 0:T], ones[:], sumsq[:], start=True, stop=True)
                if i > 2:
                    for tt in range(TT):
                        ins = mm(ps_stat[:, T + tt:T + tt + 1], sumsq[:, tt * P:(tt + 1) * P], ones[:, 0:1],
                                 start=True, stop=True)
                ins.then_inc(stat, 1)

            def final_norms():
                pe.wait_ge(summed, 4)
                mm(ps_stat[:, 0:T], ones[:], sumsq[:], start=True, stop=True).then_inc(stat, 1)
                mm(ps_stat[:, T:2 * T], ones[:], sumsq_f, start=True, stop=True).then_inc(stat_f, 1)

            def ffn(i, stats=None):
                n0, e0 = seg(f"up{i}")
                waits = KD * SPLITS.index(f"up{i}")

                def step(t, it=0):
                    if i == 0 and t % KD == KD - 1:
                        group_sum(t // KD, it)
                    chunk_in(n0 + t, it)
                    bank_free(e0 + t, it, RING)
                    feature_tiles(n0 + t, acc[(e0 + t) % 2], range(2), 2 * P, KD, waits if t == 0 else None
                                  ).then_inc(chunk_used, 1)

                up_turns(pe, i, step, stats)
                n0, e0 = seg(f"down{i}")
                wide_ = 2 if i == 0 else 1
                with pe.Fori(0, 2 * KD // RING, wide_) as it:
                    for t in range(wide_ * RING):
                        if i == 0 and t == 1:
                            group_sum(2, it)
                        m, side = t // 2, t % 2
                        chunk_in(n0 + t, it)
                        if side == 0:
                            bank_free(e0 + m, it, 2)
                        if t < 2:
                            pe.wait_ge(hlo_ready, KF * i + KF // 2 * (side + 1))
                        vh = kview(whi, (n0 + t) % RING, KF // 2, P)
                        vl = kview(wlo, (n0 + t) % RING, KF // 2, P)
                        for k in range(KF // 2):
                            kk = side * (KF // 2) + k
                            ins = three(acc[(e0 + m) % 2][:, 0:T], vh[:, k], vl[:, k], hhi[:, kk], hlo[:, kk],
                                        kk == 0, kk == KF - 1)
                        ins.then_inc(chunk_used, 1)

            def level_column(hd, tt):
                return (4 * (hd % 2) + 2 * (hd // 2) + tt) * P

            def level_scores(m, l):
                s = LEVELS[l]
                c = m * len(LEVELS) + l
                if c:
                    pe.wait_ge(level_taken, c)
                if s:
                    pe.wait_ge(xqk_ready, m * (len(LEVELS) - 1) + l + 1)
                for hd in range(4):
                    r, hp = slice(64 * (hd % 2), 64 * (hd % 2) + 64), hd // 2
                    key = xqk[:, l % 2] if s else lk
                    query = xqk[:, l % 2] if s else lq
                    if l == 0:
                        j = level_column(hd, 0)
                        ins = mm(wide[:, j:j + P], key[r, hp, 0:P], query[r, hp, P:T], start=True, stop=True)
                    else:
                        for tt in range(TT):
                            c = slice(tt * P, (tt + 1) * P)
                            j = level_column(hd, tt)
                            ins = mm(wide[:, j:j + P], key[r, hp, c], query[r, hp, c], start=True, stop=True)
                ins.then_inc(level_ready, 1)

            def lin_out(m):
                dv = LIN_DV[m]
                pe.wait_ge(level_taken, (m + 1) * len(LEVELS))
                for hd in range(4):
                    vals = [lv[:, tt, hd * dv:(hd + 1) * dv] for tt in range(TT)]
                    if m == 0:
                        dst = wide[:, hd * T:(hd + 1) * T]
                    else:
                        dst = wide[64 * (hd % 2):64 * (hd % 2) + 64, hd // 2 * T:(hd // 2 + 1) * T]
                    j = level_column(hd, 0) // P
                    mm(dst[:, 0:P], vals[0], intra[:, j], start=True, stop=True)
                    mm(dst[:, P:T], vals[0], cross[:, j // 2], start=True, stop=False)
                    ins = mm(dst[:, P:T], vals[1], intra[:, j + 1], start=False, stop=True)
                ins.then_inc(lin_ready, 1)

            def lin_norm(m):
                pe.wait_ge(lin_sq, m + 1)
                w = LIN_DV[m] * 4 // P
                xs = xqk[:].rearrange("p a b t -> p (a b t)")
                for j in range(w // 2):
                    ins = mm(wide[:, j * 512:(j + 1) * 512], ones[:] if m == 0 else same_head,
                             xs[:, j * 512:(j + 1) * 512], start=True, stop=True)
                ins.then_inc(lin_stat, 1)

            def att_scores(m, t):
                c = sum(ATT_HEADS[:m]) + t
                if c:
                    pe.wait_ge(exp_ready, 2 * c if t == 0 or m == 0 else 2 * c - 2)
                if m == 0:
                    q, k = aq[:, t], ak[:, t]
                else:
                    q, k = qz[:, t], ak[:, t // 2]
                ps = score_bank(m, t)
                if m == 0 and t == 0:
                    pe.wait_ge(toe_in, 16)
                if m and t == 0:
                    pe.wait_ge(qk_normed, m)
                    pe.wait_ge(negc_ready, m)
                for dst, qs, n in ((ps[:, 0:P], slice(0, P), P), (ps[:, P:3 * P], slice(P, T), T)):
                    mm(dst, q[:, qs], k[:, 0:n], start=True, stop=False)
                    if m == 0:
                        ins = mm(dst, anti, toe[:, t, T - n:T], start=False, stop=True)
                    else:
                        mm(dst, pick(t), negc[:, 0:n], start=False, stop=False)
                        ins = mm(dst[:, n - P:n], ident, causal, start=False, stop=True)
                ins.then_inc(scores_ready, 1)

            def att_turn(m, t):
                c = sum(ATT_HEADS[:m]) + t
                pe.wait_ge(prob_ready, c + 1)
                if c:
                    pe.wait_ge(prob_t_ready, c)
                for j in range(3):
                    ins = nc.tensor.transpose(ps_turn[:, j * P:(j + 1) * P], prob[:, j * P:(j + 1) * P], ident)
                ins.then_inc(prob_turned, 1)

            def att_out(m, t):
                c = sum(ATT_HEADS[:m]) + t
                dh = ATT_DH[m]
                pe.wait_ge(prob_t_ready, c + 1)
                if c:
                    pe.wait_ge(att_taken, c)
                vals = [av[:, tt, t * dh:(t + 1) * dh] for tt in range(TT)]
                r = slice(0, P) if m == 0 else slice(64 * (t % 2), 64 * (t % 2) + 64)
                dst = ps_stat[r, T:2 * T]
                mm(dst[:, 0:P], vals[0], prob_t[:, 0:P], start=True, stop=True)
                mm(dst[:, P:T], vals[0], prob_t[:, P:2 * P], start=True, stop=False)
                mm(dst[:, P:T], vals[1], prob_t[:, 2 * P:3 * P], start=False, stop=True).then_inc(att_ready, 1)

            def att_phase(m, t):
                if t is None:
                    return
                if 0 <= t < ATT_HEADS[m]:
                    att_scores(m, t)
                if 1 <= t < ATT_HEADS[m] + 1:
                    att_turn(m, t - 1)
                if 2 <= t < ATT_HEADS[m] + 2:
                    att_out(m, t - 2)

            def qk_stat(m, j):
                c = 2 * (m - 1) + j
                for half_, ps in enumerate((ps_turn, ps_score)):
                    pe.wait_ge(qk_squared, 2 * c + half_ + 1)
                    mm(ps[:], same_head, qk_sq[:].rearrange("p k t -> p (k t)")[:, 512 * half_:512 * half_ + 512],
                       start=True, stop=True).then_inc(qk_summed, 1)

            def mixer(m):
                n0, e0 = seg(f"in{m}")
                waits = KD * SPLITS.index(f"in{m}")
                if m:
                    pe.wait_ge(evacuated, e0 + 2)
                    pe.wait_ge(wff_ready, 2)
                    for k in range(KD):
                        ins = mm(ps_score[0:FF_N, 0:T], wff[:, m - 1, k], h[:, k], start=k == 0, stop=k == KD - 1)
                    ins.then_inc(f_ready, 1)
                    norm(f"in{m}")
                for s in range(STEPS[m]):
                    if m == 0 and s in (0, 4, 8):
                        group_sum(4 + s // 4)
                    chunk_in(n0 + s)
                    bank_free(e0 + s)
                    dst = acc[(e0 + s) % 2]
                    for side in range(2):
                        if IN_CHUNKS[m][s][2] == "t":
                            ins = token_tiles(n0 + s, dst, [side])
                        else:
                            ins = feature_tiles(n0 + s, dst, [side], 256, KD, waits if s == 0 else None)
                        if side:
                            ins.then_inc(chunk_used, 1)
                        att_phase(m, att_slot(m, s, side))
                        if m and side == 0 and s == LIN_OUT[m]:
                            lin_out(m)
                    if m == 0 and s == 0:
                        for k in range(KD):
                            ins = mm(ps_stat[0:GLR_N, T:2 * T], wlr[:, k], u[:, k], start=k == 0, stop=k == KD - 1)
                        ins.then_inc(pe_glr, 1)
                        pe.wait_ge(dve_glr, 1)
                        for hp in range(2):
                            ins = mm(wide[:, hp * T:(hp + 1) * T], wgl[:, hp * P:(hp + 1) * P], glr,
                                     start=True, stop=True)
                        ins.then_inc(pe_z, 1)
                    if m and s in (Q_AT, K_AT):
                        qk_stat(m, s == K_AT)
                    l = s - LIN_FIRST[m] - 1
                    if 0 <= l < len(LEVELS):
                        level_scores(m, l)
                    if m == 0 and s == LIN_OUT[m]:
                        lin_out(m)
                    if s == LIN_OUT[m] + (m == 0):
                        lin_norm(m)
                if m == 0:
                    n0, e0 = seg("branch")
                    pe.wait_ge(ulo_ready, KD * SPLITS.index("branch") + KD)
                    for t in range(KD):
                        chunk_in(n0 + t)
                        bank_free(e0 + t)
                        vh, vl = kview(whi, (n0 + t) % RING, KD, P), kview(wlo, (n0 + t) % RING, KD, P)
                        for j in range(2):
                            for k in range(4 * j, 4 * j + 4):
                                ins = three(acc[(e0 + t) % 2][:, j * T:(j + 1) * T], vh[:, k], vl[:, k], mix_hi[:, k],
                                            mix_lo[:, k], k % 4 == 0, k % 4 == 3)
                        ins.then_inc(chunk_used, 1)
                n0, e0 = seg(f"out{m}")
                waits = KD * SPLITS.index(f"out{m}")
                if m == 0:
                    for t in range(4):
                        chunk_in(n0 + t)
                        bank_free(e0 + t)
                        feature_tiles(n0 + t, acc[(e0 + t) % 2], range(2), 256, KD, waits if t == 0 else None
                                      ).then_inc(chunk_used, 1)
                    return
                order = [k for kk in PAIRS[m] for k in (2 * kk, 2 * kk + 1)]
                for ts, tiles in (((0, 1), order[:6]), ((0, 1), order[6:]), ((2,), order), ((3,), order)):
                    for t in ts:
                        if order[0] in tiles:
                            chunk_in(n0 + t)
                            bank_free(e0 + t)
                        vh, vl = kview(whi, (n0 + t) % RING, KD, 256), kview(wlo, (n0 + t) % RING, KD, 256)
                        for j in range(2):
                            c = slice(j * P, (j + 1) * P)
                            for k in tiles:
                                if t == 0 and j == 0:
                                    pe.wait_ge(ulo_ready, waits + 2 * (order.index(k) // 2) + 2)
                                ins = three(acc[(e0 + t) % 2][:, j * T:(j + 1) * T], vh[:, k, c], vl[:, k, c],
                                            mix_hi[:, k], mix_lo[:, k], j == 0 and k == order[0],
                                            j == 1 and k == order[-1])
                        if order[-1] in tiles:
                            ins.then_inc(chunk_used, 1)

            pe.sem_inc(chunk_used, RING)
            pe.wait_ge(consts, 16)
            pe.wait_ge(small, 16 * len(small_loads))
            nc.tensor.transpose(ps_score[:, 0:A_ROWS], stage[0:A_ROWS, 0], const[0:A_ROWS, C_IDENT:C_IDENT + A_ROWS])
            nc.tensor.transpose(ps_score[:, P:P + B_ROWS], stage[0:B_ROWS, 1],
                                const[0:B_ROWS, C_IDENT:C_IDENT + B_ROWS]).then_inc(turned_a, 1)
            pe.wait_ge(x_in, 16)
            xt = u[:].rearrange("p k t -> p (k t)")
            for k in range(KD):
                if k >= 2:
                    pe.wait_ge(x_taken, k - 1)
                for tt in range(TT):
                    at = k % 2 * 512 + tt * P
                    ins = nc.tensor.transpose(wide[:, at:at + P],
                                              xt[:, tt * D + k * P:tt * D + (k + 1) * P], ident)
                ins.then_inc(x_turned, 1)
            pe.wait_ge(set_up, 4)
            pe.wait_ge(c_ready, 1)
            for k in range(DIRECT):
                if k == DIRECT - 1:
                    norm("up0")
                early_tile(k)
            for half_ in range(2):
                pe.wait_ge(early_step, KD - DIRECT + half_)
                for j in range(half_ * KD, (half_ + 1) * KD):
                    ins = mm(ps_mod[:, j:j + 1], early_sum[:, j * P:(j + 1) * P], ones[:, 0:1],
                             start=False, stop=j == 2 * KD - 1)
                ins.then_inc(mod_ready, 2)
            pe.wait_ge(later, 16 * len(later_loads))
            mm(ps_turn[0:4, 0:384], rel[:], prob[0:NUM_BUCKETS, :], start=True, stop=True
               ).then_inc(toe_psum, 1)
            ffn(0)
            norm("in0")
            mixer(0)
            norm("up1")
            ffn(1)
            for layer in (1, 2):
                ffn(2 * layer, final_norms if layer == 1 else lambda: norm("up4"))
                mixer(layer)
                ffn(2 * layer + 1, lambda: norm(f"up{2 * layer + 1}"))
            pe.wait_ge(evacuated, 2 + UNIT["down5"] + KD)
            for c in range(TT * KD // 4):
                tt, k0 = c // 2, 4 * (c % 2)
                if c >= 2:
                    pe.wait_ge(out_taken, c - 1)
                for k in range(4):
                    at = c % 2 * 512 + k * P
                    ins = nc.tensor.transpose(wide[:, at:at + P], h[:, k0 + k, tt * P:(tt + 1) * P], ident)
                ins.then_inc(out_turned, 1)


_INS = ["x", "c", "w_ada", "b_ada", "norm_ff1", "w_ff1_gate", "w_ff1_up", "w_ff1_down", "norm_mix", "w_in", "w_gla_lr",
        "b_gla_lr", "gla_norm", "rel_bias", "w_br_gla", "w_br_moba", "w_out", "norm_ff2", "w_ff2_gate", "w_ff2_up",
        "w_ff2_down", "norm_final", "ffn1_norm_2", "ffn1_w_in_2", "ffn1_w_out_2", "mix_norm_2", "w_mix_in_2",
        "conv_w_2", "hgrn_lb_logits_2", "hgrn_out_gain_2", "fox_q_gain_2", "fox_k_gain_2", "fox_f_bias_2",
        "w_mix_out_2", "ffn2_norm_2", "ffn2_w_in_2", "ffn2_w_out_2"]


def kernel(**inputs):
    import concourse.bacc as bacc
    from concourse.bass_utils import run_bass_kernel_spmd

    nc = bacc.Bacc("TRN2", target_bir_lowering=False, num_devices=1)
    arrays, aps = {}, {}
    constants, masks, by_distance = shape_constants()
    given = {name: np.ascontiguousarray(inputs[name]) for name in _INS}
    for name, value in {**given, "shape_constants": constants, "level_masks": masks,
                        "by_distance": by_distance}.items():
        arrays[f"in_{name}"] = value
        aps[name] = nc.dram_tensor(f"in_{name}", value.shape, mybir.dt.from_np(value.dtype), kind="ExternalInput").ap()
    out = nc.dram_tensor("out", (1, T, D), F32, kind="ExternalOutput").ap()
    build(nc, aps, out)
    result = run_bass_kernel_spmd(nc, [arrays], core_ids=[0])
    return result.results[0]["out"]
```
